# Optimizing a Trainium2 kernel written in Bass

```python
import math
import jax, jax.numpy as jnp
from jax import lax
import numpy as np

D_MODEL = 2048
BATCH = 1
SEQ = 512
DEPTH = 2

HEAD_DIM = 64
MIX_WIDTH = D_MODEL // 4
BRANCH_W = MIX_WIDTH // 2
N_HEADS = BRANCH_W // HEAD_DIM
N_IN_PARTS = 8
ROPE_THETA = 10000.0
DIL_PAIRS = ((128, 1), (512, 4), (2048, 16))
DIL_STEPS = 128
MOBA_BLOCK = 256
MOBA_TOPK = 3
DIFF_HEAD_DIM = HEAD_DIM // 2
Q_BLOCK = 128
RMS_EPS = 1e-6
N_ODD = DEPTH // 2


def _rmsnorm(x, g):
    xf = x.astype(jnp.float32)
    y = xf * lax.rsqrt(jnp.mean(xf * xf, axis=-1, keepdims=True) + RMS_EPS)
    return (y * g.astype(jnp.float32)).astype(x.dtype)

def _rope(t, pos):
    d = t.shape[-1]
    half = d // 2
    inv = ROPE_THETA ** (-jnp.arange(half, dtype=jnp.float32) / half)
    ang = pos.astype(jnp.float32)[:, None] * inv[None, :]
    cos, sin = jnp.cos(ang), jnp.sin(ang)
    tf = t.astype(jnp.float32)
    t1, t2 = tf[..., :half], tf[..., half:]
    return jnp.concatenate([t1 * cos - t2 * sin, t1 * sin + t2 * cos], axis=-1).astype(t.dtype)

def _heads(t):
    b, s, _ = t.shape
    return t.reshape(b, s, N_HEADS, -1).transpose(0, 2, 1, 3)

def _merge(t):
    b, h, s, d = t.shape
    return t.transpose(0, 2, 1, 3).reshape(b, s, h * d)

def _dilated_branch(q, k, v, r):
    b, h, s, d = q.shape
    L = -(-s // (r * DIL_STEPS)) * DIL_STEPS
    pad = L * r - s
    nb = L // DIL_STEPS

    def to_phase(t):
        t = jnp.pad(t, ((0, 0), (0, 0), (0, pad), (0, 0)))
        t = t.reshape(b, h, L, r, d).transpose(0, 1, 3, 2, 4)
        return t.reshape(b, h, r, nb, DIL_STEPS, d)

    qb, kb, vb = to_phase(q), to_phase(k), to_phase(v)
    prev = lambda t: jnp.pad(t, ((0, 0), (0, 0), (0, 0), (1, 0), (0, 0), (0, 0)))[:, :, :, :-1]
    kk = jnp.concatenate([prev(kb), kb], axis=4)
    vv = jnp.concatenate([prev(vb), vb], axis=4)
    sc = jnp.einsum('bhrnqd,bhrnkd->bhrnqk', qb, kk).astype(jnp.float32) / math.sqrt(d)
    i = jnp.arange(DIL_STEPS)[:, None]
    j = jnp.arange(2 * DIL_STEPS)[None, :]
    band = (j >= i) & (j <= i + DIL_STEPS)
    exists = (jnp.arange(nb)[:, None, None] > 0) | (j[None] >= DIL_STEPS)
    mask = band[None] & exists
    sc = jnp.where(mask, sc, -jnp.inf)
    m = jnp.max(sc, axis=-1, keepdims=True)
    p = jnp.exp(sc - m)
    den = jnp.sum(p, axis=-1)
    o = jnp.einsum('bhrnqk,bhrnkd->bhrnqd', p, vv.astype(jnp.float32)) / den[..., None]
    lse = m[..., 0] + jnp.log(den)
    o = o.reshape(b, h, r, L, d).transpose(0, 1, 3, 2, 4).reshape(b, h, L * r, d)[:, :, :s]
    lse = lse.reshape(b, h, r, L).transpose(0, 1, 3, 2).reshape(b, h, L * r)[:, :, :s]
    return o, lse

def _dilated_mixture(q, k, v):
    outs, lses = [], []
    for _, r in DIL_PAIRS:
        o, l = _dilated_branch(q, k, v, r)
        outs.append(o)
        lses.append(l)
    w = jax.nn.softmax(jnp.stack(lses, axis=0), axis=0)[..., None]
    return jnp.sum(w * jnp.stack(outs, axis=0), axis=0).astype(q.dtype)

def _moba(q, k, v):
    b, h, s, d = q.shape
    sp = -(-s // MOBA_BLOCK) * MOBA_BLOCK
    nblk = sp // MOBA_BLOCK
    kp = jnp.pad(k, ((0, 0), (0, 0), (0, sp - s), (0, 0)))
    vp = jnp.pad(v, ((0, 0), (0, 0), (0, sp - s), (0, 0)))
    kb = kp.reshape(b, h, nblk, MOBA_BLOCK, d)
    vb = vp.reshape(b, h, nblk, MOBA_BLOCK, d)
    kmean = jnp.mean(kb.astype(jnp.float32), axis=3)
    n_sel = min(MOBA_TOPK, nblk)
    nch = s // Q_BLOCK
    qc = q.reshape(b, h, nch, Q_BLOCK, d).transpose(2, 0, 1, 3, 4)
    starts = jnp.arange(nch, dtype=jnp.int32) * Q_BLOCK
    b_ix = jnp.arange(b)[:, None, None, None]
    h_ix = jnp.arange(h)[None, :, None, None]
    scale = 1.0 / math.sqrt(d)
    kpos_blk = jnp.arange(MOBA_BLOCK)

    def chunk(args):
        qch, t0 = args
        cur = t0 // MOBA_BLOCK
        gate = jnp.einsum('bhqd,bhnd->bhqn', qch.astype(jnp.float32), kmean)
        gate = jnp.where(jnp.arange(nblk) < cur, gate, -jnp.inf)
        _, sel = lax.top_k(gate, n_sel)
        kg = kb[b_ix, h_ix, sel]
        vg = vb[b_ix, h_ix, sel]
        k_own = lax.dynamic_slice_in_dim(kp, cur * MOBA_BLOCK, MOBA_BLOCK, axis=2)
        v_own = lax.dynamic_slice_in_dim(vp, cur * MOBA_BLOCK, MOBA_BLOCK, axis=2)
        s_sel = jnp.einsum('bhqd,bhqnkd->bhqnk', qch, kg).astype(jnp.float32) * scale
        s_sel = jnp.where((jnp.arange(n_sel) < cur)[:, None], s_sel, -jnp.inf)
        s_own = jnp.einsum('bhqd,bhkd->bhqk', qch, k_own).astype(jnp.float32) * scale
        qpos = t0 + jnp.arange(Q_BLOCK)
        s_own = jnp.where(cur * MOBA_BLOCK + kpos_blk[None, :] <= qpos[:, None], s_own, -jnp.inf)
        n_sk = n_sel * MOBA_BLOCK
        p = jax.nn.softmax(jnp.concatenate([s_sel.reshape(b, h, Q_BLOCK, n_sk), s_own], axis=-1), axis=-1)
        p_sel = p[..., :n_sk].reshape(b, h, Q_BLOCK, n_sel, MOBA_BLOCK).astype(v.dtype)
        p_own = p[..., n_sk:].astype(v.dtype)
        return (jnp.einsum('bhqnk,bhqnkd->bhqd', p_sel, vg)
                + jnp.einsum('bhqk,bhkd->bhqd', p_own, v_own))

    out = lax.map(chunk, (qc, starts))
    return out.transpose(1, 2, 0, 3, 4).reshape(b, h, s, d)

def _diff_attention(q, k, v, lam, subln_g, lambda_init):
    s = k.shape[-2]
    scale = 1.0 / math.sqrt(q.shape[-1])
    lf = lam.astype(jnp.float32)
    lam_val = jnp.exp(jnp.sum(lf[0] * lf[1])) - jnp.exp(jnp.sum(lf[2] * lf[3])) + lambda_init
    outs = []
    for t0 in range(0, s, Q_BLOCK):
        kl = t0 + Q_BLOCK
        sc = jnp.einsum('bhiqd,bhikd->bhiqk', q[:, :, :, t0:kl], k[:, :, :, :kl]).astype(jnp.float32) * scale
        causal = jnp.arange(kl)[None, :] <= (t0 + jnp.arange(Q_BLOCK))[:, None]
        p = jax.nn.softmax(jnp.where(causal, sc, -jnp.inf), axis=-1)
        a = p[:, :, 0] - lam_val * p[:, :, 1]
        outs.append(jnp.einsum('bhqk,bhkd->bhqd', a.astype(v.dtype), v[:, :, :kl]))
    o = _rmsnorm(jnp.concatenate(outs, axis=2), subln_g)
    return (o.astype(jnp.float32) * (1.0 - lambda_init)).astype(v.dtype)

def _stick_breaking(q, k, v):
    b, h, s, d = q.shape
    scale = 1.0 / math.sqrt(d)
    ar = jnp.arange(Q_BLOCK)
    tri = (ar[:, None] > ar[None, :]).astype(jnp.float32)
    outs = []
    for i, t0 in enumerate(range(0, s, Q_BLOCK)):
        nc = i + 1
        kl = nc * Q_BLOCK
        z = jnp.einsum('bhqd,bhkd->bhqk', q[:, :, t0:kl], k[:, :, :kl]).astype(jnp.float32) * scale
        before = jnp.arange(kl)[None, :] < (t0 + ar)[:, None]
        ln1m = jnp.where(before, jax.nn.log_sigmoid(-z), 0.0)
        ln1m_c = ln1m.reshape(b, h, Q_BLOCK, nc, Q_BLOCK)
        tri_c = (jnp.arange(nc)[:, None] > jnp.arange(nc)[None, :]).astype(jnp.float32)
        tail = (jnp.einsum('bhqcj,js->bhqcs', ln1m_c, tri)
                + jnp.einsum('bhqe,ec->bhqc', jnp.sum(ln1m_c, axis=-1), tri_c)[..., None])
        log_a = jnp.where(before, z + ln1m + tail.reshape(b, h, Q_BLOCK, kl), -jnp.inf)
        outs.append(jnp.einsum('bhqk,bhkd->bhqd', jnp.exp(log_a).astype(v.dtype), v[:, :, :kl]))
    return jnp.concatenate(outs, axis=2)

def first_inputs(seed: int = 0) -> dict:
    key = jax.random.key(seed)
    ks = jax.random.split(key, 8)
    x = jax.random.normal(ks[0], (BATCH, SEQ, D_MODEL), jnp.float32)
    norm_g = 1.0 + 0.02 * jax.random.normal(ks[1], (DEPTH, D_MODEL), jnp.float32)
    w_in = jax.random.normal(ks[2], (DEPTH, D_MODEL, N_IN_PARTS * BRANCH_W), jnp.float32) * D_MODEL ** -0.5
    w_out = jax.random.normal(ks[3], (DEPTH, MIX_WIDTH, D_MODEL), jnp.float32) * MIX_WIDTH ** -0.5
    diff_lam = 0.1 * jax.random.normal(ks[4], (N_ODD, 4, DIFF_HEAD_DIM), jnp.float32)
    diff_subln_g = 1.0 + 0.02 * jax.random.normal(ks[5], (N_ODD, HEAD_DIM), jnp.float32)
    final_norm_g = 1.0 + 0.02 * jax.random.normal(ks[6], (D_MODEL,), jnp.float32)
    return {"x": x, "norm_g": norm_g, "w_in": w_in, "w_out": w_out,
            "diff_lam": diff_lam, "diff_subln_g": diff_subln_g,
            "final_norm_g": final_norm_g}

def first_block(x, norm_g, w_in, w_out, diff_lam, diff_subln_g, final_norm_g):
    b, s, _ = x.shape
    pos = jnp.arange(s)
    for layer in range(DEPTH):
        h = _rmsnorm(x, norm_g[layer])
        proj = jnp.einsum('bsd,de->bse', h, w_in[layer])
        parts = jnp.split(proj, N_IN_PARTS, axis=-1)
        if layer % 2 == 0:
            qa, ka, va, ga, qb, kb, vb, gb = parts
            oa = _dilated_mixture(_rope(_heads(qa), pos), _rope(_heads(ka), pos), _heads(va))
            ob = _moba(_rope(_heads(qb), pos), _rope(_heads(kb), pos), _heads(vb))
            y = jnp.concatenate([_merge(oa) * jax.nn.silu(ga),
                                 _merge(ob) * jax.nn.silu(gb)], axis=-1)
        else:
            qc, kc, vc, gc, qd, kd, vd, gd = parts
            li = layer // 2
            lambda_init = 0.8 - 0.6 * math.exp(-0.3 * layer)
            split2 = lambda t: t.reshape(b, s, N_HEADS, 2, DIFF_HEAD_DIM).transpose(0, 2, 3, 1, 4)
            oc = _diff_attention(_rope(split2(qc), pos), _rope(split2(kc), pos), _heads(vc),
                                 diff_lam[li], diff_subln_g[li], lambda_init)
            od = _stick_breaking(_heads(qd), _heads(kd), _heads(vd))
            y = jnp.concatenate([_merge(oc) * jax.nn.silu(gc),
                                 _merge(od) * jax.nn.silu(gd)], axis=-1)
        x = x + jnp.einsum('bse,ed->bsd', y.astype(x.dtype), w_out[layer])
    return _rmsnorm(x, final_norm_g)


DEPTH_2 = 1

D_MIX = D_MODEL
D_A = D_MIX // 4
D_B = D_MIX // 4
D_C = D_MIX // 4
D_D = D_MIX // 4
GDN_HEAD_DIM = 128
GDN_HEADS = D_A // GDN_HEAD_DIM
GDN_CONV = 4
GDN_CHUNK = 64
GDN_CHUNK_LOG2 = 6
LRU_BLOCKS = 8
LRU_BLOCK_DIM = D_B // LRU_BLOCKS
LRU_CONV = 4
LRU_C = 8.0
SGU_GROUPS = 4
SGU_GROUP_DIM = D_C // SGU_GROUPS
SGU_CHUNK = 128
SCONV_WIDTH = 3
D_FF = (D_MODEL * 11) // 4
FFN_CONV = 3
IN_SIZES = (D_A, D_A, D_A, D_A, GDN_HEADS, GDN_HEADS, D_B, D_B, 2 * D_C, D_D, D_D, D_D)
N_IN = 4 * D_A + 2 * GDN_HEADS + 2 * D_B + 2 * D_C + 3 * D_D
EPS = 1e-6


def _split(t, sizes):
    idx, acc = [], 0
    for s in sizes[:-1]:
        acc += s
        idx.append(acc)
    return jnp.split(t, idx, axis=-1)

def rms_norm(x, w):
    xf = x.astype(jnp.float32)
    y = xf * lax.rsqrt(jnp.mean(xf * xf, axis=-1, keepdims=True) + EPS)
    return (y * w.astype(jnp.float32)).astype(x.dtype)

def layer_norm(x, w, b):
    xf = x.astype(jnp.float32)
    mu = jnp.mean(xf, axis=-1, keepdims=True)
    xc = xf - mu
    y = xc * lax.rsqrt(jnp.mean(xc * xc, axis=-1, keepdims=True) + EPS)
    return y * w.astype(jnp.float32) + b.astype(jnp.float32)

def causal_dwconv(x, w, b=None):
    K, C = w.shape
    y = lax.conv_general_dilated(x, w[:, None, :].astype(x.dtype), window_strides=(1,),
                                 padding=[(K - 1, 0)], dimension_numbers=('NWC', 'WIO', 'NWC'),
                                 feature_group_count=C)
    if b is not None:
        y = y + b.astype(x.dtype)
    return y

def l2norm(t):
    return t * lax.rsqrt(jnp.sum(t * t, axis=-1, keepdims=True) + EPS)

def chunk_gated_delta_rule(q, k, v, g, beta):
    Bn, S, H, Dk = q.shape
    Dv = v.shape[-1]
    nC = S // GDN_CHUNK
    C = GDN_CHUNK
    q = l2norm(q) * (Dk ** -0.5)
    k = l2norm(k)

    def chunks(t):
        return t.reshape(Bn, nC, C, H, -1).transpose(0, 3, 1, 2, 4)

    qc, kc, vc = chunks(q), chunks(k), chunks(v)
    gc = g.reshape(Bn, nC, C, H).transpose(0, 3, 1, 2)
    bc = beta.reshape(Bn, nC, C, H).transpose(0, 3, 1, 2)
    gcum = jnp.cumsum(gc, axis=-1)
    causal = jnp.tril(jnp.ones((C, C), dtype=bool))
    strict = jnp.tril(jnp.ones((C, C), dtype=bool), -1)
    diff = gcum[..., :, None] - gcum[..., None, :]
    decay = jnp.where(causal, jnp.exp(jnp.where(causal, diff, 0.0)), 0.0)
    kb = kc * bc[..., None]
    M = jnp.where(strict, jnp.einsum('bhncd,bhnsd->bhncs', kb, kc) * decay, 0.0)
    N = -M
    T = jnp.eye(C, dtype=jnp.float32) + N
    P = N
    for _ in range(GDN_CHUNK_LOG2 - 1):
        P = jnp.einsum('bhnij,bhnjk->bhnik', P, P)
        T = T + jnp.einsum('bhnij,bhnjk->bhnik', T, P)
    w = jnp.einsum('bhncs,bhnsd->bhncd', T, kb * jnp.exp(gcum)[..., None])
    u = jnp.einsum('bhncs,bhnsd->bhncd', T, vc * bc[..., None])
    attn = jnp.where(causal, jnp.einsum('bhncd,bhnsd->bhncs', qc, kc) * decay, 0.0)
    q_g = qc * jnp.exp(gcum)[..., None]
    k_g = kc * jnp.exp(gcum[..., -1:] - gcum)[..., None]
    g_last = jnp.exp(gcum[..., -1])

    def step(state, inp):
        q_i, a_i, u_i, w_i, k_i, gl_i = inp
        v_new = u_i - jnp.einsum('bhck,bhkv->bhcv', w_i, state)
        o_i = jnp.einsum('bhck,bhkv->bhcv', q_i, state) + jnp.einsum('bhcs,bhsv->bhcv', a_i, v_new)
        state = state * gl_i[..., None, None] + jnp.einsum('bhck,bhcv->bhkv', k_i, v_new)
        return state, o_i

    xs = tuple(jnp.moveaxis(t, 2, 0) for t in (q_g, attn, u, w, k_g, g_last))
    s0 = jnp.zeros((Bn, H, Dk, Dv), jnp.float32)
    _, o = lax.scan(step, s0, xs)
    return o.transpose(1, 0, 3, 2, 4).reshape(Bn, S, H, Dv)

def gdn_mixer(q, k, v, z, b, a, conv_w, a_log, dt_bias, norm_w):
    Bn, S, _ = q.shape
    qkv = jax.nn.silu(causal_dwconv(jnp.concatenate([q, k, v], axis=-1), conv_w))
    q, k, v = jnp.split(qkv, 3, axis=-1)

    def heads(t):
        return t.reshape(Bn, S, GDN_HEADS, GDN_HEAD_DIM).astype(jnp.float32)

    beta = jax.nn.sigmoid(b.astype(jnp.float32))
    g = -jnp.exp(a_log.astype(jnp.float32)) * jax.nn.softplus(a.astype(jnp.float32) + dt_bias.astype(jnp.float32))
    o = chunk_gated_delta_rule(heads(q), heads(k), heads(v), g, beta)
    o = o * lax.rsqrt(jnp.mean(o * o, axis=-1, keepdims=True) + EPS) * norm_w.astype(jnp.float32) * jax.nn.silu(heads(z))
    return o.reshape(Bn, S, D_A).astype(z.dtype)

def lru_scan(a, b):
    def combine(l, r):
        return (l[0] * r[0], r[0] * l[1] + r[1])
    _, h = lax.associative_scan(combine, (a, b), axis=1)
    return h

def rglru_mixer(xb, gate, conv_w, conv_b, wa, ba, wx, bx, lam):
    Bn, S, _ = xb.shape
    xc = causal_dwconv(xb, conv_w, conv_b).astype(jnp.float32)
    xblk = xc.reshape(Bn, S, LRU_BLOCKS, LRU_BLOCK_DIM)
    r = jax.nn.sigmoid(jnp.einsum('bshi,hij->bshj', xblk, wa.astype(jnp.float32)) + ba.astype(jnp.float32)).reshape(Bn, S, D_B)
    i = jax.nn.sigmoid(jnp.einsum('bshi,hij->bshj', xblk, wx.astype(jnp.float32)) + bx.astype(jnp.float32)).reshape(Bn, S, D_B)
    log_a = -LRU_C * r * jax.nn.softplus(-lam.astype(jnp.float32))
    a = jnp.exp(log_a)
    mult = jnp.sqrt(-jnp.expm1(2.0 * log_a))
    h = lru_scan(a, mult * (i * xc))
    return (h * jax.nn.gelu(gate.astype(jnp.float32))).astype(xb.dtype)

def sgu_mixer(uv, ln_w, ln_b, ws, bs):
    Bn, S, _ = uv.shape
    uvf = jax.nn.gelu(uv.astype(jnp.float32))
    u, v = jnp.split(uvf, 2, axis=-1)
    v = layer_norm(v, ln_w, ln_b)
    v = v.reshape(Bn, S // SGU_CHUNK, SGU_CHUNK, SGU_GROUPS, SGU_GROUP_DIM)
    mask = jnp.tril(jnp.ones((SGU_CHUNK, SGU_CHUNK), dtype=bool))
    wsm = jnp.where(mask, ws.astype(jnp.float32), 0.0)
    v = jnp.einsum('gts,bnsgd->bntgd', wsm, v) + bs.astype(jnp.float32).T[:, :, None]
    return (u * v.reshape(Bn, S, D_C)).astype(uv.dtype)

def short_conv_mixer(bg, cg, hh, conv_w):
    return bg * causal_dwconv(cg * hh, conv_w)

def conv_ffn(h, up, conv_w, conv_b, down):
    hid = causal_dwconv(h @ up.astype(h.dtype), conv_w, conv_b)
    gate, val = jnp.split(hid, 2, axis=-1)
    return (jax.nn.gelu(gate) * val) @ down.astype(h.dtype)

def second_inputs(seed: int = 0) -> dict:
    key = jax.random.key(seed)
    ks = iter(jax.random.split(key, 48))
    L = DEPTH_2
    f32 = jnp.float32

    def nrm(shape, scale):
        return jax.random.normal(next(ks), shape, f32) * scale

    def gain(shape):
        return 1.0 + 0.1 * jax.random.normal(next(ks), shape, f32)

    def unif(shape, lo, hi):
        return jax.random.uniform(next(ks), shape, f32, lo, hi)

    s = unif((L, D_B), 0.9, 0.999) ** (1.0 / LRU_C)
    lru_lambda = jnp.log(s) - jnp.log1p(-s)
    dt = jnp.exp(unif((L, GDN_HEADS), float(np.log(1e-3)), float(np.log(1e-1))))
    gdn_dt_bias = dt + jnp.log(-jnp.expm1(-dt))
    return {
        "x": nrm((BATCH, SEQ, D_MODEL), 1.0),
        "pre_mix_norm": gain((L, D_MODEL)),
        "w_in": nrm((L, D_MODEL, N_IN), D_MODEL ** -0.5),
        "gdn_conv_w": nrm((L, GDN_CONV, 3 * D_A), GDN_CONV ** -0.5),
        "gdn_a_log": jnp.log(unif((L, GDN_HEADS), 1.0, 16.0)),
        "gdn_dt_bias": gdn_dt_bias,
        "gdn_norm_w": gain((L, GDN_HEAD_DIM)),
        "lru_conv_w": nrm((L, LRU_CONV, D_B), LRU_CONV ** -0.5),
        "lru_conv_b": nrm((L, D_B), 0.01),
        "lru_wa": nrm((L, LRU_BLOCKS, LRU_BLOCK_DIM, LRU_BLOCK_DIM), LRU_BLOCK_DIM ** -0.5),
        "lru_ba": nrm((L, LRU_BLOCKS, LRU_BLOCK_DIM), 0.01),
        "lru_wx": nrm((L, LRU_BLOCKS, LRU_BLOCK_DIM, LRU_BLOCK_DIM), LRU_BLOCK_DIM ** -0.5),
        "lru_bx": nrm((L, LRU_BLOCKS, LRU_BLOCK_DIM), 0.01),
        "lru_lambda": lru_lambda,
        "sgu_ln_w": gain((L, D_C)),
        "sgu_ln_b": nrm((L, D_C), 0.01),
        "sgu_ws": nrm((L, SGU_GROUPS, SGU_CHUNK, SGU_CHUNK), SGU_CHUNK ** -0.5),
        "sgu_b": gain((L, SGU_GROUPS, SGU_CHUNK)),
        "sconv_w": nrm((L, SCONV_WIDTH, D_D), SCONV_WIDTH ** -0.5),
        "grp_norm_w": gain((L, 3, D_B)),
        "w_out": nrm((L, D_MIX, D_MODEL), D_MIX ** -0.5),
        "post_mix_norm": gain((L, D_MODEL)),
        "pre_ffn_norm": gain((L, D_MODEL)),
        "ffn_up": nrm((L, D_MODEL, 2 * D_FF), D_MODEL ** -0.5),
        "ffn_conv_w": nrm((L, FFN_CONV, 2 * D_FF), FFN_CONV ** -0.5),
        "ffn_conv_b": nrm((L, 2 * D_FF), 0.01),
        "ffn_down": nrm((L, D_FF, D_MODEL), D_FF ** -0.5),
        "post_ffn_norm": gain((L, D_MODEL)),
    }

def second_block(x, pre_mix_norm, w_in, gdn_conv_w, gdn_a_log, gdn_dt_bias, gdn_norm_w,
              lru_conv_w, lru_conv_b, lru_wa, lru_ba, lru_wx, lru_bx, lru_lambda,
              sgu_ln_w, sgu_ln_b, sgu_ws, sgu_b, sconv_w, grp_norm_w, w_out,
              post_mix_norm, pre_ffn_norm, ffn_up, ffn_conv_w, ffn_conv_b, ffn_down,
              post_ffn_norm):
    for l in range(DEPTH_2):
        h = rms_norm(x, pre_mix_norm[l])
        p = h @ w_in[l].astype(h.dtype)
        (q, k, v, z, b_gdn, a_gdn, lru_x, lru_gate, sgu_uv, sc_b, sc_c, sc_h) = _split(p, IN_SIZES)
        y_a = gdn_mixer(q, k, v, z, b_gdn, a_gdn, gdn_conv_w[l], gdn_a_log[l], gdn_dt_bias[l], gdn_norm_w[l])
        y_b = rms_norm(rglru_mixer(lru_x, lru_gate, lru_conv_w[l], lru_conv_b[l], lru_wa[l], lru_ba[l],
                                   lru_wx[l], lru_bx[l], lru_lambda[l]), grp_norm_w[l, 0])
        y_c = rms_norm(sgu_mixer(sgu_uv, sgu_ln_w[l], sgu_ln_b[l], sgu_ws[l], sgu_b[l]), grp_norm_w[l, 1])
        y_d = rms_norm(short_conv_mixer(sc_b, sc_c, sc_h, sconv_w[l]), grp_norm_w[l, 2])
        y = jnp.concatenate([y_a, y_b, y_c, y_d], axis=-1) @ w_out[l].astype(h.dtype)
        x = x + rms_norm(y, post_mix_norm[l])
        h = rms_norm(x, pre_ffn_norm[l])
        y = conv_ffn(h, ffn_up[l], ffn_conv_w[l], ffn_conv_b[l], ffn_down[l])
        x = x + rms_norm(y, post_ffn_norm[l])
    return x


def setup_inputs(seed=0):
    out = dict(first_inputs(seed))
    for name, value in second_inputs(seed + 1).items():
        if name != "x":
            out[name + "_2"] = value
    return out


def reference(
    x, norm_g, w_in, w_out, diff_lam, diff_subln_g, final_norm_g, pre_mix_norm_2, w_in_2,
    gdn_conv_w_2, gdn_a_log_2, gdn_dt_bias_2, gdn_norm_w_2, lru_conv_w_2, lru_conv_b_2,
    lru_wa_2, lru_ba_2, lru_wx_2, lru_bx_2, lru_lambda_2, sgu_ln_w_2, sgu_ln_b_2, sgu_ws_2,
    sgu_b_2, sconv_w_2, grp_norm_w_2, w_out_2, post_mix_norm_2, pre_ffn_norm_2, ffn_up_2,
    ffn_conv_w_2, ffn_conv_b_2, ffn_down_2, post_ffn_norm_2,
):
    x = first_block(
        x, norm_g, w_in, w_out, diff_lam, diff_subln_g, final_norm_g,
    )
    return second_block(
        x, pre_mix_norm_2, w_in_2, gdn_conv_w_2, gdn_a_log_2, gdn_dt_bias_2, gdn_norm_w_2,
        lru_conv_w_2, lru_conv_b_2, lru_wa_2, lru_ba_2, lru_wx_2, lru_bx_2, lru_lambda_2,
        sgu_ln_w_2, sgu_ln_b_2, sgu_ws_2, sgu_b_2, sconv_w_2, grp_norm_w_2, w_out_2,
        post_mix_norm_2, pre_ffn_norm_2, ffn_up_2, ffn_conv_w_2, ffn_conv_b_2, ffn_down_2,
        post_ffn_norm_2,
    )


_drawn_inputs = setup_inputs


def setup_inputs(seed=0):
    import zlib

    import numpy as np

    out = dict(_drawn_inputs(seed))
    spreads = {}
    factors = {'diff_lam': 3.224,
     'diff_subln_g': 6.403,
     'lru_ba_2': 64.0,
     'lru_bx_2': 33.249,
     'sgu_ln_b_2': 22.615,
     'ffn_conv_b_2': 6.853,
     'lru_conv_b_2': 3.219}
    for name, (base, spread) in spreads.items():
        noise = np.random.default_rng([zlib.crc32(name.encode()), seed]).standard_normal(out[name].shape)
        drawn = base * np.exp(spread * noise) if base else spread * noise
        out[name] = __import__('jax').numpy.asarray(drawn.astype(out[name].dtype))
    for name, factor in factors.items():
        out[name] = (out[name] * factor).astype(out[name].dtype)
    return out
```

```python
from contextlib import ExitStack

import numpy as np

import concourse.bass as bass
from concourse import mybir

F32 = mybir.dt.float32
F32R = mybir.dt.float32r
ALU = mybir.AluOpType
ACT = mybir.ActivationFunctionType
AX = mybir.AxisListType.X

P128 = 128
D = 2048
S = 512
KT = D // P128
UNIT = 2048
NEG = -1.0e30
EPS = 1e-6
HEAD = 64
N_HEADS = 4
PAD = 4
D_FF = (D * 11) // 4
SEGS = D_FF // 512
FFT = D_FF // P128

U_IN = 16
U_OUT = 4
U_UP, U_DOWN = 8, 4
U_L = [0, U_IN + U_OUT]
U_M2 = 2 * (U_IN + U_OUT)
M2_QUADS = dict(lru=2, sgu=2, sc=3, qkvz=4)
U_LRU = U_M2
U_SGU = U_LRU + 4 * M2_QUADS["lru"]
U_SC = U_SGU + 4 * M2_QUADS["sgu"]
U_QKVZ = U_SC + 4 * M2_QUADS["sc"]
U_WO2 = U_QKVZ + 4 * M2_QUADS["qkvz"]
U_FFN = U_WO2 + 16
N_UNITS = U_FFN + SEGS * (U_UP + U_DOWN)
G_L = [0, 8]
G_LRU = 16
G_SGU = G_LRU + 4
G_SC = G_SGU + 4
G_QKVZ = G_SC + 6
G_WO2 = G_QKVZ + 8
G_FFN = G_WO2 + 8

PARAM_SIZES = [("g0", 16), ("g1", 16), ("final", 16), ("pre_mix", 16), ("post_mix", 16), ("pre_ffn", 16),
               ("post_ffn", 16), ("gdn_conv", 48), ("gdn_norm", 1), ("lru_conv", 16), ("lru_b", 4),
               ("ba", 4), ("bx", 4), ("lam", 4), ("sc_conv", 12), ("grp", 12), ("subln", 1),
               ("ffn_conv", 6 * FFT), ("ffn_b", 2 * FFT)]
PARAM = {}
_n = 0
for _name, _size in PARAM_SIZES:
    PARAM[_name] = _n
    _n += _size
N_PARAM = _n

CONST_SIZES = [("ident", 128), ("ones", 128), ("eps", 1), ("one", 1), ("pad", 6),
               ("rot0", 128), ("rot1", 128), ("suffix", 128), ("before01", 128), ("notbefore", 128),
               ("dilated", 512), ("causal", 512), ("cos0", 512), ("sin0", 512), ("cos1", 512), ("sin1", 512),
               ("chunk_tri", 128), ("chunk_all", 128), ("half_a", 128), ("half_b", 128),
               ("decay_mask", 128), ("strict01", 128), ("tri01", 128)]
CONST = {}
_n = 0
for _name, _size in CONST_SIZES:
    CONST[_name] = _n
    _n += _size
N_CONST = _n


def shape_constants():
    c = np.zeros((P128, N_CONST), np.float32)

    def put(name, a):
        c[:, CONST[name]:CONST[name] + a.shape[1]] = a

    p, f = np.arange(128)[:, None], np.arange(128)[None, :]
    same = (p // 64) == (f // 64)
    put("ident", (p == f).astype(np.float32))
    put("ones", np.ones((128, 128), np.float32))
    put("eps", np.full((128, 1), EPS, np.float32))
    put("one", np.ones((128, 1), np.float32))
    for n, dim in ((0, 64), (1, 32)):
        half = dim // 2
        rot = np.zeros((128, 128), np.float32)
        for i in range(128):
            if i % dim < half:
                rot[i + half, i] = -1.0
            else:
                rot[i - half, i] = 1.0
        put(f"rot{n}", rot)
        inv = np.float32(10000.0) ** (-np.arange(half, dtype=np.float32) / np.float32(half))
        ang = np.arange(S, dtype=np.float32)[None, :] * inv.astype(np.float32)[np.arange(128) % half][:, None]
        put(f"cos{n}", np.cos(ang).astype(np.float32))
        put(f"sin{n}", np.sin(ang).astype(np.float32))
    put("suffix", (p >= f).astype(np.float32))
    put("before01", (p < f).astype(np.float32))
    put("notbefore", np.where(p < f, 0.0, NEG).astype(np.float32))
    dist = np.concatenate([128 * b + p - f for b in (3, 2, 1, 0)], axis=1)
    put("causal", np.where(dist >= 0, 0.0, NEG).astype(np.float32))
    n = ((dist >= 0) & (dist <= 128)).astype(int) + ((dist >= 0) & (dist % 4 == 0)) + ((dist >= 0) & (dist % 16 == 0))
    put("dilated", np.where(n > 0, np.log(np.maximum(n, 1)) * HEAD ** 0.5, NEG).astype(np.float32))
    put("chunk_tri", (same & (p <= f)).astype(np.float32))
    put("chunk_all", same.astype(np.float32))
    put("half_a", np.broadcast_to(p < 64, (128, 128)).astype(np.float32))
    put("half_b", np.broadcast_to(p >= 64, (128, 128)).astype(np.float32))
    put("decay_mask", np.where(same & (f >= p), 0.0, NEG).astype(np.float32))
    put("strict01", (same & (f > p)).astype(np.float32))
    put("tri01", (f >= p).astype(np.float32))
    return c


class Order:

    def __init__(self, eng, sem):
        self.eng, self.sem, self.n, self.loop = eng, sem, 0, None

    def link(self, ins):
        ins.then_inc(self.sem, 1)
        self.n += 1
        self.eng.wait_ge(self.sem, self.value())

    def value(self):
        if self.loop is None:
            return self.n
        i, start, per = self.loop
        return start + i * per + (self.n - start)

    def enter(self, i, per):
        self.loop = (i, self.n, per)

    def leave(self, trips):
        _, start, per = self.loop
        assert self.n - start == per, (self.n - start, per)
        self.n, self.loop = start + trips * per, None


def bc(ap, n):
    return ap.unsqueeze(2).broadcast_to([ap.shape[0], ap.shape[1], n])


def bm(ap, n):
    return ap.unsqueeze(1).broadcast_to([ap.shape[0], n, ap.shape[1]])


def two_blocks_kernel(nc, weights, x_in, params, consts, w_ba, alog_dt, lam_rows, sgu_rows, sgu_wsT,
                      lru_wa, lru_wx, out):
    ctx = ExitStack()
    with ctx:
        sems = {}

        def sem(name):
            if name not in sems:
                sems[name] = ctx.enter_context(nc.semaphore(name))
            return sems[name]

        IN_LAYER_0 = dict(l_scores=32, l_scores_read=32, l_probs=32, neg_max=8, l_turned=8, l_pt_a=8, l_pt_b=8,
                          l_o=8, l_o_read=8, l_y_turned=4, rotated=8, rot_read=8, roped=8, v_turned=4,
                          v_tok_ready=4, gates=2, y1=4, y1_hi_ready=4, y1_ready=4, attn_c_landed=128, y_taken=0)

        def since(name, l, n):
            return sem(name), n + (IN_LAYER_0[name] if l else 0)

        class Region:
            def __init__(self, at, end):
                self.at, self.end = at, end

            def take(self, name, shape, dt=F32):
                size = int(np.prod(shape[1:])) * 4
                at = self.at
                self.at = (at + size + 31) // 32 * 32
                assert self.at <= self.end, (name, self.at, self.end)
                return nc.alloc_sbuf_tensor_at(name, shape, dt, offset=at)

        BASE, END = 16512, 229344
        top = Region(BASE, END)
        params_sb = top.take("params_sb", [128, N_PARAM])
        head_c = top.take("head_c", [128, 264])
        rstd = top.take("rstd", [128, S])
        root = top.take("root", [128, S])
        credit = top.take("credit", [128, 16])
        squares = top.take("squares", [128, 2, S])
        raw = top.take("raw", [128, 2, UNIT])
        w_hi = top.take("w_hi", [128, 2, UNIT], F32R)
        w_lo = top.take("w_lo", [128, 2, UNIT], F32R)
        X0 = top.at
        X = top.take("X", [128, KT, S])
        H0 = top.at
        h_hi = top.take("h_hi", [128, KT, S], F32R)
        h_lo = top.take("h_lo", [128, KT, S], F32R)
        W0 = top.at
        ident, ones = head_c[:, 0:128], head_c[:, 128:256]
        eps_c, one_c = head_c[:, 256:257], head_c[:, 257:258]

        wl = Region(W0, END)
        proj = wl.take("proj", [128, 16, PAD + S])
        y1_hi = wl.take("y1_hi", [128, 4, S], F32R)
        y1_lo = wl.take("y1_lo", [128, 4, S], F32R)
        hl = Region(H0, W0)
        probs = hl.take("probs", [128, 4, 1280])
        probs_t = hl.take("probs_t", [128, 2, 1280])
        v_tok = hl.take("v_tok", [128, 4, 512])
        o_tok = hl.take("o_tok", [128, 4, 512])
        cos_sb = hl.take("cos_sb", [128, S])
        sin_sb = hl.take("sin_sb", [128, S])
        mask_sb = hl.take("mask_sb", [128, 2, 512])
        rot_sin = hl.take("rot_sin", [128, 2, S])
        attn_c = hl.take("attn_c", [128, 4, 128])
        y1 = root
        small = hl.take("small", [128, 512])
        row_max, neg_max, den, rden = (small[:, 32 * k:32 * k + 32] for k in range(4))
        lam_sb = small[:, 128:256]
        lam_s = small[:, 256:264]
        lam_prod = small[:, 264:296]
        o_ss, o_root, o_rstd = (small[:, 320 + 16 * k:336 + 16 * k] for k in range(3))

        Y = nc.alloc_sbuf_tensor_at("Y", [128, 16, S], F32, offset=X0)
        wm = Region(proj_end := (W0 + 16 * (PAD + S) * 4 + 31) // 32 * 32, END)
        gate_a = wm.take("gate_a", [128, 4, 128])
        gate_x = wm.take("gate_x", [128, 4, 128])
        sgu_sb = wm.take("sgu_sb", [128, 3, 512])
        sgu_w = wm.take("sgu_w", [128, 4, 128])
        tri01 = wm.take("tri01", [128, 128])
        lru_s = wm.take("lru_s", [128, 32])
        stats = wm.take("stats", [128, 4, 16])
        wg = Region(proj_end, END)
        pows = wg.take("pows", [128, 2, 2, 2, 512])
        wscan = Region(proj_end, END)
        state = wscan.take("state", [128, 2, 512])
        state_g = wscan.take("state_g", [128, 512])
        v_new = wscan.take("v_new", [128, 512])
        conv_out = nc.alloc_sbuf_tensor_at("conv_out", [128, 12, S], F32, offset=H0)
        hg = Region(H0, W0)
        k_be = hg.take("k_be", [128, 4, 512])
        k_g = hg.take("k_g", [128, 4, 512])
        v_b = hg.take("v_b", [128, 4, 512])
        inv_t = hg.take("inv_t", [128, 4, 512])
        attn_t = hg.take("attn_t", [128, 4, 512])
        w_t = hg.take("w_t", [128, 4, 512])
        u_b = hg.take("u_b", [128, 4, 512])
        tmp_a = hg.take("tmp_a", [128, 2, 512])
        tmp_b = hg.take("tmp_b", [128, 2, 512])
        gs0 = nc.alloc_sbuf_tensor_at("gdn_small", [128, 1024], F32, offset=X0)
        gdn_c = nc.alloc_sbuf_tensor_at("gdn_c", [128, 6, 128], F32, offset=X0 + 4096)
        ba_raw = gs0[:, 0:128]
        ba_tok = gs0[:, 128:160]
        beta, gate, g_tmp, exp_g, be, kgs = (gs0[:, 160 + 16 * k:176 + 16 * k] for k in range(6))
        g_sums = gs0[:, 256:320]
        g_last = gs0[:, 320:352]
        rstd_tok = gs0[:, 352:356]
        alog_sb = gs0[:, 360:368]
        ba_hi = nc.alloc_sbuf_tensor_at("ba_hi", [128, 128], F32R, offset=X0 + 8192 - 1024)
        ba_lo = nc.alloc_sbuf_tensor_at("ba_lo", [128, 128], F32R, offset=X0 + 8192 - 512)
        y2_hi, y2_lo = h_hi, h_lo
        y2 = nc.alloc_sbuf_tensor_at("y2", [128, 16, S], F32, offset=W0)

        y_acc = nc.alloc_sbuf_tensor_at("y_acc", [128, 16, S], F32, offset=X0)
        wf = Region(W0, END)
        f_hi = wf.take("f_hi", [128, 2, 4, S], F32R)
        f_lo = wf.take("f_lo", [128, 2, 4, S], F32R)
        hid = wf.take("hid", [128, 2, 2 + S])
        f_gate = wf.take("f_gate", [128, 2, S])
        f_val = wf.take("f_val", [128, 2, S])
        x_back = nc.alloc_sbuf_tensor_at("x_back", [128, 16, S], F32, offset=H0)

        ps = ctx.enter_context(nc.psum_tensor("ps", [128, 8, 512], F32))
        SS = 7

        rstd_g = squares[:, 0, :]
        lru_xc, lru_r, lru_i, lru_a = Y[:, 8:12, :], Y[:, 12:16, :], Y[:, 0:4, :], Y[:, 4:8, :]
        lru_a2 = proj[:, 8:12, PAD:]
        GDN_D = 128

        x_spill = nc.dram_tensor("x_spill", (128, KT, S), F32, kind="Internal").ap()
        x_spill2 = nc.dram_tensor("x_spill2", (128, KT, S), F32, kind="Internal").ap()

        def par(name, at=0, n=1):
            c = PARAM[name]
            return params_sb[:, c + at:c + at + n]

        def dpar(name, at):
            return params_sb[:, bass.ds(at + PARAM[name], 1)]

        raw_landed = [sem("raw_landed_0"), sem("raw_landed_1")]
        w_hi_ready = sem("w_hi_ready")
        w_ready = sem("w_ready")
        w_used = sem("w_used")
        bank_free = sem("bank_free")
        x_ready = sem("x_ready")
        h_hi_ready = sem("h_hi_ready")
        h_ready = sem("h_ready")
        sq_ready = sem("sq_ready")
        sq_used = sem("sq_used")
        root_ready = sem("root_ready")
        rstd_ready = sem("rstd_ready")
        params_landed = sem("params_landed")
        down_free = sem("down_free")
        down_tile = sem("down_tile")
        f_ready = sem("f_ready")
        x_landed = [sem(f"x_landed_{k}") for k in range(4)]
        dve_order, act_order, pool_order = sem("dve_order"), sem("act_order"), sem("pool_order")

        block = ctx.enter_context(nc.Block())

        OUT_BANKS = [4, 5, 6, 0]
        Q_OFF = [0, 128, 384, 768]
        K_OFF = [0, 512, 1024, 896]
        Z_OFF = [0, 512, 896, 1152]

        @block.sync
        def _(sp):
            for k in range(4):
                sp.dma_start(X[:, 4 * k:4 * k + 4, :], x_in[:, 4 * k:4 * k + 4, :]).then_inc(x_landed[k], 16)
            with sp.Fori(0, N_UNITS // 2) as i:
                for s in range(2):
                    sp.wait_ge(w_ready, 2 * i + (s + 1))
                    sp.dma_start(raw[:, s, :], weights[2 * i + s]).then_inc(raw_landed[s], 16)

        @block.gpsimd
        def _(pool):
            order = Order(pool, pool_order)
            pool.dma_start(head_c[:, :], consts[:, 0:264]).then_inc(params_landed, 16)
            pool.dma_start(params_sb[:, :], params).then_inc(params_landed, 16)
            for l in range(2):
                pool.wait_ge(w_used, U_L[l] + U_IN + 1)
                for dst, name, n in ((cos_sb[:, :], f"cos{l}", 512), (sin_sb[:, :], f"sin{l}", 512),
                                     (mask_sb[:, 0, :], "dilated", 512), (mask_sb[:, 1, :], "causal", 512),
                                     (attn_c[:, 0, :], f"rot{l}", 128), (attn_c[:, 1, :], "suffix", 128),
                                     (attn_c[:, 2, :], "before01", 128), (attn_c[:, 3, :], "notbefore", 128)):
                    pool.dma_start(dst, consts[:, CONST[name]:CONST[name] + n]).then_inc(sem("attn_c_landed"), 16)
                if l == 1:
                    pool.dma_start(lam_sb, lam_rows.partition_broadcast(128)).then_inc(sem("lam_landed"), 16)
            pool.wait_ge(x_ready, 2 * 16)
            order.link(pool.memset(proj[:, :, 0:PAD], 0.0))
            order.link(pool.memset(gate_a[:, :, :], 0.0))
            pool.memset(gate_x[:, :, :], 0.0).then_inc(sem("pads_ready"), 1)
            pool.wait_ge(sem("pads_ready"), 1)
            for dst, src in ((gate_a, lru_wa), (gate_x, lru_wx)):
                for b in range(2):
                    pool.dma_start(dst[64 * b:64 * b + 64, :, 64 * b:64 * b + 64],
                                   src.rearrange("(t b) i j -> b i t j", b=2)[b]).then_inc(sem("mix_c_landed"), 16)
            for k in range(3):
                pool.dma_start(sgu_sb[:, k, :], sgu_rows[k].partition_broadcast(128)).then_inc(sem("mix_c_landed"), 16)
            pool.dma_start(sgu_w[:, :, :], sgu_wsT).then_inc(sem("mix_c_landed"), 16)
            pool.dma_start(tri01[:, :], consts[:, CONST["tri01"]:CONST["tri01"] + 128]).then_inc(sem("mix_c_landed"), 16)
            for k in range(4):
                pool.wait_ge(x_ready, 2 * 16 + 4 * k + 4)
                pool.dma_start(x_spill[:, 4 * k:4 * k + 4, :], X[:, 4 * k:4 * k + 4, :]).then_inc(sem("x_spilled"), 16)
            pool.wait_ge(sem("group_normed"), 3)
            for k, name in enumerate(("chunk_tri", "chunk_all", "half_a", "half_b", "decay_mask", "strict01")):
                pool.dma_start(gdn_c[:, k, :], consts[:, CONST[name]:CONST[name] + 128]).then_inc(sem("mix_c_landed"), 16)
            pool.dma_start(ba_raw, w_ba).then_inc(sem("mix_c_landed"), 16)
            pool.dma_start(alog_sb, alog_dt.partition_broadcast(128)).then_inc(sem("mix_c_landed"), 16)
            pool.wait_ge(h_ready, 64)
            pool.wait_ge(sem("x_spilled"), 64)
            for k in range(4):
                pool.dma_start(X[:, 4 * k:4 * k + 4, :], x_spill[:, 4 * k:4 * k + 4, :]).then_inc(sem("x_back"), 16)
            for k in range(4):
                pool.wait_ge(x_ready, 48 + 4 * k + 4)
                pool.dma_start(x_spill2[:, 4 * k:4 * k + 4, :], X[:, 4 * k:4 * k + 4, :]).then_inc(sem("x_spilled"), 16)
            pool.wait_ge(sem("x_spilled"), 128)
            pool.wait_ge(h_ready, 80)
            pool.wait_ge(sq_ready, 96)
            pool.memset(y_acc[:, :, :], 0.0).then_inc(sem("acc_zeroed"), 1)
            pool.wait_ge(w_used, N_UNITS - U_DOWN - U_DOWN + 1)
            for k in range(4):
                pool.dma_start(x_back[:, 4 * k:4 * k + 4, :], x_spill2[:, 4 * k:4 * k + 4, :]).then_inc(sem("x_back"), 16)
            for k in range(4):
                pool.wait_ge(sem("out_tiles"), 4 * k + 4)
                pool.dma_start(out[:, 4 * k:4 * k + 4, :], y_acc[:, 4 * k:4 * k + 4, :]).then_inc(sem("out_stored"), 16)
            pool.wait_ge(sem("out_stored"), 64)

        @block.tensor
        def _(pe):
            pe.nop().then_inc(w_used, 1)
            pe.wait_ge(params_landed, 32)

            def sum_squares(stage):
                for t in range(KT):
                    pe.wait_ge(sq_ready, 16 * stage + t + 1)
                    pe.matmul(ps[:, SS, :], ones, squares[:, t % 2, :], start=(t == 0),
                              stop=(t == KT - 1)).then_inc(sq_used, 1)

            def project(u0, g0, quads, h0, hi=h_hi, lo=h_lo, lag=None):
                with pe.Fori(0, quads) as i:
                    for s in range(4):
                        g, half = s // 2, s % 2
                        pe.wait_ge(w_ready, u0 + 4 * i + s + 3)
                        if half == 0:
                            pe.wait_ge(bank_free, g0 + 2 * i + g + 1)
                        for k in range(8):
                            t = 8 * half + k
                            pe.wait_ge(h_ready, h0 + t + 1)
                            for j in range(2):
                                w = slice(k * 256 + j * 128, k * 256 + j * 128 + 128)
                                o = ps[:, 2 * g + j, :]
                                pe.matmul(o, w_hi[:, s % 2, w], hi[:, t, :], start=(t == 0), stop=False)
                                pe.matmul(o, w_hi[:, s % 2, w], lo[:, t, :], start=False, stop=False)
                                mm = pe.matmul(o, w_lo[:, s % 2, w], hi[:, t, :], start=False, stop=(t == 15))
                        mm.then_inc(w_used, 1)
                        if lag is not None and half == 0:
                            lag(i, g)

            def scores(n, q, k, r0, rows):
                for i in range(4):
                    if n >= 1:
                        pe.wait_ge(*since("l_scores_read", l, 4 * (n - 1) + i + 1))
                    pe.matmul(ps[:, i, 0:128 * (i + 1)], q[r0:r0 + rows, PAD + 128 * i:PAD + 128 * i + 128],
                              k[r0:r0 + rows, PAD:PAD + 128 * (i + 1)], start=True, stop=True)\
                      .then_inc(sem("l_scores"), 1)

            def turn_probs(n, buf):
                if n >= 1:
                    pe.wait_ge(*since("l_pt_a", l, n))
                    pe.wait_ge(*since("l_pt_b", l, n))
                for kt in (0, 1, 3, 2):
                    for i in range(kt, 4):
                        at = K_OFF[kt] + 128 * (i - kt)
                        mm = pe.transpose(ps[:, 4 + at // 512, at % 512:at % 512 + 128],
                                          probs[:, buf, Q_OFF[i] + 128 * kt:Q_OFF[i] + 128 * kt + 128], ident)
                mm.then_inc(sem("l_turned"), 1)

            def weigh_values(n, h, br):
                pe.wait_ge(*since("l_pt_a", l, n + 1))
                pe.wait_ge(*since("l_pt_b", l, n + 1))
                if n >= 1:
                    pe.wait_ge(*since("l_o_read", l, n))
                for i in range(4):
                    for kt in range(i + 1):
                        at = K_OFF[kt] + 128 * (i - kt)
                        mm = pe.matmul(ps[:, 7, 64 * i:64 * i + 64], probs_t[:, n % 2, at:at + 128],
                                       v_tok[:, kt, 256 * br + 64 * h:256 * br + 64 * h + 64],
                                       start=(kt == 0), stop=(kt == i))
                mm.then_inc(sem("l_o"), 1)

            def turn_outputs(tiles, n_read):
                pe.wait_ge(*since("l_o_read", l, n_read))
                for t in tiles:
                    for i in range(4):
                        mm = pe.transpose(ps[:, t, 128 * i:128 * i + 128], o_tok[:, i, 128 * t:128 * t + 128], ident)
                    mm.then_inc(sem("l_y_turned"), 1)

            def stick_scores(h):
                q, k = proj[:, 8 + h // 2, :], proj[:, 10 + h // 2, :]
                r0 = 64 * (h % 2)
                if h >= 1:
                    pe.wait_ge(sem("z_read"), 4 * h)
                for kt in range(4):
                    at = (0, 512, 1024, 1280)[kt]
                    mm = pe.matmul(ps[:, at // 512, at % 512:at % 512 + 512 - 128 * kt],
                                   k[r0:r0 + 64, PAD + 128 * kt:PAD + 128 * kt + 128],
                                   q[r0:r0 + 64, PAD + 128 * kt:PAD + 512], start=True, stop=True)
                mm.then_inc(sem("z_scores"), 1)

            def stick_suffix(h):
                pe.wait_ge(sem("sp_ready"), h + 1)
                if h >= 1:
                    pe.wait_ge(sem("tail_read"), 4 * h)
                sp_b = probs[:, 2 * (h % 2) + 1, :]
                for kt in range(4):
                    at = (0, 512, 1024, 1280)[kt]
                    n = 512 - 128 * kt
                    for k2 in range(kt, 4):
                        o = at % 512 + 128 * (k2 - kt)
                        mm = pe.matmul(ps[:, 4 + at // 512, o:at % 512 + n],
                                       attn_c[:, 1, :] if k2 == kt else ones,
                                       sp_b[:, Z_OFF[k2]:Z_OFF[k2] + 512 - 128 * k2],
                                       start=(k2 == kt), stop=(k2 == 3))
                    mm.then_inc(sem("tail"), 1)

            def stick_values(h):
                pe.wait_ge(sem("stick_a"), h + 1)
                a_b = probs[:, 2 * (h % 2), :]
                for kt in range(4):
                    mm = pe.matmul(ps[64 * (h % 2):64 * (h % 2) + 64, 3 if h < 2 else 7, 128 * kt:512],
                                   v_tok[:, kt, 256 + 64 * h:320 + 64 * h],
                                   a_b[:, Z_OFF[kt]:Z_OFF[kt] + 512 - 128 * kt], start=(kt == 0), stop=(kt == 3))
                mm.then_inc(sem("stick_o"), 1)

            def project_out(l):
                for q in range(4):
                    u = U_L[l] + U_IN + q
                    pe.wait_ge(w_ready, u + 3)
                    for j in range(4):
                        if q >= 1:
                            pe.wait_ge(x_ready, 16 * l + 4 * (q - 1) + j + 1)
                        for k in range(4):
                            if q == 0 and j == 0:
                                pe.wait_ge(*since("y1_ready", l, k + 1))
                            w = slice(k * 512 + j * 128, k * 512 + j * 128 + 128)
                            o = ps[:, OUT_BANKS[j], :]
                            pe.matmul(o, w_hi[:, q % 2, w], y1_hi[:, k, :], start=(k == 0), stop=False)
                            pe.matmul(o, w_hi[:, q % 2, w], y1_lo[:, k, :], start=False, stop=False)
                            mm = pe.matmul(o, w_lo[:, q % 2, w], y1_hi[:, k, :], start=False, stop=(k == 3))
                        if j < 3:
                            mm.then_inc(sem("out_tile"), 1)
                        else:
                            mm.then_inc(w_used, 1)
                        n = 4 * (q - 1) + j
                        if n >= 0:
                            pe.wait_ge(sq_ready, 16 * (l + 1) + n + 1)
                            pe.matmul(ps[:, SS, :], ones, squares[:, n % 2, :], start=(n == 0),
                                      stop=False).then_inc(sq_used, 1)
                for n in range(12, 16):
                    pe.wait_ge(sq_ready, 16 * (l + 1) + n + 1)
                    pe.matmul(ps[:, SS, :], ones, squares[:, n % 2, :], start=False,
                              stop=(n == 15)).then_inc(sq_used, 1)

            sum_squares(0)
            for l in range(2):
                project(U_L[l], G_L[l], 4, 16 * l)
                pe.wait_ge(*since("attn_c_landed", l, 16 * 8))
                pe.wait_ge(bank_free, G_L[l] + 8 + 2)
                for n, t in enumerate([0, 1, 2, 3, 8, 9, 10, 11] if l == 0 else [0, 1, 2, 3]):
                    if n >= 2:
                        pe.wait_ge(*since("rot_read", l, n - 1))
                    pe.matmul(ps[:, n % 2, :], attn_c[:, 0, :], proj[:, t, PAD:PAD + S], start=True,
                              stop=True).then_inc(sem("rotated"), 1)
                for tt in range(4):
                    for c, t in enumerate((4, 5, 12, 13)):
                        mm = pe.transpose(ps[:, 2 + tt, 128 * c:128 * c + 128],
                                          proj[:, t, PAD + 128 * tt:PAD + 128 * tt + 128], ident)
                    mm.then_inc(sem("v_turned"), 1)
                pe.wait_ge(*since("rot_read", l, 8 if l == 0 else 4))
                pe.wait_ge(*since("v_tok_ready", l, 4))
                if l == 0:
                    qk = [(proj[:, 8 * b + h // 2, :], proj[:, 8 * b + 2 + h // 2, :], 64 * (h % 2), 64)
                          for b in range(2) for h in range(4)]
                    pe.wait_ge(*since("roped", l, 8))
                    scores(0, *qk[0])
                    for n in range(8):
                        if n < 7:
                            scores(n + 1, *qk[n + 1])
                        pe.wait_ge(*since("l_probs", l, 4 * (n + 1)))
                        turn_probs(n, n % 4)
                        weigh_values(n, n % 4, n // 4)
                    turn_outputs(range(4), 8)
                else:
                    pe.wait_ge(*since("roped", l, 4))
                    qk = [(proj[:, h // 2, :], proj[:, 2 + h // 2, :], 64 * (h % 2) + 32 * c, 32)
                          for h in range(4) for c in range(2)]
                    scores(0, *qk[0])
                    scores(1, *qk[1])
                    for n in range(4):
                        if n < 3:
                            scores(2 * n + 2, *qk[2 * n + 2])
                            scores(2 * n + 3, *qk[2 * n + 3])
                        pe.wait_ge(sem("diff_probs"), n + 1)
                        turn_probs(n, 2 * (n % 2))
                        weigh_values(n, n, 0)
                    pe.wait_ge(sem("diff_normed"), 1)
                    turn_outputs(range(2), 4)
                    pe.wait_ge(*since("y_taken", l, 2))
                    pe.wait_ge(*since("l_scores_read", l, 32))
                    stick_scores(0)
                    for h in range(4):
                        if h < 3:
                            stick_scores(h + 1)
                        stick_suffix(h)
                        if h >= 1:
                            stick_values(h - 1)
                    stick_values(3)
                project_out(l)

            def group_norm(k, sq):
                for t in range(4):
                    pe.wait_ge(sem("group_sq"), 4 * k + t + 1)
                    mm = pe.matmul(ps[:, SS, :], ones, sq[:, t, :], start=(t == 0), stop=(t == 3))
                mm.then_inc(sem("group_sums"), 1)

            sum_squares(3)
            project(U_LRU, G_LRU, M2_QUADS["lru"], 32)
            pe.wait_ge(sem("mix_c_landed"), 16 * 9)
            for t in range(4):
                pe.wait_ge(sem("lru_conved"), t + 1)
                pe.matmul(ps[:, t, :], gate_a[:, t, :], lru_xc[:, t, :], start=True, stop=True).then_inc(sem("lru_gates"), 1)
                pe.matmul(ps[:, 4 + t, :], gate_x[:, t, :], lru_xc[:, t, :], start=True, stop=True).then_inc(sem("lru_gates"), 1)
            group_norm(0, Y[:, 8:12, :])
            project(U_SGU, G_SGU, M2_QUADS["sgu"], 32)
            pe.wait_ge(sem("sgu_gelu"), 2)
            pe.wait_ge(bank_free, G_SC + 2)
            for tt in range(4):
                for t in range(4):
                    mm = pe.transpose(ps[:, tt, 128 * t:128 * t + 128],
                                      proj[:, 12 + t, PAD + 128 * tt:PAD + 128 * tt + 128], ident)
                mm.then_inc(sem("sgu_turned"), 1)
            pe.wait_ge(sem("sgu_normed"), 1)
            for g in range(4):
                for tt in range(4):
                    mm = pe.matmul(ps[:, g, 128 * tt:128 * tt + 128], Y[:, 12 + tt, 128 * g:128 * g + 128],
                                   sgu_w[:, g, :], start=True, stop=True)
                mm.then_inc(sem("sgu_mixed"), 1)
            group_norm(1, Y[:, 12:16, :])
            project(U_SC, G_SC, M2_QUADS["sc"], 32)
            group_norm(2, Y[:, 0:4, :])
            project(U_QKVZ, G_QKVZ, M2_QUADS["qkvz"], 32)
            pe.wait_ge(sem("ba_split"), 1)
            pe.wait_ge(bank_free, G_WO2 + 2)
            for tt in range(4):
                for k in range(KT):
                    w = slice(8 * k, 8 * k + 8)
                    o = ps[:, 4, 8 * tt:8 * tt + 8]
                    x = slice(128 * tt, 128 * tt + 128)
                    pe.matmul(o, h_hi[:, k, x], ba_hi[:, w], start=(k == 0), stop=False)
                    pe.matmul(o, h_lo[:, k, x], ba_hi[:, w], start=False, stop=False)
                    mm = pe.matmul(o, h_hi[:, k, x], ba_lo[:, w], start=False, stop=(k == KT - 1))
            mm.then_inc(sem("ba_done"), 1)
            for tt in range(4):
                mm = pe.transpose(ps[:, 5, 128 * tt:128 * tt + 128], rstd[:, 128 * tt:128 * tt + 128], ident)
            mm.then_inc(sem("rstd_turned"), 1)
            pe.wait_ge(sem("gate_ready"), 1)
            for k in range(4):
                mm = pe.matmul(ps[:, 6, 16 * k:16 * k + 16], gdn_c[:, k, :], gate, start=True, stop=True)
            mm.then_inc(sem("g_summed"), 1)
            pe.wait_ge(sem("g_sums_read"), 1)
            for t in range(8):
                pe.wait_ge(sem("l2_sq"), t + 1)
                pe.matmul(ps[:, t, :], ones, conv_out[:, t, :], start=True, stop=True).then_inc(sem("l2_sums"), 1)
            pe.wait_ge(sem("l2_normed"), 8)

            def per_tile(o, lhs, rhs):
                for tt in range(4):
                    x = slice(128 * tt, 128 * tt + 128)
                    mm = pe.matmul(o[:, x], lhs[:, x], rhs[:, x], start=True, stop=True)
                return mm

            for pair in range(2):
                heads = [(m, 2 * pair + m, 4 * m) for m in range(2)]
                for m, h, b in heads:
                    if pair:
                        pe.wait_ge(sem("w_t_ready"), h - 1)
                        pe.wait_ge(sem("u_ready"), h - 1)
                    k, v = proj[:, 4 + h, PAD:], proj[:, 8 + h, PAD:]
                    for tt in range(4):
                        x = slice(128 * tt, 128 * tt + 128)
                        pe.transpose(ps[:, b, x], k[:, x], ident)
                        mm = pe.transpose(ps[:, b + 1, x], v[:, x], ident)
                    mm.then_inc(sem("kv_turned"), 1)
                    pe.wait_ge(sem("diags"), h + 1)
                    pe.matmul(ps[:, b + 2, :], ones, tmp_a[:, m, :], start=True, stop=True)
                    pe.matmul(ps[:, b + 3, :], ones, tmp_b[:, m, :], start=True, stop=True).then_inc(sem("rows_spread"), 1)
                for m, h, b in heads:
                    q, k = proj[:, h, PAD:], proj[:, 4 + h, PAD:]
                    pe.wait_ge(sem("kv_taken"), h + 1)
                    per_tile(ps[:, b, :], k, q).then_inc(sem("qk_done"), 1)
                    pe.wait_ge(sem("kb_ready"), h + 1)
                    per_tile(ps[:, b + 1, :], k, tmp_b[:, m, :]).then_inc(sem("kk_done"), 1)
                for m, h, b in heads:
                    pe.wait_ge(sem("nt_ready"), h + 1)
                    for tt in range(4):
                        x = slice(128 * tt, 128 * tt + 128)
                        mm = pe.transpose(ps[:, b + 2, x], pows[:, m, 0, 1, x], ident)
                    mm.then_inc(sem("n_turned"), 1)
                for it in range(5):
                    v, w = it % 2, 1 - it % 2
                    for m, h, b in heads:
                        n = (5 * pair + it) * 2 + m
                        n2 = (4 * pair + it) * 2 + m
                        if it == 0:
                            pe.wait_ge(sem("n_ready"), h + 1)
                            pe.wait_ge(sem("attn_ready"), h + 1)
                        per_tile(ps[:, b, :], pows[:, m, v, 1, :], pows[:, m, v, 0, :]).then_inc(sem("n_squared"), 1)
                        if it < 4:
                            per_tile(ps[:, b + 1, :], pows[:, m, v, 0, :], pows[:, m, v, 1, :]).then_inc(sem("nt_squared"), 1)
                    for m, h, b in heads:
                        n = (5 * pair + it) * 2 + m
                        pe.wait_ge(sem("n_power"), n + 1)
                        pe.wait_ge(sem("inv_ready"), (6 * pair + it) * 2 + m + 1)
                        per_tile(ps[:, b + 2, :], pows[:, m, w, 0, :], inv_t[:, h, :]).then_inc(sem("inv_step"), 1)
                        if it < 4:
                            pe.wait_ge(sem("nt_power"), (4 * pair + it) * 2 + m + 1)
                for m, h, b in heads:
                    pe.wait_ge(sem("inv_ready"), (6 * pair + 5) * 2 + m + 1)
                    per_tile(ps[:, b, :], k_be[:, h, :], inv_t[:, h, :]).then_inc(sem("w_t_done"), 1)
                    per_tile(ps[:, b + 1, :], inv_t[:, h, :], v_b[:, h, :]).then_inc(sem("u_done"), 1)
            pe.wait_ge(sem("w_t_ready"), 4)
            pe.wait_ge(sem("u_ready"), 4)
            for c in range(8):
                r, tt = 64 * (c % 2), c // 2
                x = slice(128 * tt + r, 128 * tt + r + 64)
                rows = slice(r, r + 64)
                pe.wait_ge(sem("state_ready"), c + 1)
                for h in range(4):
                    mm = pe.matmul(ps[rows, 0, 128 * h:128 * h + 128], w_t[:, h, x], state[:, c % 2, 128 * h:128 * h + 128],
                                   start=True, stop=True)
                mm.then_inc(sem("w_state"), 1)
                pe.wait_ge(sem("v_new_ready"), c + 1)
                for h in range(4):
                    mm = pe.matmul(ps[:, 3, 128 * h:128 * h + 128], k_g[rows, h, 128 * tt:128 * tt + 128],
                                   v_new[rows, 128 * h:128 * h + 128], start=True, stop=True)
                mm.then_inc(sem("state_add"), 1)
                if c >= 2:
                    pe.wait_ge(sem("o_taken"), c - 1)
                for h in range(4):
                    o = ps[:, 1 + c % 2, 64 * h:64 * h + 64]
                    pe.matmul(o, state[:, c % 2, 128 * h:128 * h + 128], proj[:, h, PAD + x.start:PAD + x.stop],
                              start=True, stop=False)
                    mm = pe.matmul(o, v_new[rows, 128 * h:128 * h + 128], attn_t[rows, h, x], start=False, stop=True)
                mm.then_inc(sem("o_done"), 1)
            for h in range(4):
                pe.wait_ge(sem("gdn_sq"), h + 1)
                pe.matmul(ps[:, 4 + h, :], ones, k_be[:, h, :], start=True, stop=True).then_inc(sem("gdn_sums"), 1)

            def project_y(i, quad):
                for s in range(4):
                    g, half = s // 2, s % 2
                    pe.wait_ge(w_ready, U_WO2 + 4 * i + s + 3)
                    if half == 0:
                        pe.wait_ge(bank_free, G_WO2 + 2 * i + g + 1)
                    for k in range(8):
                        t = 8 * half + k
                        pe.wait_ge(h_ready, 48 + t + 1)
                        for j in range(2):
                            w = slice(k * 256 + j * 128, k * 256 + j * 128 + 128)
                            o = ps[:, 2 * g + j, :]
                            pe.matmul(o, w_hi[:, s % 2, w], h_hi[:, t, :], start=(t == 0), stop=False)
                            pe.matmul(o, w_hi[:, s % 2, w], h_lo[:, t, :], start=False, stop=False)
                            mm = pe.matmul(o, w_lo[:, s % 2, w], h_hi[:, t, :], start=False, stop=(t == 15))
                    mm.then_inc(w_used, 1)
                    if half == 0 and not (quad == 0 and g == 0):
                        for j in range(2):
                            pe.wait_ge(sq_ready, 64 + 4 * i + (2 * (g - 1) + j + 1))
                            pe.matmul(ps[:, SS, :], ones, squares[:, j, :], start=(quad == 0 and j == 0),
                                      stop=False).then_inc(sq_used, 1)

            project_y(0, 0)
            with pe.Fori(1, 4) as i:
                project_y(i, 1)
            for j in range(2):
                pe.wait_ge(sq_ready, 64 + 14 + j + 1)
                pe.matmul(ps[:, SS, :], ones, squares[:, j, :], start=False, stop=(j == 1)).then_inc(sq_used, 1)
            sum_squares(5)

            def ffn_up(u, g):
                for s in range(8):
                    half = s % 2
                    pe.wait_ge(w_ready, u + s + 3)
                    if half == 0:
                        pe.wait_ge(bank_free, g + s // 2 + 1)
                    for k in range(8):
                        t = 8 * half + k
                        pe.wait_ge(h_ready, 64 + t + 1)
                        for j in range(2):
                            w = slice(k * 256 + j * 128, k * 256 + j * 128 + 128)
                            o = ps[:, 2 * (s // 2 % 2) + j, :]
                            pe.matmul(o, w_hi[:, s % 2, w], h_hi[:, t, :], start=(t == 0), stop=False)
                            pe.matmul(o, w_hi[:, s % 2, w], h_lo[:, t, :], start=False, stop=False)
                            mm = pe.matmul(o, w_lo[:, s % 2, w], h_hi[:, t, :], start=False, stop=(t == 15))
                    mm.then_inc(w_used, 1)

            def ffn_down(u, seg, par_, last=False):
                for q in range(4):
                    pe.wait_ge(w_ready, u + q + 3)
                    for j in range(4):
                        pe.wait_ge(down_free, seg * 16 + (4 * q + j + 1))
                        for k in range(4):
                            if q == 0 and j == 0:
                                pe.wait_ge(f_ready, seg * 2 + (k // 2 + 1))
                            w = slice(k * 512 + j * 128, k * 512 + j * 128 + 128)
                            o = ps[:, 4 + j, :]
                            pe.matmul(o, w_hi[:, q % 2, w], f_hi[:, par_, k, :], start=(k == 0), stop=False)
                            pe.matmul(o, w_hi[:, q % 2, w], f_lo[:, par_, k, :], start=False, stop=False)
                            mm = pe.matmul(o, w_lo[:, q % 2, w], f_hi[:, par_, k, :], start=False, stop=(k == 3))
                        mm.then_inc(w_used if j == 3 else down_tile, 1)
                        n = 4 * (q - 1) + j
                        if last and n >= 0:
                            pe.wait_ge(sq_ready, 96 + n + 1)
                            pe.matmul(ps[:, 0, :], ones, squares[:, n % 2, :], start=(n == 0),
                                      stop=False).then_inc(sq_used, 1)

            ffn_up(U_FFN, G_FFN)
            with pe.Fori(0, (SEGS - 1) // 2) as i:
                for e in range(2):
                    u = U_FFN + 8 + 24 * i + 12 * e
                    ffn_up(u, G_FFN + 4 + 8 * i + 4 * e)
                    ffn_down(u + 8, 2 * i + e, e)
            ffn_down(N_UNITS - 4, SEGS - 1, (SEGS - 1) % 2, last=True)
            for n in range(12, 16):
                pe.wait_ge(sq_ready, 96 + n + 1)
                pe.matmul(ps[:, 0, :], ones, squares[:, n % 2, :], start=False, stop=(n == 15)).then_inc(sq_used, 1)

        @block.scalar
        def _(act):
            order = Order(act, act_order)
            A = nc.scalar.activation

            def step_hi(u0, pairs, s):
                slot = (s + 1) % 2
                act.wait_ge(raw_landed[slot], (pairs + ((s + 1) // 2 + 1)) * 16)
                act.wait_ge(w_used, u0 + s + 1)
                A(w_hi[:, slot, :], raw[:, slot, :], ACT.Copy).then_inc(w_hi_ready, 1)

            def square(n, t_ap):
                if n >= 2:
                    act.wait_ge(sq_used, n - 1)
                A(squares[:, n % 2, :], t_ap, ACT.Square).then_inc(sq_ready, 1)

            def one_over_rms_root(n_sq, k):
                act.wait_ge(sq_used, n_sq)
                if k >= 1:
                    act.wait_ge(rstd_ready, k)
                A(root[:, :], ps[:, SS, :], ACT.Sqrt, bias=eps_c, scale=1.0 / D).then_inc(root_ready, 1)

            act.wait_ge(params_landed, 32)
            act.wait_ge(raw_landed[0], 16)
            A(w_hi[:, 0, :], raw[:, 0, :], ACT.Copy).then_inc(w_hi_ready, 1)
            for t in range(KT):
                act.wait_ge(x_landed[t // 4], 16)
                A(h_hi[:, t, :], X[:, t, :], ACT.Identity, scale=par("g0", t)).then_inc(h_hi_ready, 1)
                square(t, X[:, t, :])
            one_over_rms_root(16, 0)
            for l in range(2):
                with act.Fori(0, 4) as i:
                    for s in range(4):
                        step_hi(U_L[l] + 4 * i, U_L[l] // 2 + 2 * i, s)
                for tt in range(4):
                    act.wait_ge(*since("v_turned", l, tt + 1))
                    A(v_tok[:, tt, :], ps[:, 2 + tt, :], ACT.Copy).then_inc(sem("v_tok_ready"), 1)
                act.wait_ge(bank_free, G_L[l] + 8 + 2)
                for t in (6, 14):
                    A(proj[:, t:t + 2, PAD:], proj[:, t:t + 2, PAD:], ACT.Silu).then_inc(sem("gates"), 1)

                def exps(n, buf):
                    act.wait_ge(*since("neg_max", l, n + 1))
                    for i in range(4):
                        b = probs[:, buf, Q_OFF[i]:Q_OFF[i] + 128 * (i + 1)]
                        A(b, b, ACT.Exp, bias=neg_max[:, 4 * n + i:4 * n + i + 1],
                          accum_out=den[:, 4 * n + i:4 * n + i + 1]).then_inc(sem("l_probs"), 1)

                def take_pt_a(n):
                    act.wait_ge(*since("l_turned", l, n + 1))
                    if n >= 2:
                        act.wait_ge(*since("l_o", l, n - 1))
                    A(probs_t[:, n % 2, 0:512], ps[:, 4, :], ACT.Copy).then_inc(sem("l_pt_a"), 1)

                if l == 0:
                    exps(0, 0)
                    for n in range(8):
                        if n < 7:
                            exps(n + 1, (n + 1) % 4)
                        take_pt_a(n)
                else:
                    act.wait_ge(sem("lam_sums"), 2)
                    A(lam_s[:, 2:4], lam_s[:, 0:2], ACT.Exp).then_inc(sem("lam_exp"), 1)
                    exps(0, 0)
                    exps(1, 1)
                    for n in range(4):
                        if n < 3:
                            exps(2 * n + 2, (2 * n + 2) % 4)
                            exps(2 * n + 3, (2 * n + 3) % 4)
                        take_pt_a(n)
                    act.wait_ge(sem("diff_ss"), 1)
                    A(o_root, o_ss, ACT.Sqrt, bias=eps_c, scale=1.0 / HEAD).then_inc(sem("diff_root"), 1)

                def round_y(k):
                    act.wait_ge(*since("y1", l, k + 1))
                    A(y1_hi[:, k, :], y1[:, :], ACT.Copy).then_inc(sem("y1_hi_ready"), 1)

                if l == 1:
                    round_y(0)
                    round_y(1)

                    def stick_z(h):
                        z, L = probs[:, 2 * (h % 2), :], probs[:, 2 * (h % 2) + 1, :]
                        act.wait_ge(sem("z_scores"), h + 1)
                        if h >= 2:
                            act.wait_ge(sem("stick_o"), h - 1)
                        for kt in range(4):
                            at = (0, 512, 1024, 1280)[kt]
                            n = 512 - 128 * kt
                            A(z[:, Z_OFF[kt]:Z_OFF[kt] + n], ps[:, at // 512, at % 512:at % 512 + n], ACT.Copy,
                              scale=HEAD ** -0.5).then_inc(sem("z_read"), 1)
                        act.wait_ge(sem("z_read"), 4 * h + 4)
                        order.link(A(L, z, ACT.Abs))
                        order.link(A(L, L, ACT.Exp, scale=-1.0))
                        A(L, L, ACT.Ln, bias=one_c).then_inc(sem("log1p"), 1)

                    def stick_exp(h):
                        z = probs[:, 2 * (h % 2), :]
                        act.wait_ge(sem("log_a"), h + 1)
                        A(z, z, ACT.Exp).then_inc(sem("stick_a"), 1)

                    stick_z(0)
                    for h in range(4):
                        if h < 3:
                            stick_z(h + 1)
                        stick_exp(h)
                    round_y(2)
                    round_y(3)
                else:
                    for k in range(4):
                        round_y(k)
                for q in range(4):
                    step_hi(U_L[l] + U_IN, (U_L[l] + U_IN) // 2, q)
                    for j in range(4):
                        t = 4 * q + j
                        act.wait_ge(x_ready, 16 * l + t + 1)
                        if l == 0:
                            A(h_hi[:, t, :], X[:, t, :], ACT.Identity, scale=par("g1", t)).then_inc(h_hi_ready, 1)
                        square(16 * (l + 1) + t, X[:, t, :])
                one_over_rms_root(16 * (l + 2), l + 1)

            def split_tiles(x0, n0, gain):
                for t in range(KT):
                    act.wait_ge(x_ready, x0 + t + 1)
                    A(h_hi[:, t, :], X[:, t, :], ACT.Identity, scale=par(gain, t)).then_inc(h_hi_ready, 1)
                    square(n0 + t, X[:, t, :])

            def steps_hi(u0, quads):
                with act.Fori(0, quads) as i:
                    for s in range(4):
                        step_hi(u0 + 4 * i, u0 // 2 + 2 * i, s)

            def group_norm(k, y, sq):
                act.wait_ge(sem("mixer_out"), k + 1)
                for t in range(4):
                    A(sq[:, t, :], y[:, t, :], ACT.Square).then_inc(sem("group_sq"), 1)
                act.wait_ge(sem("group_sums"), k + 1)
                A(root[:, :], ps[:, SS, :], ACT.Sqrt, bias=eps_c, scale=1.0 / 512).then_inc(sem("group_root"), 1)

            split_tiles(32, 48, "pre_mix")
            one_over_rms_root(64, 3)
            order.link(A(lru_s[:, 0:4], par("lam", 0, 4), ACT.Abs))
            order.link(A(lru_s[:, 0:4], lru_s[:, 0:4], ACT.Exp, scale=-1.0))
            A(lru_s[:, 4:8], lru_s[:, 0:4], ACT.Ln, bias=one_c).then_inc(sem("lam_log"), 1)
            steps_hi(U_LRU, M2_QUADS["lru"])
            for t in range(4):
                act.wait_ge(sem("lru_gates"), 2 * t + 1)
                A(lru_r[:, t, :], ps[:, t, :], ACT.Sigmoid, bias=par("ba", t)).then_inc(sem("lru_sig"), 1)
                act.wait_ge(sem("lru_gates"), 2 * t + 2)
                A(lru_i[:, t, :], ps[:, 4 + t, :], ACT.Sigmoid, bias=par("bx", t)).then_inc(sem("lru_sig"), 1)
            act.wait_ge(sem("lru_rate"), 1)
            act.wait_ge(sem("lru_sig"), 8)
            for t in range(4):
                A(lru_a[:, t, :], lru_r[:, t, :], ACT.Exp, scale=lru_s[:, 8 + t:9 + t]).then_inc(sem("lru_a"), 1)
            for t in range(4):
                A(lru_r[:, t, :], lru_r[:, t, :], ACT.Tanh, scale=lru_s[:, 8 + t:9 + t]).then_inc(sem("lru_tanh"), 1)
            A(proj[:, 4:8, PAD:], proj[:, 4:8, PAD:], ACT.Gelu_apprx_tanh).then_inc(sem("lru_gelu"), 1)
            act.wait_ge(sem("lru_m"), 1)
            A(lru_r, lru_r, ACT.Sqrt, scale=-1.0).then_inc(sem("lru_mult"), 1)
            group_norm(0, Y[:, 4:8, :], Y[:, 8:12, :])
            steps_hi(U_SGU, M2_QUADS["sgu"])
            act.wait_ge(bank_free, G_SC + 2)
            for t in (12, 8):
                A(proj[:, t:t + 4, PAD:], proj[:, t:t + 4, PAD:], ACT.Gelu_apprx_tanh).then_inc(sem("sgu_gelu"), 1)
            act.wait_ge(sem("sgu_stats"), 1)
            A(stats[:, :, 8:9], stats[:, :, 7:8], ACT.Sqrt, bias=eps_c).then_inc(sem("sgu_root"), 1)
            group_norm(1, Y[:, 8:12, :], Y[:, 12:16, :])
            steps_hi(U_SC, M2_QUADS["sc"])
            group_norm(2, Y[:, 12:16, :], Y[:, 0:4, :])
            act.wait_ge(sem("mix_c_landed"), 16 * 17)
            A(ba_hi[:, :], ba_raw, ACT.Copy).then_inc(sem("ba_hi_ready"), 1)
            steps_hi(U_QKVZ, M2_QUADS["qkvz"])
            act.wait_ge(sem("ba_tok"), 1)
            A(beta.rearrange("p (h t) -> p t h", h=4), ba_tok.rearrange("p (t c) -> p t c", c=8)[:, :, 0:4],
              ACT.Sigmoid).then_inc(sem("beta_ready"), 1)
            act.wait_ge(sem("a_dt"), 1)
            A(alog_sb[:, 0:4], alog_sb[:, 0:4], ACT.Exp).then_inc(sem("a_exp"), 1)
            order.link(A(exp_g, g_tmp, ACT.Abs))
            order.link(A(exp_g, exp_g, ACT.Exp, scale=-1.0))
            A(exp_g, exp_g, ACT.Ln, bias=one_c).then_inc(sem("a_log1p"), 1)
            act.wait_ge(sem("g_sums_read"), 1)
            A(exp_g, g_sums[:, 0:16], ACT.Exp).then_inc(sem("exp_g_ready"), 1)
            A(g_last, g_sums[:, 32:64], ACT.Exp).then_inc(sem("exp_g_ready"), 1)
            act.wait_ge(sem("kgs_log"), 1)
            A(kgs, kgs, ACT.Exp).then_inc(sem("exp_g_ready"), 1)
            for k in range(3):
                act.wait_ge(sem("qkv_conved"), k + 1)
                A(proj[:, 4 * k:4 * k + 4, PAD:], conv_out[:, 4 * k:4 * k + 4, :], ACT.Silu).then_inc(sem("qkv_silu"), 1)
            A(proj[:, 12:16, PAD:], proj[:, 12:16, PAD:], ACT.Silu).then_inc(sem("z_silu"), 1)
            act.wait_ge(sem("qkv_silu"), 3)
            for t in range(8):
                A(conv_out[:, t, :], proj[:, t, PAD:], ACT.Square).then_inc(sem("l2_sq"), 1)
            for t in range(8):
                act.wait_ge(sem("l2_sums"), t + 1)
                A(conv_out[:, t, :], ps[:, t, :], ACT.Sqrt, bias=eps_c).then_inc(sem("l2_root"), 1)
            for pair in range(2):
                heads = [(m, 2 * pair + m, 4 * m) for m in range(2)]
                for m, h, b in heads:
                    act.wait_ge(sem("rows_spread"), h + 1)
                    if pair:
                        act.wait_ge(sem("inv_step"), 2 * 5 * pair)
                    A(pows[:, m, 1, 0, :], ps[:, b + 2, :], ACT.Exp).then_inc(sem("exp_row"), 1)
                    act.wait_ge(sem("decay_log"), h + 1)
                    A(tmp_a[:, m, :], tmp_a[:, m, :], ACT.Exp).then_inc(sem("decay_ready"), 1)
                for m, h, b in heads:
                    act.wait_ge(sem("n_turned"), h + 1)
                    A(pows[:, m, 0, 0, :], ps[:, b + 2, :], ACT.Copy).then_inc(sem("n_ready"), 1)
                for it in range(5):
                    for m, h, b in heads:
                        n = (5 * pair + it) * 2 + m
                        act.wait_ge(sem("n_squared"), n + 1)
                        if it == 0:
                            act.wait_ge(sem("q_scaled"), h + 1)
                        A(pows[:, m, 1 - it % 2, 0, :], ps[:, b, :], ACT.Copy).then_inc(sem("n_power"), 1)
                for m, h, b in heads:
                    act.wait_ge(sem("w_t_done"), h + 1)
                    A(w_t[:, h, :], ps[:, b, :], ACT.Copy).then_inc(sem("w_t_ready"), 1)
            for c in range(8):
                act.wait_ge(sem("o_done"), c + 1)
                A(proj[:, 8:12, PAD + 64 * c:PAD + 64 * c + 64], ps[:, 1 + c % 2, 0:256].rearrange("p (h n) -> p h n", h=4),
                  ACT.Copy).then_inc(sem("o_taken"), 1)
            act.wait_ge(sem("o_taken"), 8)
            for h in range(4):
                A(k_be[:, h, :], proj[:, 8 + h, PAD:], ACT.Square).then_inc(sem("gdn_sq"), 1)
            for h in range(4):
                act.wait_ge(sem("gdn_sums"), h + 1)
                A(k_g[:, h, :], ps[:, 4 + h, :], ACT.Sqrt, bias=eps_c, scale=1.0 / GDN_D).then_inc(sem("gdn_root"), 1)

            act.wait_ge(sem("mixer_out"), 4)
            with act.Fori(0, 16) as i:
                A(h_hi[:, i, :], Y[:, i, :], ACT.Copy).then_inc(h_hi_ready, 1)
            for g in range(8):
                for s in range(2):
                    step_hi(U_WO2 + 2 * g, U_WO2 // 2 + g, s)
                act.wait_ge(bank_free, G_WO2 + g + 3)
                for t in (2 * g, 2 * g + 1):
                    square(64 + t, y2[:, t, :])
            one_over_rms_root(80, 4)
            split_tiles(48, 80, "pre_ffn")
            one_over_rms_root(96, 5)

            def ffn_up(u, pairs, seg, par_):
                for s in range(8):
                    step_hi(u, pairs, s)
                    b, c = s // 4, s // 2 % 2
                    if s % 2 and c == 0:
                        act.wait_ge(sem("f_gates"), seg * 2 + (b + 1))
                        A(f_gate[:, :, :], f_gate[:, :, :], ACT.Gelu_apprx_tanh).then_inc(sem("f_gelu"), 1)
                    if s % 2 and c == 1:
                        act.wait_ge(sem("f_gated"), seg * 2 + (b + 1))
                        A(f_hi[:, par_, 2 * b:2 * b + 2, :], f_val[:, :, :], ACT.Copy).then_inc(sem("f_hi_ready"), 1)

            def ffn_down(u, pairs):
                for q in range(4):
                    step_hi(u, pairs, q)

            ffn_up(U_FFN, U_FFN // 2, 0, 0)
            with act.Fori(0, (SEGS - 1) // 2) as i:
                for e in range(2):
                    off = 8 + 12 * e
                    ffn_up(U_FFN + off + 24 * i, (U_FFN + off) // 2 + 12 * i, 2 * i + (1 + e), 1 - e)
                    ffn_down(U_FFN + off + 8 + 24 * i, (U_FFN + off + 8) // 2 + 12 * i)
            for q in range(4):
                if q < 3:
                    step_hi(N_UNITS - 4, (N_UNITS - 4) // 2, q)
                for j in range(4):
                    n = 4 * q + j
                    act.wait_ge(down_free, 4 + 16 * (SEGS - 1) + n + 1)
                    square(96 + n, y_acc[:, n, :])
            act.wait_ge(sq_used, 112)
            act.wait_ge(rstd_ready, 6)
            A(root[:, :], ps[:, 0, :], ACT.Sqrt, bias=eps_c, scale=1.0 / D).then_inc(root_ready, 1)

        @block.vector
        def _(dve):
            order = Order(dve, dve_order)
            V = nc.vector

            def step_lo(u0, s):
                slot = (s + 1) % 2
                dve.wait_ge(w_hi_ready, u0 + s + 2)
                V.tensor_tensor(w_lo[:, slot, :], raw[:, slot, :], w_hi[:, slot, :].bitcast(F32),
                                ALU.subtract).then_inc(w_ready, 1)

            def low_part(n, t, g):
                dve.wait_ge(h_hi_ready, n + 1)
                V.scalar_tensor_tensor(out=h_lo[:, t, :], in0=X[:, t, :], scalar=g,
                                       in1=h_hi[:, t, :].bitcast(F32), op0=ALU.mult,
                                       op1=ALU.subtract).then_inc(h_ready, 1)

            def one_over_root(k):
                dve.wait_ge(root_ready, k + 1)
                V.reciprocal(rstd[:, :], root[:, :]).then_inc(rstd_ready, 1)
                dve.wait_ge(rstd_ready, k + 1)

            def project(u0, quads, tile0):
                with dve.Fori(0, quads) as i:
                    for s in range(4):
                        step_lo(u0 + 4 * i, s)
                        if s % 2:
                            dve.wait_ge(w_used, u0 + 4 * i + s + 1 + 1)
                            for j in range(2):
                                ins = V.tensor_tensor(proj[:, 4 * i + (tile0 + s - 1 + j), PAD:PAD + S],
                                                      ps[:, s - 1 + j, :], rstd[:, :], ALU.mult)
                            ins.then_inc(bank_free, 1)

            V.memset(credit[:, 0:1], 0.0).then_inc(bank_free, 1)
            V.memset(credit[:, 1:2], 0.0).then_inc(bank_free, 1)
            V.memset(credit[:, 4:5], 0.0).then_inc(w_ready, 1)
            V.memset(credit[:, 5:6], 0.0).then_inc(w_ready, 1)
            dve.wait_ge(params_landed, 32)
            dve.wait_ge(w_hi_ready, 1)
            V.tensor_tensor(w_lo[:, 0, :], raw[:, 0, :], w_hi[:, 0, :].bitcast(F32),
                            ALU.subtract).then_inc(w_ready, 1)
            for t in range(KT):
                low_part(t, t, par("g0", t))
            one_over_root(0)
            for l in range(2):
                project(U_L[l], 4, 0)
                dve.wait_ge(bank_free, G_L[l] + 8 + 2)
                dve.wait_ge(*since("attn_c_landed", l, 16 * 8))
                for n, t in enumerate([0, 1, 2, 3, 8, 9, 10, 11] if l == 0 else [0, 1, 2, 3]):
                    tile = proj[:, t, PAD:PAD + S]
                    dve.wait_ge(*since("rotated", l, n + 1))
                    V.tensor_tensor(rot_sin[:, n % 2, :], ps[:, n % 2, :], sin_sb[:, :], ALU.mult)\
                     .then_inc(sem("rot_read"), 1)
                    order.link(V.tensor_tensor(tile, tile, cos_sb[:, :], ALU.mult))
                    dve.wait_ge(*since("rot_read", l, n + 1))
                    V.tensor_tensor(tile, tile, rot_sin[:, n % 2, :], ALU.add).then_inc(sem("roped"), 1)

                def mask_scores(n, buf, mask, scale, free=None):
                    if free is not None:
                        dve.wait_ge(*free)
                    for i in range(4):
                        dve.wait_ge(*since("l_scores", l, 4 * n + i + 1))
                        V.tensor_tensor_reduce(
                            out=probs[:, buf, Q_OFF[i]:Q_OFF[i] + 128 * (i + 1)], in0=ps[:, i, 0:128 * (i + 1)],
                            in1=mask_sb[:, mask, 128 * (3 - i):512], scale=scale, scalar=-3.0e38, op0=ALU.add,
                            op1=ALU.max, accum_out=row_max[:, 4 * n + i:4 * n + i + 1])\
                         .then_inc(sem("l_scores_read"), 1)
                    dve.wait_ge(*since("l_scores_read", l, 4 * n + 4))
                    V.tensor_scalar(neg_max[:, 4 * n:4 * n + 4], row_max[:, 4 * n:4 * n + 4], -1.0, None,
                                    ALU.mult).then_inc(sem("neg_max"), 1)

                def take_pt_b(n):
                    dve.wait_ge(*since("l_turned", l, n + 1))
                    if n >= 2:
                        dve.wait_ge(*since("l_o", l, n - 1))
                    V.tensor_copy(probs_t[:, n % 2, 512:1280],
                                  ps[:, 5:7, :].rearrange("p b n -> p (b n)")[:, 0:768])\
                     .then_inc(sem("l_pt_b"), 1)

                def finish_y(k, src, gate_t, scale=None):
                    if k >= 1:
                        dve.wait_ge(*since("y1_ready", l, k))
                    if scale is None:
                        V.tensor_tensor(y1[:, :], src, proj[:, gate_t, PAD:], ALU.mult).then_inc(sem("y1"), 1)
                    else:
                        V.scalar_tensor_tensor(out=y1[:, :], in0=src, scalar=scale, in1=proj[:, gate_t, PAD:],
                                               op0=ALU.mult, op1=ALU.mult).then_inc(sem("y1"), 1)
                    dve.wait_ge(*since("y1_hi_ready", l, k + 1))
                    V.tensor_tensor(y1_lo[:, k, :], y1[:, :], y1_hi[:, k, :].bitcast(F32),
                                    ALU.subtract).then_inc(sem("y1_ready"), 1)

                def wait_gates():
                    dve.wait_ge(*since("gates", l, 2))

                if l == 0:
                    mask_scores(0, 0, 0, HEAD ** -0.5)
                    for n in range(8):
                        if n < 7:
                            mask_scores(n + 1, (n + 1) % 4, (n + 1) // 4, HEAD ** -0.5,
                                        since("l_turned", l, n - 2) if n >= 3 else None)
                        dve.wait_ge(*since("l_probs", l, 4 * n + 4))
                        order.link(V.reciprocal(rden[:, 4 * n:4 * n + 4], den[:, 4 * n:4 * n + 4]))
                        take_pt_b(n)
                        dve.wait_ge(*since("l_o", l, n + 1))
                        V.tensor_tensor(o_tok[:, :, 64 * n:64 * n + 64],
                                        ps[:, 7, 0:256].rearrange("p (i d) -> p i d", d=64),
                                        bc(rden[:, 4 * n:4 * n + 4], 64), ALU.mult)\
                         .then_inc(sem("l_o_read"), 1)
                    wait_gates()
                    for k in range(4):
                        dve.wait_ge(*since("l_y_turned", l, k + 1))
                        finish_y(k, ps[:, k, :], (6, 7, 14, 15)[k])
                else:
                    lambda_init = 0.8 - 0.6 * float(np.exp(-0.3))
                    dve.wait_ge(sem("lam_landed"), 16)
                    for k in range(2):
                        V.tensor_tensor_reduce(out=lam_prod, in0=lam_sb[:, 64 * k:64 * k + 32],
                                               in1=lam_sb[:, 64 * k + 32:64 * k + 64], scale=1.0, scalar=0.0,
                                               op0=ALU.mult, op1=ALU.add, accum_out=lam_s[:, k:k + 1])\
                         .then_inc(sem("lam_sums"), 1)
                        dve.wait_ge(sem("lam_sums"), k + 1)
                    dve.wait_ge(sem("lam_exp"), 1)
                    order.link(V.tensor_tensor(lam_s[:, 4:5], lam_s[:, 3:4], lam_s[:, 2:3], ALU.subtract))
                    order.link(V.tensor_scalar(lam_s[:, 5:6], lam_s[:, 4:5], -lambda_init, None, ALU.add))
                    mask_scores(0, 0, 1, 32 ** -0.5)
                    mask_scores(1, 1, 1, 32 ** -0.5)
                    for n in range(4):
                        if n < 3:
                            mask_scores(2 * n + 2, (2 * n + 2) % 4, 1, 32 ** -0.5,
                                        since("l_turned", l, n) if n >= 1 else None)
                            mask_scores(2 * n + 3, (2 * n + 3) % 4, 1, 32 ** -0.5)
                        dve.wait_ge(*since("l_probs", l, 8 * n + 8))
                        order.link(V.reciprocal(rden[:, 8 * n:8 * n + 8], den[:, 8 * n:8 * n + 8]))
                        order.link(V.tensor_scalar(rden[:, 8 * n + 4:8 * n + 8], rden[:, 8 * n + 4:8 * n + 8],
                                                   lam_s[:, 5:6], None, ALU.mult))
                        b0 = 2 * (n % 2)
                        for i in range(4):
                            b = slice(Q_OFF[i], Q_OFF[i] + 128 * (i + 1))
                            ins = V.tensor_scalar(probs[:, b0, b], probs[:, b0, b],
                                                  rden[:, 8 * n + i:8 * n + i + 1], None, ALU.mult)
                        order.link(ins)
                        for i in range(4):
                            b = slice(Q_OFF[i], Q_OFF[i] + 128 * (i + 1))
                            ins = V.scalar_tensor_tensor(out=probs[:, b0, b], in0=probs[:, b0 + 1, b],
                                                         scalar=rden[:, 8 * n + 4 + i:8 * n + 5 + i],
                                                         in1=probs[:, b0, b], op0=ALU.mult, op1=ALU.add)
                        ins.then_inc(sem("diff_probs"), 1)
                        take_pt_b(n)
                        dve.wait_ge(*since("l_o", l, n + 1))
                        V.tensor_copy(o_tok[:, :, 64 * n:64 * n + 64],
                                      ps[:, 7, 0:256].rearrange("p (i d) -> p i d", d=64))\
                         .then_inc(sem("l_o_read"), 1)
                    dve.wait_ge(*since("l_o_read", l, 4))
                    order.link(V.tensor_tensor(o_tok[:, :, 256:512], o_tok[:, :, 0:256], o_tok[:, :, 0:256], ALU.mult))
                    V.tensor_reduce(o_ss, o_tok[:, :, 256:512].rearrange("p i (h d) -> p i h d", d=64), AX,
                                    ALU.add).then_inc(sem("diff_ss"), 1)
                    dve.wait_ge(sem("diff_root"), 1)
                    order.link(V.reciprocal(o_rstd, o_root))
                    order.link(V.tensor_scalar(o_rstd, o_rstd, 1.0 - lambda_init, None, ALU.mult))
                    for i in range(4):
                        o = o_tok[:, i, 0:256].rearrange("p (h d) -> p h d", d=64)
                        ins = V.tensor_tensor(o, o, bc(o_rstd[:, 4 * i:4 * i + 4], 64), ALU.mult)
                    ins.then_inc(sem("diff_normed"), 1)
                    wait_gates()
                    for k in range(2):
                        dve.wait_ge(*since("l_y_turned", l, k + 1))
                        finish_y(k, ps[:, k, :], 6 + k, par("subln"))
                        V.memset(credit[:, 8 + k:9 + k], 0.0).then_inc(sem("y_taken"), 1)

                    def stick_sp(h):
                        z, L = probs[:, 2 * (h % 2), :], probs[:, 2 * (h % 2) + 1, :]
                        dve.wait_ge(sem("log1p"), h + 1)
                        order.link(V.scalar_tensor_tensor(out=L, in0=z, scalar=0.0, in1=L, op0=ALU.max, op1=ALU.add))
                        for kt in range(4):
                            b = L[:, Z_OFF[kt]:Z_OFF[kt] + 128]
                            ins = V.tensor_tensor(b, b, attn_c[:, 2, :], ALU.mult)
                        ins.then_inc(sem("sp_ready"), 1)

                    def stick_log(h):
                        z = probs[:, 2 * (h % 2), :]
                        for kt in range(4):
                            at = (0, 512, 1024, 1280)[kt]
                            n = 512 - 128 * kt
                            dve.wait_ge(sem("tail"), 4 * h + min(kt + 1, 2) + 2 * (kt >= 2))
                            V.tensor_tensor(z[:, Z_OFF[kt]:Z_OFF[kt] + n], z[:, Z_OFF[kt]:Z_OFF[kt] + n],
                                            ps[:, 4 + at // 512, at % 512:at % 512 + n],
                                            ALU.subtract).then_inc(sem("tail_read"), 1)
                        dve.wait_ge(sem("tail_read"), 4 * h + 4)
                        for kt in range(4):
                            b = z[:, Z_OFF[kt]:Z_OFF[kt] + 128]
                            ins = V.tensor_tensor(b, b, attn_c[:, 3, :], ALU.add)
                        ins.then_inc(sem("log_a"), 1)

                    stick_sp(0)
                    for h in range(4):
                        if h < 3:
                            stick_sp(h + 1)
                        stick_log(h)
                    dve.wait_ge(sem("stick_o"), 4)
                    for k in range(2):
                        finish_y(2 + k, ps[:, 3 if k == 0 else 7, :], 14 + k)
                for q in range(4):
                    step_lo(U_L[l] + U_IN, q)
                    for j in range(4):
                        t = 4 * q + j
                        if j < 3:
                            dve.wait_ge(sem("out_tile"), 12 * l + 3 * q + j + 1)
                        else:
                            dve.wait_ge(w_used, U_L[l] + U_IN + q + 1 + 1)
                        V.tensor_tensor(X[:, t, :], X[:, t, :], ps[:, OUT_BANKS[j], :], ALU.add).then_inc(x_ready, 1)
                        if l == 0 and t >= 1:
                            low_part(16 + t - 1, t - 1, par("g1", t - 1))
                if l == 0:
                    low_part(31, 15, par("g1", 15))
                one_over_root(l + 1)

            def low_pair(n0, i, gain):
                for s in range(2):
                    dve.wait_ge(h_hi_ready, n0 + 2 * i + s + 1)
                    V.scalar_tensor_tensor(out=h_lo[:, 2 * i + s, :], in0=X[:, 2 * i + s, :], scalar=dpar(gain, 2 * i + s),
                                           in1=h_hi[:, 2 * i + s, :].bitcast(F32), op0=ALU.mult,
                                           op1=ALU.subtract).then_inc(h_ready, 1)

            def conv(outs, ins, taps, pad, last, bias=None):
                n = len(taps[0])
                for k in range(n):
                    for r, (o, x) in enumerate(zip(outs, ins)):
                        xk = x[:, pad - n + 1 + k:pad - n + 1 + k + S]
                        if k == 0:
                            ins_ = V.tensor_scalar(o, xk, taps[r][0], bias[r] if bias else None, ALU.mult,
                                                   ALU.add if bias else ALU.bypass)
                        else:
                            ins_ = V.scalar_tensor_tensor(out=o, in0=xk, scalar=taps[r][k], in1=o, op0=ALU.mult, op1=ALU.add)
                        if last is not None and k == n - 1:
                            ins_.then_inc(last, 1)
                    if k < n - 1:
                        order.link(ins_)
                return ins_

            def group_norm(k, y):
                dve.wait_ge(sem("group_root"), k + 1)
                order.link(V.reciprocal(rstd_g, root[:, :]))
                for t in range(4):
                    ins = V.scalar_tensor_tensor(out=y[:, t, :], in0=y[:, t, :], scalar=par("grp", 4 * k + t), in1=rstd_g,
                                                 op0=ALU.mult, op1=ALU.mult)
                ins.then_inc(sem("group_normed"), 1)

            with dve.Fori(0, 8) as i:
                for s in range(2):
                    t = 2 * i + s
                    V.scalar_tensor_tensor(out=X[:, t, :], in0=X[:, t, :], scalar=dpar("final", t), in1=rstd[:, :],
                                           op0=ALU.mult, op1=ALU.mult).then_inc(x_ready, 1)
                low_pair(32, i, "pre_mix")
            one_over_root(3)
            dve.wait_ge(sem("lam_log"), 1)
            order.link(V.tensor_scalar(lru_s[:, 12:16], par("lam", 0, 4), -1.0, 0.0, ALU.mult, ALU.max))
            order.link(V.tensor_tensor(lru_s[:, 16:20], lru_s[:, 12:16], lru_s[:, 4:8], ALU.add))
            V.tensor_scalar(lru_s[:, 8:12], lru_s[:, 16:20], -8.0, None, ALU.mult).then_inc(sem("lru_rate"), 1)
            dve.wait_ge(sem("pads_ready"), 1)
            project(U_LRU, M2_QUADS["lru"], 0)
            dve.wait_ge(bank_free, G_SGU + 2)
            dve.wait_ge(sem("x_spilled"), 64)
            conv([lru_xc[:, t, :] for t in range(4)], [proj[:, t, :] for t in range(4)],
                 [[par("lru_conv", 4 * t + k) for k in range(4)] for t in range(4)], PAD, sem("lru_conved"),
                 [par("lru_b", t) for t in range(4)])
            dve.wait_ge(sem("lru_a"), 4)
            order.link(V.tensor_tensor(lru_a2, lru_a, lru_a, ALU.mult))
            dve.wait_ge(sem("lru_tanh"), 4)
            V.scalar_tensor_tensor(out=lru_r, in0=lru_a2, scalar=1.0, in1=lru_r, op0=ALU.add, op1=ALU.mult)\
             .then_inc(sem("lru_m"), 1)
            order.link(V.tensor_tensor(lru_i, lru_i, lru_xc, ALU.mult))
            dve.wait_ge(sem("lru_mult"), 1)
            order.link(V.tensor_tensor(lru_i, lru_i, lru_r, ALU.mult))
            for t in range(4):
                ins = V.tensor_tensor_scan(lru_xc[:, t, :], lru_a[:, t, :], lru_i[:, t, :], 0.0, ALU.mult, ALU.add)
            order.link(ins)
            dve.wait_ge(sem("lru_gelu"), 1)
            V.tensor_tensor(Y[:, 4:8, :], lru_xc, proj[:, 4:8, PAD:], ALU.mult).then_inc(sem("mixer_out"), 1)
            group_norm(0, Y[:, 4:8, :])
            project(U_SGU, M2_QUADS["sgu"], 8)
            dve.wait_ge(sem("mix_c_landed"), 16 * 9)
            order.link(V.tensor_tensor(sgu_w[:, :, :], sgu_w[:, :, :], bm(tri01[:, :], 4), ALU.mult))
            for tt in range(4):
                dve.wait_ge(sem("sgu_turned"), tt + 1)
                ins = V.bn_stats(stats[:, tt, 0:6], ps[:, tt, :])
            order.link(ins)
            for tt in range(4):
                ins = V.bn_aggr(stats[:, tt, 6:8], stats[:, tt, 0:6])
            ins.then_inc(sem("sgu_stats"), 1)
            dve.wait_ge(sem("sgu_root"), 1)
            order.link(V.reciprocal(stats[:, :, 9:10], stats[:, :, 8:9]))
            dve.wait_ge(sem("group_normed"), 1)
            for tt in range(4):
                ins = V.tensor_scalar(Y[:, 12 + tt, :], ps[:, tt, :], stats[:, tt, 6:7], stats[:, tt, 9:10],
                                      ALU.subtract, ALU.mult)
            order.link(ins)
            order.link(V.tensor_tensor(Y[:, 12:16, :], Y[:, 12:16, :], bm(sgu_sb[:, 0, :], 4), ALU.mult))
            V.tensor_tensor(Y[:, 12:16, :], Y[:, 12:16, :], bm(sgu_sb[:, 1, :], 4), ALU.add).then_inc(sem("sgu_normed"), 1)
            for g in range(4):
                dve.wait_ge(sem("sgu_mixed"), g + 1)
                ins = V.tensor_tensor(Y[:, 8 + g, :].rearrange("p (n t) -> p n t", t=128),
                                      ps[:, g, :].rearrange("p (n t) -> p n t", t=128),
                                      bm(sgu_sb[:, 2, 128 * g:128 * g + 128], 4), ALU.add)
            order.link(ins)
            dve.wait_ge(sem("sgu_gelu"), 2)
            V.tensor_tensor(Y[:, 8:12, :], Y[:, 8:12, :], proj[:, 8:12, PAD:], ALU.mult).then_inc(sem("mixer_out"), 1)
            group_norm(1, Y[:, 8:12, :])
            project(U_SC, M2_QUADS["sc"], 0)
            dve.wait_ge(bank_free, G_QKVZ + 2)
            order.link(V.tensor_tensor(proj[:, 4:8, PAD:], proj[:, 4:8, PAD:], proj[:, 8:12, PAD:], ALU.mult))
            order.link(conv([Y[:, 12 + t, :] for t in range(4)], [proj[:, 4 + t, :] for t in range(4)],
                            [[par("sc_conv", 3 * t + k) for k in range(3)] for t in range(4)], PAD, None))
            V.tensor_tensor(Y[:, 12:16, :], Y[:, 12:16, :], proj[:, 0:4, PAD:], ALU.mult).then_inc(sem("mixer_out"), 1)
            group_norm(2, Y[:, 12:16, :])
            dve.wait_ge(sem("ba_hi_ready"), 1)
            V.tensor_tensor(ba_lo[:, :], ba_raw, ba_hi[:, :].bitcast(F32), ALU.subtract).then_inc(sem("ba_split"), 1)
            project(U_QKVZ, M2_QUADS["qkvz"], 0)
            dve.wait_ge(sem("rstd_turned"), 1)
            order.link(V.tensor_copy(rstd_tok, ps[:, 5, :].rearrange("p (t n) -> p t n", n=128)[:, :, 0]))
            V.tensor_tensor(ba_tok.rearrange("p (t c) -> p t c", c=8), ps[:, 4, 0:32].rearrange("p (t c) -> p t c", c=8),
                            bc(rstd_tok, 8), ALU.mult).then_inc(sem("ba_tok"), 1)
            dve.wait_ge(sem("ba_tok"), 1)
            V.tensor_tensor(g_tmp.rearrange("p (h t) -> p t h", h=4), ba_tok.rearrange("p (t c) -> p t c", c=8)[:, :, 4:8],
                            bm(alog_sb[:, 4:8], 4), ALU.add).then_inc(sem("a_dt"), 1)
            dve.wait_ge(sem("a_log1p"), 1)
            order.link(V.scalar_tensor_tensor(out=g_tmp, in0=g_tmp, scalar=0.0, in1=exp_g, op0=ALU.max, op1=ALU.add))
            V.scalar_tensor_tensor(out=gate.rearrange("p (h t) -> p h t", h=4), in0=g_tmp.rearrange("p (h t) -> p h t", h=4),
                                   scalar=-1.0, in1=bc(alog_sb[:, 0:4], 4), op0=ALU.mult, op1=ALU.mult)\
             .then_inc(sem("gate_ready"), 1)
            dve.wait_ge(sem("g_summed"), 1)
            V.tensor_copy(g_sums, ps[:, 6, 0:64]).then_inc(sem("g_sums_read"), 1)
            dve.wait_ge(sem("g_sums_read"), 1)
            V.tensor_tensor(kgs, g_sums[:, 16:32], g_sums[:, 0:16], ALU.subtract).then_inc(sem("kgs_log"), 1)
            dve.wait_ge(sem("exp_g_ready"), 3)
            order.link(V.tensor_tensor(be, beta, exp_g, ALU.mult))
            for k in range(3):
                order.link(conv([conv_out[:, 4 * k + t, :] for t in range(4)], [proj[:, 4 * k + t, :] for t in range(4)],
                                [[par("gdn_conv", 4 * (4 * k + t) + n) for n in range(4)] for t in range(4)], PAD, None))
                V.memset(credit[:, 12 + k:13 + k], 0.0).then_inc(sem("qkv_conved"), 1)
            for t in range(8):
                dve.wait_ge(sem("l2_root"), t + 1)
                order.link(V.reciprocal(conv_out[:, t, :], conv_out[:, t, :]))
                V.scalar_tensor_tensor(out=proj[:, t, PAD:], in0=proj[:, t, PAD:], scalar=GDN_D ** -0.5 if t < 4 else 1.0,
                                       in1=conv_out[:, t, :], op0=ALU.mult, op1=ALU.mult).then_inc(sem("l2_normed"), 1)

            def t4(ap):
                return ap.rearrange("p (t n) -> p t n", n=128)

            for pair in range(2):
                heads = [(m, 2 * pair + m, 4 * m) for m in range(2)]
                for m, h, b in heads:
                    hs = slice(4 * h, 4 * h + 4)
                    V.tensor_tensor(t4(tmp_a[:, m, :]), bm(ident, 4), bc(g_sums[:, hs], 128), ALU.mult)
                    V.tensor_tensor(t4(tmp_b[:, m, :]), bm(ident, 4), bc(beta[:, hs], 128), ALU.mult)\
                     .then_inc(sem("diags"), 1)
                    dve.wait_ge(sem("kv_turned"), h + 1)
                    if h == 0:
                        dve.wait_ge(sem("l2_normed"), 8)
                    V.tensor_tensor(t4(k_be[:, h, :]), t4(ps[:, b, :]), bc(be[:, hs], 128), ALU.mult)
                    V.tensor_tensor(t4(k_g[:, h, :]), t4(ps[:, b, :]), bc(kgs[:, hs], 128), ALU.mult)
                    V.tensor_tensor(t4(v_b[:, h, :]), t4(ps[:, b + 1, :]), bc(beta[:, hs], 128), ALU.mult)\
                     .then_inc(sem("kv_taken"), 1)
                for m, h, b in heads:
                    hs = slice(4 * h, 4 * h + 4)
                    dve.wait_ge(sem("exp_row"), h + 1)
                    order.link(V.tensor_tensor(t4(tmp_a[:, m, :]), t4(ps[:, b + 2, :]), bc(g_sums[:, hs], 128), ALU.subtract))
                    V.tensor_tensor(t4(tmp_a[:, m, :]), t4(tmp_a[:, m, :]), bm(gdn_c[:, 4, :], 4), ALU.add)\
                     .then_inc(sem("decay_log"), 1)
                    V.tensor_tensor(tmp_b[:, m, :], proj[:, 4 + h, PAD:], ps[:, b + 3, :], ALU.mult)\
                     .then_inc(sem("kb_ready"), 1)
                for m, h, b in heads:
                    dve.wait_ge(sem("decay_ready"), h + 1)
                    order.link(V.tensor_tensor(t4(inv_t[:, h, :]), t4(tmp_a[:, m, :]), bm(gdn_c[:, 5, :], 4), ALU.mult))
                    dve.wait_ge(sem("kk_done"), h + 1)
                    V.scalar_tensor_tensor(out=pows[:, m, 0, 1, :], in0=ps[:, b + 1, :], scalar=-1.0, in1=inv_t[:, h, :],
                                           op0=ALU.mult, op1=ALU.mult).then_inc(sem("nt_ready"), 1)
                    dve.wait_ge(sem("nt_ready"), h + 1)
                    V.tensor_tensor(t4(inv_t[:, h, :]), t4(pows[:, m, 0, 1, :]), bm(ident, 4), ALU.add)\
                     .then_inc(sem("inv_ready"), 1)
                    V.tensor_tensor(attn_t[:, h, :], ps[:, b, :], tmp_a[:, m, :], ALU.mult).then_inc(sem("attn_ready"), 1)
                    V.tensor_tensor(proj[:, h, PAD:], proj[:, h, PAD:], pows[:, m, 1, 0, :], ALU.mult)\
                     .then_inc(sem("q_scaled"), 1)
                for it in range(5):
                    if it < 4:
                        for m, h, b in heads:
                            dve.wait_ge(sem("nt_squared"), (4 * pair + it) * 2 + m + 1)
                            V.tensor_copy(pows[:, m, 1 - it % 2, 1, :], ps[:, b + 1, :]).then_inc(sem("nt_power"), 1)
                    for m, h, b in heads:
                        dve.wait_ge(sem("inv_step"), (5 * pair + it) * 2 + m + 1)
                        V.tensor_tensor(inv_t[:, h, :], inv_t[:, h, :], ps[:, b + 2, :], ALU.add)\
                         .then_inc(sem("inv_ready"), 1)
                for m, h, b in heads:
                    dve.wait_ge(sem("u_done"), h + 1)
                    V.tensor_copy(u_b[:, h, :], ps[:, b + 1, :]).then_inc(sem("u_ready"), 1)
            dve.wait_ge(sem("inv_step"), 20)
            V.memset(state[:, 0, :], 0.0).then_inc(sem("state_ready"), 1)
            for c in range(8):
                r, tt, half = 64 * (c % 2), c // 2, c % 2
                dve.wait_ge(sem("w_state"), c + 1)
                V.tensor_tensor(v_new[r:r + 64, :].rearrange("p (h n) -> p h n", h=4),
                                u_b[r:r + 64, :, 128 * tt:128 * tt + 128],
                                ps[r:r + 64, 0, :].rearrange("p (h n) -> p h n", h=4), ALU.subtract)\
                 .then_inc(sem("v_new_ready"), 1)
                dve.wait_ge(sem("state_ready"), c + 1)
                order.link(V.tensor_tensor(state_g[:, :].rearrange("p (h n) -> p h n", h=4),
                                           state[:, c % 2, :].rearrange("p (h n) -> p h n", h=4),
                                           bc(g_last[:, 16 * half + tt:16 * half + 16:4], 128), ALU.mult))
                dve.wait_ge(sem("state_add"), c + 1)
                if c >= 1:
                    dve.wait_ge(sem("o_done"), c)
                V.tensor_tensor(state[:, (c + 1) % 2, :], state_g[:, :], ps[:, 3, :], ALU.add).then_inc(sem("state_ready"), 1)
            dve.wait_ge(sem("z_silu"), 1)
            for h in range(4):
                dve.wait_ge(sem("gdn_root"), h + 1)
                order.link(V.reciprocal(k_g[:, h, :], k_g[:, h, :]))
                order.link(V.scalar_tensor_tensor(out=Y[:, h, :], in0=proj[:, 8 + h, PAD:], scalar=par("gdn_norm"),
                                                  in1=k_g[:, h, :], op0=ALU.mult, op1=ALU.mult))
                ins = V.tensor_tensor(Y[:, h, :], Y[:, h, :], proj[:, 12 + h, PAD:], ALU.mult)
            ins.then_inc(sem("mixer_out"), 1)

            with dve.Fori(0, 16) as i:
                dve.wait_ge(h_hi_ready, 48 + i + 1)
                V.tensor_tensor(h_lo[:, i, :], Y[:, i, :], h_hi[:, i, :].bitcast(F32), ALU.subtract).then_inc(h_ready, 1)
            with dve.Fori(0, 4) as i:
                for s in range(4):
                    step_lo(U_WO2 + 4 * i, s)
                    if s % 2:
                        dve.wait_ge(w_used, U_WO2 + 4 * i + s + 1 + 1)
                        V.tensor_copy(y2[:, bass.ds(4 * i + (s - 1), 2), :], ps[:, s - 1:s + 1, :]).then_inc(bank_free, 1)
            one_over_root(4)
            dve.wait_ge(sem("x_back"), 64)
            with dve.Fori(0, 8) as i:
                order.enter(i, 1)
                for s in range(2):
                    t = 2 * i + s
                    ins = V.scalar_tensor_tensor(out=y2[:, t, :], in0=y2[:, t, :], scalar=dpar("post_mix", t),
                                                 in1=rstd[:, :], op0=ALU.mult, op1=ALU.mult)
                order.link(ins)
                for s in range(2):
                    t = 2 * i + s
                    V.tensor_tensor(X[:, t, :], X[:, t, :], y2[:, t, :], ALU.add).then_inc(x_ready, 1)
                low_pair(64, i, "pre_ffn")
                order.leave(8)
            one_over_root(5)

            for k in range(4):
                V.memset(credit[:, 4 * k:4 * k + 1], 0.0).then_inc(down_free, 1)
            order.link(V.memset(hid[:, :, 0:2], 0.0))

            def ffn_group(u, s, seg, b, c):
                dve.wait_ge(w_used, u + s + 1 + 1)
                for j in range(2):
                    ins = V.tensor_tensor(hid[:, j, 2:], ps[:, 2 * c + j, :], rstd[:, :], ALU.mult)
                ins.then_inc(bank_free, 1)
                dve.wait_ge(bank_free, seg * 4 + (G_FFN + 2 * b + c + 3))
                dst = f_val if c else f_gate
                tile = [seg * 4 + (FFT * c + 2 * b + j) for j in range(2)]
                ins = conv([dst[:, j, :] for j in range(2)], [hid[:, j, :] for j in range(2)],
                           [[dpar("ffn_conv", tile[j] * 3 + k) for k in range(3)] for j in range(2)], 2, None,
                           [dpar("ffn_b", tile[j]) for j in range(2)])
                if c == 0:
                    ins.then_inc(sem("f_gates"), 1)
                else:
                    order.link(ins)
                    dve.wait_ge(sem("f_gelu"), seg * 2 + (b + 1))
                    V.tensor_tensor(f_val[:, :, :], f_gate[:, :, :], f_val[:, :, :], ALU.mult).then_inc(sem("f_gated"), 1)

            def ffn_low(seg, b, par_):
                dve.wait_ge(sem("f_hi_ready"), seg * 2 + (b + 1))
                V.tensor_tensor(f_lo[:, par_, 2 * b:2 * b + 2, :], f_val[:, :, :],
                                f_hi[:, par_, 2 * b:2 * b + 2, :].bitcast(F32), ALU.subtract).then_inc(f_ready, 1)

            def ffn_up(u, seg, par_):
                for s in range(8):
                    step_lo(u, s)
                    if s % 2:
                        ffn_group(u, s, seg, s // 4, s // 2 % 2)
                        if s % 4 == 3:
                            ffn_low(seg, s // 4, par_)

            def ffn_down(u, seg, last=False):
                for q in range(4):
                    if not (last and q == 3):
                        step_lo(u, q)
                    for j in range(4):
                        if j < 3:
                            dve.wait_ge(down_tile, seg * 12 + (3 * q + j + 1))
                        else:
                            dve.wait_ge(w_used, u + q + 1 + 1)
                        V.tensor_tensor(y_acc[:, 4 * q + j, :], y_acc[:, 4 * q + j, :], ps[:, 4 + j, :],
                                        ALU.add).then_inc(down_free, 1)

            PER_SEG = 2 * (2 + 3)
            ffn_up(U_FFN, 0, 0)
            dve.wait_ge(sem("acc_zeroed"), 1)
            with dve.Fori(0, (SEGS - 1) // 2) as i:
                order.enter(i, 2 * PER_SEG)
                for e in range(2):
                    u = U_FFN + 8 + 12 * e + 24 * i
                    ffn_up(u, 2 * i + (1 + e), 1 - e)
                    ffn_down(u + 8, 2 * i + e)
                order.leave((SEGS - 1) // 2)
            ffn_down(N_UNITS - 4, SEGS - 1, last=True)
            one_over_root(6)
            dve.wait_ge(sem("x_back"), 128)
            with dve.Fori(0, 8) as i:
                order.enter(i, 1)
                for s in range(2):
                    t = 2 * i + s
                    ins = V.scalar_tensor_tensor(out=y_acc[:, t, :], in0=y_acc[:, t, :], scalar=dpar("post_ffn", t),
                                                 in1=rstd[:, :], op0=ALU.mult, op1=ALU.mult)
                order.link(ins)
                for s in range(2):
                    t = 2 * i + s
                    V.tensor_tensor(y_acc[:, t, :], y_acc[:, t, :], x_back[:, t, :], ALU.add).then_inc(sem("out_tiles"), 1)
                order.leave(8)


def unit_of(w, t0, nt, cols):
    a = w[t0 * 128:(t0 + nt) * 128, cols].reshape(nt, 128, -1)
    return a.transpose(1, 0, 2).reshape(128, -1)


def group_units(w, c0, groups):
    return [unit_of(w, 8 * half, 8, slice(c0 + 256 * g, c0 + 256 * g + 256)) for g in range(groups) for half in range(2)]


def columns(v):
    return v.reshape(-1, 128).T


def kernel(**inp):
    import concourse.bacc as bacc
    from concourse.bass_utils import run_bass_kernel_spmd

    a = {k: np.ascontiguousarray(v) for k, v in inp.items()}
    units = []
    for l in range(2):
        units += group_units(a["w_in"][l], 0, 8)
        units += [unit_of(a["w_out"][l], 0, 4, slice(512 * q, 512 * q + 512)) for q in range(4)]
    w2 = a["w_in_2"][0]
    units += group_units(w2, 2056, 4) + group_units(w2, 3080, 4) + group_units(w2, 4104, 6) + group_units(w2, 0, 8)
    units += group_units(a["w_out_2"][0], 0, 8)
    up, down = a["ffn_up_2"][0], a["ffn_down_2"][0]

    def ups(s):
        return [u for b in range(2) for c in (0, D_FF) for u in group_units(up, c + 512 * s + 256 * b, 1)]

    def downs(s):
        return [unit_of(down, 4 * s, 4, slice(512 * q, 512 * q + 512)) for q in range(4)]

    units += ups(0)
    for s in range(1, SEGS):
        units += ups(s) + downs(s - 1)
    units += downs(SEGS - 1)
    assert len(units) == N_UNITS
    weights = np.stack(units)

    def taps(w):
        return w.reshape(w.shape[0], -1, 128).transpose(2, 1, 0).reshape(128, -1)

    vals = dict(g0=columns(a["norm_g"][0]), g1=columns(a["norm_g"][1]), final=columns(a["final_norm_g"]),
                pre_mix=columns(a["pre_mix_norm_2"][0]), post_mix=columns(a["post_mix_norm_2"][0]),
                pre_ffn=columns(a["pre_ffn_norm_2"][0]), post_ffn=columns(a["post_ffn_norm_2"][0]),
                gdn_conv=taps(a["gdn_conv_w_2"][0]), gdn_norm=columns(a["gdn_norm_w_2"][0]),
                lru_conv=taps(a["lru_conv_w_2"][0]), lru_b=columns(a["lru_conv_b_2"][0]),
                ba=columns(a["lru_ba_2"][0].reshape(-1)), bx=columns(a["lru_bx_2"][0].reshape(-1)),
                lam=columns(a["lru_lambda_2"][0]), sc_conv=taps(a["sconv_w_2"][0]),
                grp=columns(a["grp_norm_w_2"][0].reshape(-1)),
                subln=columns(np.concatenate([a["diff_subln_g"][0]] * 2)),
                ffn_conv=taps(a["ffn_conv_w_2"][0]), ffn_b=columns(a["ffn_conv_b_2"][0]))
    arrays = {
        "weights": weights,
        "x_in": np.ascontiguousarray(a["x"][0].T.reshape(KT, 128, S).transpose(1, 0, 2)),
        "params": np.ascontiguousarray(np.concatenate([vals[n] for n, _ in PARAM_SIZES], axis=1)),
        "consts": shape_constants(),
        "w_ba": np.ascontiguousarray(unit_of(w2, 0, 16, slice(2048, 2056))),
        "alog_dt": np.concatenate([a["gdn_a_log_2"][0], a["gdn_dt_bias_2"][0]]),
        "lam_rows": a["diff_lam"][0].reshape(-1),
        "sgu_rows": np.stack([a["sgu_ln_w_2"][0], a["sgu_ln_b_2"][0], a["sgu_b_2"][0].reshape(-1)]),
        "sgu_wsT": np.ascontiguousarray(a["sgu_ws_2"][0].transpose(2, 0, 1)),
        "lru_wa": a["lru_wa_2"][0],
        "lru_wx": a["lru_wx_2"][0],
    }
    nc = bacc.Bacc("TRN2", target_bir_lowering=False, num_devices=1)
    args = [nc.dram_tensor(n, v.shape, mybir.dt.from_np(v.dtype), kind="ExternalInput").ap() for n, v in arrays.items()]
    args.append(nc.dram_tensor("out", (128, KT, S), F32, kind="ExternalOutput").ap())
    two_blocks_kernel(nc, *args)
    r = run_bass_kernel_spmd(nc, [arrays], core_ids=[0])
    got = r.results[0]["out"]
    return got.transpose(1, 0, 2).reshape(D, S).T.reshape(1, S, D)
```

```python
from contextlib import ExitStack

import numpy as np

import concourse.bass as bass
from concourse import mybir

F32 = mybir.dt.float32
F32R = mybir.dt.float32r
ALU = mybir.AluOpType
ACT = mybir.ActivationFunctionType
AX = mybir.AxisListType.X

P128 = 128
D = 2048
S = 512
KT = D // P128
UNIT = 2048
NEG = -1.0e30
EPS = 1e-6
HEAD = 64
N_HEADS = 4
PAD = 4
D_FF = (D * 11) // 4
SEGS = D_FF // 512
FFT = D_FF // P128

U_IN = 16
U_OUT = 4
U_UP, U_DOWN = 8, 4
U_L = [0, U_IN + U_OUT]
U_M2 = 2 * (U_IN + U_OUT)
M2_QUADS = dict(lru=2, sgu=2, sc=3, qkvz=4)
U_LRU = U_M2
U_SGU = U_LRU + 4 * M2_QUADS["lru"]
U_SC = U_SGU + 4 * M2_QUADS["sgu"]
U_QKVZ = U_SC + 4 * M2_QUADS["sc"]
U_WO2 = U_QKVZ + 4 * M2_QUADS["qkvz"]
U_FFN = U_WO2 + 16
N_UNITS = U_FFN + SEGS * (U_UP + U_DOWN)
G_L = [0, 8]
G_LRU = 16
G_SGU = G_LRU + 4
G_SC = G_SGU + 4
G_QKVZ = G_SC + 6
G_WO2 = G_QKVZ + 8
G_FFN = G_WO2 + 8

PARAM_SIZES = [("g0", 16), ("g1", 16), ("final", 16), ("pre_mix", 16), ("post_mix", 16), ("pre_ffn", 16),
               ("post_ffn", 16), ("gdn_conv", 48), ("gdn_norm", 1), ("lru_conv", 16), ("lru_b", 4),
               ("ba", 4), ("bx", 4), ("lam", 4), ("sc_conv", 12), ("grp", 12), ("subln", 1),
               ("ffn_conv", 6 * FFT), ("ffn_b", 2 * FFT)]
PARAM = {}
_n = 0
for _name, _size in PARAM_SIZES:
    PARAM[_name] = _n
    _n += _size
N_PARAM = _n

CONST_SIZES = [("ident", 128), ("ones", 128), ("eps", 1), ("one", 1), ("pad", 6),
               ("rot0", 128), ("rot1", 128), ("suffix", 128), ("before01", 128), ("notbefore", 128),
               ("dilated", 512), ("causal", 512), ("cos0", 512), ("sin0", 512), ("cos1", 512), ("sin1", 512),
               ("chunk_tri", 128), ("chunk_all", 128), ("half_a", 128), ("half_b", 128),
               ("decay_mask", 128), ("strict01", 128), ("tri01", 128)]
CONST = {}
_n = 0
for _name, _size in CONST_SIZES:
    CONST[_name] = _n
    _n += _size
N_CONST = _n


def shape_constants():
    c = np.zeros((P128, N_CONST), np.float32)

    def put(name, a):
        c[:, CONST[name]:CONST[name] + a.shape[1]] = a

    p, f = np.arange(128)[:, None], np.arange(128)[None, :]
    same = (p // 64) == (f // 64)
    put("ident", (p == f).astype(np.float32))
    put("ones", np.ones((128, 128), np.float32))
    put("eps", np.full((128, 1), EPS, np.float32))
    put("one", np.ones((128, 1), np.float32))
    for n, dim in ((0, 64), (1, 32)):
        half = dim // 2
        rot = np.zeros((128, 128), np.float32)
        for i in range(128):
            if i % dim < half:
                rot[i + half, i] = -1.0
            else:
                rot[i - half, i] = 1.0
        put(f"rot{n}", rot)
        inv = np.float32(10000.0) ** (-np.arange(half, dtype=np.float32) / np.float32(half))
        ang = np.arange(S, dtype=np.float32)[None, :] * inv.astype(np.float32)[np.arange(128) % half][:, None]
        put(f"cos{n}", np.cos(ang).astype(np.float32))
        put(f"sin{n}", np.sin(ang).astype(np.float32))
    put("suffix", (p >= f).astype(np.float32))
    put("before01", (p < f).astype(np.float32))
    put("notbefore", np.where(p < f, 0.0, NEG).astype(np.float32))
    dist = np.concatenate([128 * b + p - f for b in (3, 2, 1, 0)], axis=1)
    put("causal", np.where(dist >= 0, 0.0, NEG).astype(np.float32))
    n = ((dist >= 0) & (dist <= 128)).astype(int) + ((dist >= 0) & (dist % 4 == 0)) + ((dist >= 0) & (dist % 16 == 0))
    put("dilated", np.where(n > 0, np.log(np.maximum(n, 1)) * HEAD ** 0.5, NEG).astype(np.float32))
    put("chunk_tri", (same & (p <= f)).astype(np.float32))
    put("chunk_all", same.astype(np.float32))
    put("half_a", np.broadcast_to(p < 64, (128, 128)).astype(np.float32))
    put("half_b", np.broadcast_to(p >= 64, (128, 128)).astype(np.float32))
    put("decay_mask", np.where(same & (f >= p), 0.0, NEG).astype(np.float32))
    put("strict01", (same & (f > p)).astype(np.float32))
    put("tri01", (f >= p).astype(np.float32))
    return c


class Order:

    def __init__(self, eng, sem):
        self.eng, self.sem, self.n, self.loop = eng, sem, 0, None

    def link(self, ins):
        ins.then_inc(self.sem, 1)
        self.n += 1
        self.eng.wait_ge(self.sem, self.value())

    def value(self):
        if self.loop is None:
            return self.n
        i, start, per = self.loop
        return start + i * per + (self.n - start)

    def enter(self, i, per):
        self.loop = (i, self.n, per)

    def leave(self, trips):
        _, start, per = self.loop
        assert self.n - start == per, (self.n - start, per)
        self.n, self.loop = start + trips * per, None


def bc(ap, n):
    return ap.unsqueeze(2).broadcast_to([ap.shape[0], ap.shape[1], n])


def bm(ap, n):
    return ap.unsqueeze(1).broadcast_to([ap.shape[0], n, ap.shape[1]])


def two_blocks_kernel(nc, weights, x_in, params, consts, w_ba, alog_dt, lam_rows, sgu_rows, sgu_wsT,
                      lru_wa, lru_wx, out):
    ctx = ExitStack()
    with ctx:
        sems = {}

        def sem(name):
            if name not in sems:
                sems[name] = ctx.enter_context(nc.semaphore(name))
            return sems[name]

        IN_LAYER_0 = dict(l_scores=32, l_scores_read=32, l_probs=32, neg_max=8, l_turned=8, l_pt_a=8, l_pt_b=8,
                          l_o=8, l_o_read=8, l_y_turned=4, rotated=8, rot_read=8, roped=8, v_turned=4,
                          v_tok_ready=4, gates=2, y1=4, y1_hi_ready=4, y1_ready=4, attn_c_landed=128, y_taken=0)

        def since(name, l, n):
            return sem(name), n + (IN_LAYER_0[name] if l else 0)

        class Region:
            def __init__(self, at, end):
                self.at, self.end = at, end

            def take(self, name, shape, dt=F32):
                size = int(np.prod(shape[1:])) * 4
                at = self.at
                self.at = (at + size + 31) // 32 * 32
                assert self.at <= self.end, (name, self.at, self.end)
                return nc.alloc_sbuf_tensor_at(name, shape, dt, offset=at)

        BASE, END = 16512, 229344
        top = Region(BASE, END)
        params_sb = top.take("params_sb", [128, N_PARAM])
        head_c = top.take("head_c", [128, 264])
        rstd = top.take("rstd", [128, S])
        root = top.take("root", [128, S])
        credit = top.take("credit", [128, 16])
        squares = top.take("squares", [128, 2, S])
        raw = top.take("raw", [128, 2, UNIT])
        w_hi = top.take("w_hi", [128, 2, UNIT], F32R)
        w_lo = top.take("w_lo", [128, 2, UNIT], F32R)
        X0 = top.at
        X = top.take("X", [128, KT, S])
        H0 = top.at
        h_hi = top.take("h_hi", [128, KT, S], F32R)
        h_lo = top.take("h_lo", [128, KT, S], F32R)
        W0 = top.at
        ident, ones = head_c[:, 0:128], head_c[:, 128:256]
        eps_c, one_c = head_c[:, 256:257], head_c[:, 257:258]

        wl = Region(W0, END)
        proj = wl.take("proj", [128, 16, PAD + S])
        y1_hi = wl.take("y1_hi", [128, 4, S], F32R)
        y1_lo = wl.take("y1_lo", [128, 4, S], F32R)
        hl = Region(H0, W0)
        probs = hl.take("probs", [128, 4, 1280])
        probs_t = hl.take("probs_t", [128, 2, 1280])
        v_tok = hl.take("v_tok", [128, 4, 512])
        o_tok = hl.take("o_tok", [128, 4, 512])
        cos_sb = hl.take("cos_sb", [128, S])
        sin_sb = hl.take("sin_sb", [128, S])
        mask_sb = hl.take("mask_sb", [128, 2, 512])
        rot_sin = hl.take("rot_sin", [128, 2, S])
        attn_c = hl.take("attn_c", [128, 4, 128])
        y1 = root
        small = hl.take("small", [128, 512])
        row_max, neg_max, den, rden = (small[:, 32 * k:32 * k + 32] for k in range(4))
        lam_sb = small[:, 128:256]
        lam_s = small[:, 256:264]
        lam_prod = small[:, 264:296]
        o_ss, o_root, o_rstd = (small[:, 320 + 16 * k:336 + 16 * k] for k in range(3))

        Y = nc.alloc_sbuf_tensor_at("Y", [128, 16, S], F32, offset=X0)
        wm = Region(proj_end := (W0 + 16 * (PAD + S) * 4 + 31) // 32 * 32, END)
        gate_a = wm.take("gate_a", [128, 4, 128])
        gate_x = wm.take("gate_x", [128, 4, 128])
        sgu_sb = wm.take("sgu_sb", [128, 3, 512])
        sgu_w = wm.take("sgu_w", [128, 4, 128])
        tri01 = wm.take("tri01", [128, 128])
        lru_s = wm.take("lru_s", [128, 32])
        lru_a2 = wm.take("lru_a2", [128, 2, S])
        stats = wm.take("stats", [128, 4, 16])
        wg = Region(proj_end, END)
        pows = wg.take("pows", [128, 2, 2, 2, 512])
        wscan = Region(proj_end, END)
        N_STATES = 6
        state = wscan.take("state", [128, N_STATES, 512])
        state_g = wscan.take("state_g", [128, 512])
        v_new = wscan.take("v_new", [128, 2, 512])
        wconv = Region(proj_end, END)
        conv_out = wconv.take("conv_out", [128, 8, S])
        hg = Region(H0, W0)
        k_be = hg.take("k_be", [128, 4, 512])
        k_g = hg.take("k_g", [128, 4, 512])
        v_b = hg.take("v_b", [128, 4, 512])
        inv_t = hg.take("inv_t", [128, 4, 512])
        attn_t = hg.take("attn_t", [128, 4, 512])
        w_t = hg.take("w_t", [128, 4, 512])
        u_b = hg.take("u_b", [128, 4, 512])
        tmp_a = hg.take("tmp_a", [128, 2, 512])
        tmp_b = hg.take("tmp_b", [128, 2, 512])
        gs0 = nc.alloc_sbuf_tensor_at("gdn_small", [128, 1024], F32, offset=X0)
        gdn_c = nc.alloc_sbuf_tensor_at("gdn_c", [128, 6, 128], F32, offset=X0 + 4096)
        ba_raw = gs0[:, 0:128]
        ba_tok = gs0[:, 128:160]
        beta, gate, g_tmp, exp_g, be, kgs = (gs0[:, 160 + 16 * k:176 + 16 * k] for k in range(6))
        g_sums = gs0[:, 256:320]
        g_last = gs0[:, 320:352]
        rstd_tok = gs0[:, 352:356]
        alog_sb = gs0[:, 360:368]
        ba_hi = nc.alloc_sbuf_tensor_at("ba_hi", [128, 128], F32R, offset=X0 + 8192 - 1024)
        ba_lo = nc.alloc_sbuf_tensor_at("ba_lo", [128, 128], F32R, offset=X0 + 8192 - 512)
        y2_hi, y2_lo = h_hi, h_lo
        y2 = nc.alloc_sbuf_tensor_at("y2", [128, 16, S], F32, offset=W0)

        y_acc = nc.alloc_sbuf_tensor_at("y_acc", [128, 16, S], F32, offset=X0)
        wf = Region(W0, END)
        f_hi = wf.take("f_hi", [128, 2, 4, S], F32R)
        f_lo = wf.take("f_lo", [128, 2, 4, S], F32R)
        hid = wf.take("hid", [128, 2, 2 + S])
        f_gate = wf.take("f_gate", [128, 2, S])
        f_val = wf.take("f_val", [128, 2, S])
        x_back = nc.alloc_sbuf_tensor_at("x_back", [128, 16, S], F32, offset=H0)

        ps = ctx.enter_context(nc.psum_tensor("ps", [128, 8, 512], F32))
        SS = 7

        rstd_g = squares[:, 0, :]
        ba_rows = squares[0:8, 1, :]
        lru_xc, lru_r, lru_i, lru_a = Y[:, 8:12, :], Y[:, 12:16, :], Y[:, 0:4, :], Y[:, 4:8, :]
        QT, KT_, VT, ZT = 8, 0, 4, 12
        sc_sq = conv_out[:, 4:8, :]
        GDN_D = 128

        x_spill = nc.dram_tensor("x_spill", (128, KT, S), F32, kind="Internal").ap()
        x_spill2 = nc.dram_tensor("x_spill2", (128, KT, S), F32, kind="Internal").ap()

        def par(name, at=0, n=1):
            c = PARAM[name]
            return params_sb[:, c + at:c + at + n]

        def dpar(name, at):
            return params_sb[:, bass.ds(at + PARAM[name], 1)]

        raw_landed = [sem("raw_landed_0"), sem("raw_landed_1")]
        w_hi_ready = sem("w_hi_ready")
        w_ready = sem("w_ready")
        w_used = sem("w_used")
        bank_free = sem("bank_free")
        x_ready = sem("x_ready")
        h_hi_ready = sem("h_hi_ready")
        h_ready = sem("h_ready")
        sq_ready = sem("sq_ready")
        sq_used = sem("sq_used")
        root_ready = sem("root_ready")
        rstd_ready = sem("rstd_ready")
        params_landed = sem("params_landed")
        down_free = sem("down_free")
        down_tile = sem("down_tile")
        f_ready = sem("f_ready")
        x_landed = [sem(f"x_landed_{k}") for k in range(4)]
        dve_order, act_order, pool_order = sem("dve_order"), sem("act_order"), sem("pool_order")

        block = ctx.enter_context(nc.Block())

        OUT_BANKS = [4, 5, 6, 3]
        Q_OFF = [0, 128, 384, 768]
        K_OFF = [0, 512, 1024, 896]
        Z_OFF = [0, 512, 896, 1152]

        @block.sync
        def _(sp):
            for k in range(4):
                sp.dma_start(X[:, 4 * k:4 * k + 4, :], x_in[:, 4 * k:4 * k + 4, :]).then_inc(x_landed[k], 16)
            with sp.Fori(0, N_UNITS // 2) as i:
                for s in range(2):
                    sp.wait_ge(w_ready, 2 * i + (s + 1))
                    sp.dma_start(raw[:, s, :], weights[2 * i + s]).then_inc(raw_landed[s], 16)

        @block.gpsimd
        def _(pool):
            order = Order(pool, pool_order)

            def add_squares(stage, tiles):
                for t in tiles:
                    if t == 0:
                        continue
                    n = 16 * stage + t
                    pool.wait_ge(sq_ready, n + 1)
                    if t == 1:
                        nc.gpsimd.tensor_tensor(root[:, :], squares[:, 0, :], squares[:, 1, :], ALU.add).then_inc(sq_used, 2)
                    else:
                        pool.wait_ge(sq_used, n)
                        nc.gpsimd.tensor_tensor(root[:, :], root[:, :], squares[:, t % 2, :], ALU.add).then_inc(sq_used, 1)

            pool.dma_start(head_c[:, :], consts[:, 0:264]).then_inc(params_landed, 16)
            pool.dma_start(params_sb[:, :], params).then_inc(params_landed, 16)
            add_squares(0, range(16))
            for l in range(2):
                pool.wait_ge(w_used, U_L[l] + U_IN + 1)
                for dst, name, n in ((cos_sb[:, :], f"cos{l}", 512), (sin_sb[:, :], f"sin{l}", 512),
                                     (mask_sb[:, 0, :], "dilated", 512), (mask_sb[:, 1, :], "causal", 512),
                                     (attn_c[:, 0, :], f"rot{l}", 128), (attn_c[:, 1, :], "suffix", 128),
                                     (attn_c[:, 2, :], "before01", 128), (attn_c[:, 3, :], "notbefore", 128)):
                    pool.dma_start(dst, consts[:, CONST[name]:CONST[name] + n]).then_inc(sem("attn_c_landed"), 16)
                if l == 1:
                    pool.dma_start(lam_sb, lam_rows.partition_broadcast(128)).then_inc(sem("lam_landed"), 16)
                add_squares(l + 1, range(16))
            pool.wait_ge(x_ready, 2 * 16)
            order.link(pool.memset(proj[:, :, 0:PAD], 0.0))
            order.link(pool.memset(gate_a[:, :, :], 0.0))
            pool.memset(gate_x[:, :, :], 0.0).then_inc(sem("pads_ready"), 1)
            pool.wait_ge(sem("pads_ready"), 1)
            for dst, src in ((gate_a, lru_wa), (gate_x, lru_wx)):
                for b in range(2):
                    pool.dma_start(dst[64 * b:64 * b + 64, :, 64 * b:64 * b + 64],
                                   src.rearrange("(t b) i j -> b i t j", b=2)[b]).then_inc(sem("mix_c_landed"), 16)
            for k in range(3):
                pool.dma_start(sgu_sb[:, k, :], sgu_rows[k].partition_broadcast(128)).then_inc(sem("mix_c_landed"), 16)
            pool.dma_start(sgu_w[:, :, :], sgu_wsT).then_inc(sem("mix_c_landed"), 16)
            pool.dma_start(tri01[:, :], consts[:, CONST["tri01"]:CONST["tri01"] + 128]).then_inc(sem("mix_c_landed"), 16)
            for k in range(4):
                pool.wait_ge(x_ready, 2 * 16 + 4 * k + 4)
                pool.dma_start(x_spill[:, 4 * k:4 * k + 4, :], X[:, 4 * k:4 * k + 4, :]).then_inc(sem("x_spilled"), 16)
                add_squares(3, range(4 * k, 4 * k + 4))
            pool.wait_ge(sem("mixer_out"), 1)
            for k, name in enumerate(("chunk_tri", "chunk_all", "half_a", "half_b", "decay_mask", "strict01")):
                pool.dma_start(gdn_c[:, k, :], consts[:, CONST[name]:CONST[name] + 128]).then_inc(sem("mix_c_landed"), 16)
            pool.dma_start(ba_raw, w_ba).then_inc(sem("mix_c_landed"), 16)
            pool.dma_start(alog_sb, alog_dt.partition_broadcast(128)).then_inc(sem("mix_c_landed"), 16)
            pool.wait_ge(h_ready, 64)
            pool.wait_ge(sem("x_spilled"), 64)
            for k in range(4):
                pool.dma_start(X[:, 4 * k:4 * k + 4, :], x_spill[:, 4 * k:4 * k + 4, :]).then_inc(sem("x_back"), 16)
            add_squares(4, range(16))
            for k in range(4):
                pool.wait_ge(x_ready, 48 + 4 * k + 4)
                pool.dma_start(x_spill2[:, 4 * k:4 * k + 4, :], X[:, 4 * k:4 * k + 4, :]).then_inc(sem("x_spilled"), 16)
                add_squares(5, range(4 * k, 4 * k + 4))
            pool.wait_ge(sem("x_spilled"), 128)
            pool.wait_ge(h_ready, 80)
            pool.wait_ge(sq_ready, 96)
            pool.memset(y_acc[:, :, :], 0.0).then_inc(sem("acc_zeroed"), 1)
            pool.wait_ge(w_used, N_UNITS - U_DOWN - U_DOWN + 1)
            for k in range(4):
                pool.dma_start(x_back[:, 4 * k:4 * k + 4, :], x_spill2[:, 4 * k:4 * k + 4, :]).then_inc(sem("x_back"), 16)
            add_squares(6, range(16))
            for k in range(4):
                pool.wait_ge(sem("out_tiles"), 4 * k + 4)
                pool.dma_start(out[:, 4 * k:4 * k + 4, :], y_acc[:, 4 * k:4 * k + 4, :]).then_inc(sem("out_stored"), 16)
            pool.wait_ge(sem("out_stored"), 64)

        @block.tensor
        def _(pe):
            pe.nop().then_inc(w_used, 1)
            pe.wait_ge(params_landed, 32)

            def turn(o, x):
                return pe.transpose(o, x, ident)

            def sum_squares(stage, bank=SS):
                pe.wait_ge(sq_used, 16 * (stage + 1))
                pe.matmul(ps[:, bank, :], ones, root[:, :], start=True, stop=True).then_inc(sem("sq_summed"), 1)

            def project_unit(u0, g0, i, s, h0):
                g, half = s // 2, s % 2
                pe.wait_ge(w_ready, u0 + 4 * i + s + 3)
                if half == 0:
                    pe.wait_ge(bank_free, g0 + 2 * i + g + 1)
                for k in range(8):
                    t = 8 * half + k
                    pe.wait_ge(h_ready, h0 + t + 1)
                    for j in range(2):
                        w = slice(k * 256 + j * 128, k * 256 + j * 128 + 128)
                        o = ps[:, 2 * g + j, :]
                        pe.matmul(o, w_hi[:, s % 2, w], h_hi[:, t, :], start=(t == 0), stop=False)
                        pe.matmul(o, w_hi[:, s % 2, w], h_lo[:, t, :], start=False, stop=False)
                        mm = pe.matmul(o, w_lo[:, s % 2, w], h_hi[:, t, :], start=False, stop=(t == 15))
                mm.then_inc(w_used, 1)

            def project(u0, g0, quads, h0, norm=None):
                first = 0
                if norm is not None:
                    for s in range(4):
                        project_unit(u0, g0, 0, s, h0)
                        if s == 1:
                            sum_squares(norm)
                    first = 1
                with pe.Fori(first, quads) as i:
                    for s in range(4):
                        project_unit(u0, g0, i, s, h0)

            def scores(n, q, k, r0, rows):
                for i in range(4):
                    if n >= 1:
                        pe.wait_ge(*since("l_scores_read", l, 4 * (n - 1) + i + 1))
                    pe.matmul(ps[:, i, 0:128 * (i + 1)], q[r0:r0 + rows, PAD + 128 * i:PAD + 128 * i + 128],
                              k[r0:r0 + rows, PAD:PAD + 128 * (i + 1)], start=True, stop=True)\
                      .then_inc(sem("l_scores"), 1)

            def turn_probs(n, buf):
                if n >= 1:
                    pe.wait_ge(*since("l_pt_a", l, n))
                    pe.wait_ge(*since("l_pt_b", l, n))
                for kt in (0, 1, 3, 2):
                    for i in range(kt, 4):
                        at = K_OFF[kt] + 128 * (i - kt)
                        mm = turn(ps[:, 4 + at // 512, at % 512:at % 512 + 128],
                                          probs[:, buf, Q_OFF[i] + 128 * kt:Q_OFF[i] + 128 * kt + 128])
                mm.then_inc(sem("l_turned"), 1)

            def weigh_values(n, h, br):
                pe.wait_ge(*since("l_pt_a", l, n + 1))
                pe.wait_ge(*since("l_pt_b", l, n + 1))
                if n >= 1:
                    pe.wait_ge(*since("l_o_read", l, n))
                for i in range(4):
                    for kt in range(i + 1):
                        at = K_OFF[kt] + 128 * (i - kt)
                        mm = pe.matmul(ps[:, 7, 64 * i:64 * i + 64], probs_t[:, n % 2, at:at + 128],
                                       v_tok[:, kt, 256 * br + 64 * h:256 * br + 64 * h + 64],
                                       start=(kt == 0), stop=(kt == i))
                mm.then_inc(sem("l_o"), 1)

            def turn_outputs(tiles, n_read):
                pe.wait_ge(*since("l_o_read", l, n_read))
                for t in tiles:
                    for i in range(4):
                        mm = turn(ps[:, t, 128 * i:128 * i + 128], o_tok[:, i, 128 * t:128 * t + 128])
                    mm.then_inc(sem("l_y_turned"), 1)

            def stick_scores(h):
                q, k = proj[:, 8 + h // 2, :], proj[:, 10 + h // 2, :]
                r0 = 64 * (h % 2)
                if h >= 1:
                    pe.wait_ge(sem("z_read"), 4 * h)
                for kt in range(4):
                    at = (0, 512, 1024, 1280)[kt]
                    mm = pe.matmul(ps[:, at // 512, at % 512:at % 512 + 512 - 128 * kt],
                                   k[r0:r0 + 64, PAD + 128 * kt:PAD + 128 * kt + 128],
                                   q[r0:r0 + 64, PAD + 128 * kt:PAD + 512], start=True, stop=True)
                mm.then_inc(sem("z_scores"), 1)

            def stick_suffix(h):
                pe.wait_ge(sem("sp_ready"), h + 1)
                if h >= 1:
                    pe.wait_ge(sem("tail_read"), 4 * h)
                sp_b = probs[:, 2 * (h % 2) + 1, :]
                for kt in range(4):
                    at = (0, 512, 1024, 1280)[kt]
                    n = 512 - 128 * kt
                    for k2 in range(kt, 4):
                        o = at % 512 + 128 * (k2 - kt)
                        mm = pe.matmul(ps[:, 4 + at // 512, o:at % 512 + n],
                                       attn_c[:, 1, :] if k2 == kt else ones,
                                       sp_b[:, Z_OFF[k2]:Z_OFF[k2] + 512 - 128 * k2],
                                       start=(k2 == kt), stop=(k2 == 3))
                    mm.then_inc(sem("tail"), 1)

            def stick_values(h):
                pe.wait_ge(sem("stick_a"), h + 1)
                a_b = probs[:, 2 * (h % 2), :]
                for kt in range(4):
                    mm = pe.matmul(ps[64 * (h % 2):64 * (h % 2) + 64, 3 if h < 2 else 7, 128 * kt:512],
                                   v_tok[:, kt, 256 + 64 * h:320 + 64 * h],
                                   a_b[:, Z_OFF[kt]:Z_OFF[kt] + 512 - 128 * kt], start=(kt == 0), stop=(kt == 3))
                mm.then_inc(sem("stick_o"), 1)

            def project_out(l):
                for q in range(4):
                    u = U_L[l] + U_IN + q
                    pe.wait_ge(w_ready, u + 3)
                    for j in range(4):
                        if q >= 1:
                            pe.wait_ge(x_ready, 16 * l + 4 * (q - 1) + j + 1)
                        for k in range(4):
                            if q == 0 and j == 0:
                                pe.wait_ge(*since("y1_ready", l, k + 1))
                            w = slice(k * 512 + j * 128, k * 512 + j * 128 + 128)
                            o = ps[:, OUT_BANKS[j], :]
                            pe.matmul(o, w_hi[:, q % 2, w], y1_hi[:, k, :], start=(k == 0), stop=False)
                            pe.matmul(o, w_hi[:, q % 2, w], y1_lo[:, k, :], start=False, stop=False)
                            mm = pe.matmul(o, w_lo[:, q % 2, w], y1_hi[:, k, :], start=False, stop=(k == 3))
                        if j < 3:
                            mm.then_inc(sem("out_tile"), 1)
                        else:
                            mm.then_inc(w_used, 1)

            for l in range(2):
                project(U_L[l], G_L[l], 4, 16 * l, norm=l)
                pe.wait_ge(*since("attn_c_landed", l, 16 * 8))
                pe.wait_ge(bank_free, G_L[l] + 8 + 2)
                for n, t in enumerate([0, 1, 2, 3, 8, 9, 10, 11] if l == 0 else [0, 1, 2, 3]):
                    if n >= 2:
                        pe.wait_ge(*since("rot_read", l, n - 1))
                    pe.matmul(ps[:, n % 2, :], attn_c[:, 0, :], proj[:, t, PAD:PAD + S], start=True,
                              stop=True).then_inc(sem("rotated"), 1)
                for tt in range(4):
                    for c, t in enumerate((4, 5, 12, 13)):
                        mm = turn(ps[:, 2 + tt, 128 * c:128 * c + 128],
                                          proj[:, t, PAD + 128 * tt:PAD + 128 * tt + 128])
                    mm.then_inc(sem("v_turned"), 1)
                pe.wait_ge(*since("rot_read", l, 8 if l == 0 else 4))
                pe.wait_ge(*since("v_tok_ready", l, 4))
                if l == 0:
                    qk = [(proj[:, 8 * b + h // 2, :], proj[:, 8 * b + 2 + h // 2, :], 64 * (h % 2), 64)
                          for b in range(2) for h in range(4)]
                    pe.wait_ge(*since("roped", l, 8))
                    scores(0, *qk[0])
                    for n in range(8):
                        pe.wait_ge(*since("l_probs", l, 4 * (n + 1)))
                        turn_probs(n, n % 4)
                        if n < 7:
                            scores(n + 1, *qk[n + 1])
                        weigh_values(n, n % 4, n // 4)
                    turn_outputs(range(4), 8)
                else:
                    pe.wait_ge(*since("roped", l, 4))
                    qk = [(proj[:, h // 2, :], proj[:, 2 + h // 2, :], 64 * (h % 2) + 32 * c, 32)
                          for h in range(4) for c in range(2)]
                    scores(0, *qk[0])
                    scores(1, *qk[1])
                    for n in range(4):
                        pe.wait_ge(sem("diff_probs"), n + 1)
                        turn_probs(n, 2 * (n % 2))
                        if n < 3:
                            scores(2 * n + 2, *qk[2 * n + 2])
                        weigh_values(n, n, 0)
                        if n < 3:
                            scores(2 * n + 3, *qk[2 * n + 3])
                    pe.wait_ge(sem("diff_normed"), 1)
                    turn_outputs(range(2), 4)
                    pe.wait_ge(*since("y_taken", l, 2))
                    pe.wait_ge(*since("l_scores_read", l, 32))
                    stick_scores(0)
                    for h in range(4):
                        if h < 3:
                            stick_scores(h + 1)
                        stick_suffix(h)
                        if h >= 1:
                            stick_values(h - 1)
                    stick_values(3)
                project_out(l)

            def group_norm(k, sq):
                pe.wait_ge(sem("group_added"), k + 1)
                pe.matmul(ps[:, SS, :], ones, sq[:, 0, :], start=True, stop=True).then_inc(sem("group_sums"), 1)

            sum_squares(2)
            project(U_LRU, G_LRU, M2_QUADS["lru"], 32, norm=3)
            def lru_gates(gate, first):
                for t in range(4):
                    if first:
                        pe.wait_ge(sem("lru_conved"), t + 1)
                    else:
                        pe.wait_ge(sem("lru_sig"), t + 1)
                    pe.matmul(ps[:, 4 + t, :], gate[:, t, :], lru_xc[:, t, :], start=True,
                              stop=True).then_inc(sem("lru_gates"), 1)

            pe.wait_ge(sem("mix_c_landed"), 16 * 9)
            for n in range(2):
                for s in range(4):
                    project_unit(U_SGU, G_SGU, n, s, 32)
                    if (n, s) == (0, 1):
                        lru_gates(gate_a, True)
                    if (n, s) == (0, 2):
                        lru_gates(gate_x, False)
            for n in range(3):
                for s in range(4):
                    project_unit(U_SC, G_SC, n, s, 32)
                    if (n, s) == (0, 1):
                        pe.wait_ge(sem("lru_sig"), 8)
                        group_norm(0, Y[:, 8:12, :])
                    if (n, s) == (0, 2):
                        pe.wait_ge(sem("sgu_gelu"), 1)
                        pe.wait_ge(sem("group_root"), 1)
                        for tt in range(4):
                            for t in range(4):
                                mm = turn(ps[:, 4 + tt, 128 * t:128 * t + 128],
                                          proj[:, 12 + t, PAD + 128 * tt:PAD + 128 * tt + 128])
                            mm.then_inc(sem("sgu_turned"), 1)
                    if (n, s) == (1, 3):
                        pe.wait_ge(sem("sgu_normed"), 1)
                        for g in range(4):
                            for tt in range(4):
                                mm = pe.matmul(ps[:, 4 + g, 128 * tt:128 * tt + 128], Y[:, 12 + tt, 128 * g:128 * g + 128],
                                               sgu_w[:, g, :], start=True, stop=True)
                            mm.then_inc(sem("sgu_mixed"), 1)
                    if (n, s) == (2, 3):
                        group_norm(1, Y[:, 12:16, :])

            def l2_sums(tiles):
                for t in tiles:
                    pe.wait_ge(sem("l2_sq"), t + 1)
                    if t >= 4:
                        pe.wait_ge(sem("l2_root"), t - 3)
                    pe.matmul(ps[:, 4 + t % 4, :], ones, conv_out[:, t, :], start=True,
                              stop=True).then_inc(sem("l2_sums"), 1)

            def turn_ba():
                pe.wait_ge(sem("ba_rows"), 1)
                for tt in range(4):
                    mm = pe.transpose(ps[:, 5, 8 * tt:8 * tt + 8], ba_rows[:, 128 * tt:128 * tt + 128], ident[0:8, 0:8])
                mm.then_inc(sem("ba_turned"), 1)

            def sum_gates():
                pe.wait_ge(sem("gate_ready"), 1)
                pe.wait_ge(sem("l2_root"), 1)
                for k in range(4):
                    mm = pe.matmul(ps[:, 4, 16 * k:16 * k + 16], gdn_c[:, k, :], gate, start=True, stop=True)
                mm.then_inc(sem("g_summed"), 1)

            for n in range(4):
                for s in range(4):
                    project_unit(U_QKVZ, G_QKVZ, n, s, 32)
                    if (n, s) == (0, 3):
                        pe.wait_ge(sem("ba_split"), 1)
                        for k in range(KT):
                            w = slice(8 * k, 8 * k + 8)
                            o = ps[0:8, 4, :]
                            pe.matmul(o, ba_hi[:, w], h_hi[:, k, :], start=(k == 0), stop=False)
                            pe.matmul(o, ba_hi[:, w], h_lo[:, k, :], start=False, stop=False)
                            mm = pe.matmul(o, ba_lo[:, w], h_hi[:, k, :], start=False, stop=(k == KT - 1))
                        mm.then_inc(sem("ba_done"), 1)
                    if (n, s) == (1, 0):
                        pe.wait_ge(sem("group_root"), 2)
                        group_norm(2, sc_sq)
                    if (n, s) == (1, 1):
                        turn_ba()
                    if (n, s) == (1, 3):
                        pe.wait_ge(sem("ba_tok"), 1)
                        pe.wait_ge(sem("group_root"), 3)
                        l2_sums(range(4))
                    if (n, s) == (2, 1):
                        sum_gates()
                    if (n, s) == (2, 3):
                        pe.wait_ge(sem("g_sums_read"), 1)
                        l2_sums(range(4, 8))
            pe.wait_ge(bank_free, G_WO2 + 2)
            pe.wait_ge(sem("l2_normed"), 8)
            pe.wait_ge(sem("qkv_silu"), 3)

            def per_tile(o, lhs, rhs):
                for tt in range(4):
                    x = slice(128 * tt, 128 * tt + 128)
                    mm = pe.matmul(o[:, x], lhs[:, x], rhs[:, x], start=True, stop=True)
                return mm

            for pair in range(2):
                heads = [(m, 2 * pair + m, 4 * m) for m in range(2)]
                for m, h, b in heads:
                    if pair:
                        pe.wait_ge(sem("w_t_ready"), h - 1)
                        pe.wait_ge(sem("u_ready"), h - 1)
                    k, v = proj[:, KT_ + h, PAD:], proj[:, VT + h, PAD:]
                    for tt in range(4):
                        x = slice(128 * tt, 128 * tt + 128)
                        turn(ps[:, b, x], k[:, x])
                        mm = turn(ps[:, b + 1, x], v[:, x])
                    mm.then_inc(sem("kv_turned"), 1)
                    pe.wait_ge(sem("diags"), h + 1)
                    pe.matmul(ps[:, b + 2, :], ones, tmp_a[:, m, :], start=True, stop=True)
                    pe.matmul(ps[:, b + 3, :], ones, tmp_b[:, m, :], start=True, stop=True).then_inc(sem("rows_spread"), 1)
                for m, h, b in heads:
                    q, k = proj[:, QT + h, PAD:], proj[:, KT_ + h, PAD:]
                    pe.wait_ge(sem("kv_taken"), h + 1)
                    per_tile(ps[:, b, :], k, q).then_inc(sem("qk_done"), 1)
                    pe.wait_ge(sem("kb_ready"), h + 1)
                    per_tile(ps[:, b + 1, :], k, tmp_b[:, m, :]).then_inc(sem("kk_done"), 1)
                for m, h, b in heads:
                    pe.wait_ge(sem("nt_ready"), h + 1)
                    for tt in range(4):
                        x = slice(128 * tt, 128 * tt + 128)
                        mm = turn(ps[:, b + 2, x], pows[:, m, 0, 1, x])
                    mm.then_inc(sem("n_turned"), 1)
                for it in range(5):
                    v, w = it % 2, 1 - it % 2
                    for m, h, b in heads:
                        n = (5 * pair + it) * 2 + m
                        n2 = (4 * pair + it) * 2 + m
                        if it == 0:
                            pe.wait_ge(sem("n_ready"), h + 1)
                            pe.wait_ge(sem("attn_ready"), h + 1)
                        per_tile(ps[:, b, :], pows[:, m, v, 1, :], pows[:, m, v, 0, :]).then_inc(sem("n_squared"), 1)
                        if it < 4:
                            per_tile(ps[:, b + 1, :], pows[:, m, v, 0, :], pows[:, m, v, 1, :]).then_inc(sem("nt_squared"), 1)
                    for m, h, b in heads:
                        n = (5 * pair + it) * 2 + m
                        pe.wait_ge(sem("n_power"), n + 1)
                        pe.wait_ge(sem("inv_ready"), (6 * pair + it) * 2 + m + 1)
                        per_tile(ps[:, b + 2, :], pows[:, m, w, 0, :], inv_t[:, h, :]).then_inc(sem("inv_step"), 1)
                        if it < 4:
                            pe.wait_ge(sem("nt_power"), (4 * pair + it) * 2 + m + 1)
                for m, h, b in heads:
                    pe.wait_ge(sem("inv_ready"), (6 * pair + 5) * 2 + m + 1)
                    per_tile(ps[:, b, :], k_be[:, h, :], inv_t[:, h, :]).then_inc(sem("w_t_done"), 1)
                    per_tile(ps[:, b + 1, :], inv_t[:, h, :], v_b[:, h, :]).then_inc(sem("u_done"), 1)
            pe.wait_ge(sem("w_t_ready"), 4)
            pe.wait_ge(sem("u_ready"), 4)
            def scan_output(tt, h):
                if tt >= 2:
                    pe.wait_ge(sem("o_taken"), tt - 1)
                hs = slice(128 * h, 128 * h + 128)
                o = ps[:, 1 + tt % 2, hs]
                pe.matmul(o, v_new[:, tt % 2, hs], attn_t[:, h, 128 * tt:128 * tt + 128], start=True, stop=False)
                for half in range(2):
                    q = PAD + 128 * tt + 64 * half
                    mm = pe.matmul(o[:, 64 * half:64 * half + 64], state[:, (2 * tt + half) % N_STATES, hs],
                                   proj[:, QT + h, q:q + 64], start=False, stop=(half == 1))
                mm.then_inc(sem("o_done"), 1)

            for c in range(8):
                r, tt = 64 * (c % 2), c // 2
                x = slice(128 * tt + r, 128 * tt + r + 64)
                rows = slice(r, r + 64)
                done = c // 2 - 1
                pe.wait_ge(sem("state_ready"), c + 1)
                for h in range(4):
                    mm = pe.matmul(ps[rows, 0, 128 * h:128 * h + 128], w_t[:, h, x],
                                   state[:, c % N_STATES, 128 * h:128 * h + 128], start=True, stop=True)
                mm.then_inc(sem("w_state"), 1)
                if done >= 0:
                    scan_output(done, 2 * (c % 2))
                pe.wait_ge(sem("v_new_ready"), c + 1)
                for h in range(4):
                    mm = pe.matmul(ps[:, 3, 128 * h:128 * h + 128], k_g[rows, h, 128 * tt:128 * tt + 128],
                                   v_new[rows, tt % 2, 128 * h:128 * h + 128], start=True, stop=True)
                mm.then_inc(sem("state_add"), 1)
                if done >= 0:
                    scan_output(done, 2 * (c % 2) + 1)
            for h in range(4):
                scan_output(3, h)
            for h in range(4):
                pe.wait_ge(sem("gdn_sq"), h + 1)
                pe.matmul(ps[:, 4 + h, :], ones, k_be[:, h, :], start=True, stop=True).then_inc(sem("gdn_sums"), 1)

            def project_y(i):
                for s in range(4):
                    g, half = s // 2, s % 2
                    pe.wait_ge(w_ready, U_WO2 + 4 * i + s + 3)
                    if half == 0:
                        pe.wait_ge(bank_free, G_WO2 + 2 * i + g + 1)
                    for k in range(8):
                        t = 8 * half + k
                        pe.wait_ge(h_ready, 48 + t + 1)
                        for j in range(2):
                            w = slice(k * 256 + j * 128, k * 256 + j * 128 + 128)
                            o = ps[:, 2 * g + j, :]
                            pe.matmul(o, w_hi[:, s % 2, w], h_hi[:, t, :], start=(t == 0), stop=False)
                            pe.matmul(o, w_hi[:, s % 2, w], h_lo[:, t, :], start=False, stop=False)
                            mm = pe.matmul(o, w_lo[:, s % 2, w], h_hi[:, t, :], start=False, stop=(t == 15))
                    mm.then_inc(w_used, 1)

            with pe.Fori(0, 4) as i:
                project_y(i)
            sum_squares(4)
            def ffn_up(u, g, norm=None):
                for s in range(8):
                    half = s % 2
                    pe.wait_ge(w_ready, u + s + 3)
                    if half == 0:
                        pe.wait_ge(bank_free, g + s // 2 + 1)
                    for k in range(8):
                        t = 8 * half + k
                        pe.wait_ge(h_ready, 64 + t + 1)
                        for j in range(2):
                            w = slice(k * 256 + j * 128, k * 256 + j * 128 + 128)
                            o = ps[:, 2 * (s // 2 % 2) + j, :]
                            pe.matmul(o, w_hi[:, s % 2, w], h_hi[:, t, :], start=(t == 0), stop=False)
                            pe.matmul(o, w_hi[:, s % 2, w], h_lo[:, t, :], start=False, stop=False)
                            mm = pe.matmul(o, w_lo[:, s % 2, w], h_hi[:, t, :], start=False, stop=(t == 15))
                    mm.then_inc(w_used, 1)
                    if norm is not None and s == 1:
                        sum_squares(norm)

            def ffn_down(u, seg, par_):
                for q in range(4):
                    pe.wait_ge(w_ready, u + q + 3)
                    for j in range(4):
                        pe.wait_ge(down_free, seg * 16 + (4 * q + j + 1))
                        for k in range(4):
                            if q == 0 and j == 0:
                                pe.wait_ge(f_ready, seg * 2 + (k // 2 + 1))
                            w = slice(k * 512 + j * 128, k * 512 + j * 128 + 128)
                            o = ps[:, 4 + j, :]
                            pe.matmul(o, w_hi[:, q % 2, w], f_hi[:, par_, k, :], start=(k == 0), stop=False)
                            pe.matmul(o, w_hi[:, q % 2, w], f_lo[:, par_, k, :], start=False, stop=False)
                            mm = pe.matmul(o, w_lo[:, q % 2, w], f_hi[:, par_, k, :], start=False, stop=(k == 3))
                        mm.then_inc(w_used if j == 3 else down_tile, 1)

            ffn_up(U_FFN, G_FFN, norm=5)
            with pe.Fori(0, (SEGS - 1) // 2) as i:
                for e in range(2):
                    u = U_FFN + 8 + 24 * i + 12 * e
                    ffn_up(u, G_FFN + 4 + 8 * i + 4 * e)
                    ffn_down(u + 8, 2 * i + e, e)
            ffn_down(N_UNITS - 4, SEGS - 1, (SEGS - 1) % 2)
            sum_squares(6, 0)

        @block.scalar
        def _(act):
            order = Order(act, act_order)
            A = nc.scalar.activation

            def step_hi(u0, pairs, s):
                slot = (s + 1) % 2
                act.wait_ge(raw_landed[slot], (pairs + ((s + 1) // 2 + 1)) * 16)
                act.wait_ge(w_used, u0 + s + 1)
                A(w_hi[:, slot, :], raw[:, slot, :], ACT.Copy).then_inc(w_hi_ready, 1)

            def square(n, t_ap):
                if n >= 2:
                    act.wait_ge(sq_used, n - 1)
                A(squares[:, n % 2, :], t_ap, ACT.Square).then_inc(sq_ready, 1)

            def one_over_rms_root(k):
                act.wait_ge(sem("sq_summed"), k + 1)
                if k >= 1:
                    act.wait_ge(rstd_ready, k)
                A(root[:, :], ps[:, SS, :], ACT.Sqrt, bias=eps_c, scale=1.0 / D).then_inc(root_ready, 1)

            def steps_hi(u0, quads, norm=None):
                first = 0
                if norm is not None:
                    for s in range(4):
                        step_hi(u0, u0 // 2, s)
                        if s == 1:
                            one_over_rms_root(norm)
                    first = 1
                with act.Fori(first, quads) as i:
                    for s in range(4):
                        step_hi(u0 + 4 * i, u0 // 2 + 2 * i, s)

            act.wait_ge(params_landed, 32)
            act.wait_ge(raw_landed[0], 16)
            A(w_hi[:, 0, :], raw[:, 0, :], ACT.Copy).then_inc(w_hi_ready, 1)
            for t in range(KT):
                act.wait_ge(x_landed[t // 4], 16)
                A(h_hi[:, t, :], X[:, t, :], ACT.Identity, scale=par("g0", t)).then_inc(h_hi_ready, 1)
                square(t, X[:, t, :])
            for l in range(2):
                steps_hi(U_L[l], 4, norm=l)
                for tt in range(4):
                    act.wait_ge(*since("v_turned", l, tt + 1))
                    A(v_tok[:, tt, :], ps[:, 2 + tt, :], ACT.Copy).then_inc(sem("v_tok_ready"), 1)
                act.wait_ge(bank_free, G_L[l] + 8 + 2)
                for t in (6, 14):
                    A(proj[:, t:t + 2, PAD:], proj[:, t:t + 2, PAD:], ACT.Silu).then_inc(sem("gates"), 1)

                def exps(n, buf):
                    act.wait_ge(*since("neg_max", l, n + 1))
                    for i in range(4):
                        b = probs[:, buf, Q_OFF[i]:Q_OFF[i] + 128 * (i + 1)]
                        A(b, b, ACT.Exp, bias=neg_max[:, 4 * n + i:4 * n + i + 1],
                          accum_out=den[:, 4 * n + i:4 * n + i + 1]).then_inc(sem("l_probs"), 1)

                def take_pt_a(n):
                    act.wait_ge(*since("l_turned", l, n + 1))
                    if n >= 2:
                        act.wait_ge(*since("l_o", l, n - 1))
                    A(probs_t[:, n % 2, 0:512], ps[:, 4, :], ACT.Copy).then_inc(sem("l_pt_a"), 1)

                if l == 0:
                    exps(0, 0)
                    for n in range(8):
                        take_pt_a(n)
                        if n < 7:
                            exps(n + 1, (n + 1) % 4)
                else:
                    act.wait_ge(sem("lam_sums"), 2)
                    A(lam_s[:, 2:4], lam_s[:, 0:2], ACT.Exp).then_inc(sem("lam_exp"), 1)
                    exps(0, 0)
                    exps(1, 1)
                    for n in range(4):
                        take_pt_a(n)
                        if n < 3:
                            exps(2 * n + 2, (2 * n + 2) % 4)
                            exps(2 * n + 3, (2 * n + 3) % 4)
                    act.wait_ge(sem("diff_ss"), 1)
                    A(o_root, o_ss, ACT.Sqrt, bias=eps_c, scale=1.0 / HEAD).then_inc(sem("diff_root"), 1)

                def round_y(k):
                    act.wait_ge(*since("y1", l, k + 1))
                    A(y1_hi[:, k, :], y1[:, :], ACT.Copy).then_inc(sem("y1_hi_ready"), 1)

                if l == 1:
                    round_y(0)
                    round_y(1)

                    def stick_z(h):
                        z, L = probs[:, 2 * (h % 2), :], probs[:, 2 * (h % 2) + 1, :]
                        act.wait_ge(sem("z_scores"), h + 1)
                        if h >= 2:
                            act.wait_ge(sem("stick_o"), h - 1)
                        for kt in range(4):
                            at = (0, 512, 1024, 1280)[kt]
                            n = 512 - 128 * kt
                            A(z[:, Z_OFF[kt]:Z_OFF[kt] + n], ps[:, at // 512, at % 512:at % 512 + n], ACT.Copy,
                              scale=HEAD ** -0.5).then_inc(sem("z_read"), 1)
                        act.wait_ge(sem("z_read"), 4 * h + 4)
                        order.link(A(L, z, ACT.Abs))
                        order.link(A(L, L, ACT.Exp, scale=-1.0))
                        A(L, L, ACT.Ln, bias=one_c).then_inc(sem("log1p"), 1)

                    def stick_exp(h):
                        z = probs[:, 2 * (h % 2), :]
                        act.wait_ge(sem("log_a"), h + 1)
                        A(z, z, ACT.Exp).then_inc(sem("stick_a"), 1)

                    stick_z(0)
                    for h in range(4):
                        if h < 3:
                            stick_z(h + 1)
                        stick_exp(h)
                    round_y(2)
                    round_y(3)
                else:
                    for k in range(4):
                        round_y(k)
                for q in range(4):
                    step_hi(U_L[l] + U_IN, (U_L[l] + U_IN) // 2, q)
                    for j in range(4):
                        t = 4 * q + j
                        act.wait_ge(x_ready, 16 * l + t + 1)
                        if l == 0:
                            A(h_hi[:, t, :], X[:, t, :], ACT.Identity, scale=par("g1", t)).then_inc(h_hi_ready, 1)
                        square(16 * (l + 1) + t, X[:, t, :])
                if l == 1:
                    one_over_rms_root(2)

            def split_tiles(x0, n0, gain):
                for t in range(KT):
                    act.wait_ge(x_ready, x0 + t + 1)
                    A(h_hi[:, t, :], X[:, t, :], ACT.Identity, scale=par(gain, t)).then_inc(h_hi_ready, 1)
                    square(n0 + t, X[:, t, :])

            def group_squares(k, y, sq):
                act.wait_ge(sem("mixer_out"), k + 1)
                for t in range(4):
                    A(sq[:, t, :], y[:, t, :], ACT.Square).then_inc(sem("group_sq"), 1)

            def group_root(k):
                if k >= 1:
                    act.wait_ge(sem("group_normed"), k)
                act.wait_ge(sem("group_sums"), k + 1)
                A(root[:, :], ps[:, SS, :], ACT.Sqrt, bias=eps_c, scale=1.0 / 512).then_inc(sem("group_root"), 1)

            split_tiles(32, 48, "pre_mix")
            order.link(A(lru_s[:, 0:4], par("lam", 0, 4), ACT.Abs))
            order.link(A(lru_s[:, 0:4], lru_s[:, 0:4], ACT.Exp, scale=-1.0))
            A(lru_s[:, 4:8], lru_s[:, 0:4], ACT.Ln, bias=one_c).then_inc(sem("lam_log"), 1)
            steps_hi(U_LRU, M2_QUADS["lru"], norm=3)
            for n in range(2):
                for s in range(4):
                    step_hi(U_SGU + 4 * n, U_SGU // 2 + 2 * n, s)
                    if (n, s) == (0, 2):
                        for t in range(4):
                            act.wait_ge(sem("lru_gates"), t + 1)
                            A(lru_r[:, t, :], ps[:, 4 + t, :], ACT.Sigmoid, bias=par("ba", t)).then_inc(sem("lru_sig"), 1)
                    if (n, s) == (0, 3):
                        for t in range(4):
                            act.wait_ge(sem("lru_gates"), 4 + t + 1)
                            A(lru_i[:, t, :], ps[:, 4 + t, :], ACT.Sigmoid, bias=par("bx", t)).then_inc(sem("lru_sig"), 1)
                        act.wait_ge(sem("lru_rate"), 1)
                        act.wait_ge(sem("lru_sig"), 8)
                        for t in range(4):
                            A(lru_a[:, t, :], lru_r[:, t, :], ACT.Exp, scale=lru_s[:, 8 + t:9 + t]).then_inc(sem("lru_a"), 1)
                        for t in range(4):
                            A(lru_r[:, t, :], lru_r[:, t, :], ACT.Tanh, scale=lru_s[:, 8 + t:9 + t]).then_inc(sem("lru_tanh"), 1)
                    if (n, s) == (1, 0):
                        A(proj[:, 4:8, PAD:], proj[:, 4:8, PAD:], ACT.Gelu_apprx_tanh).then_inc(sem("lru_gelu"), 1)
                    if (n, s) == (1, 1):
                        act.wait_ge(sem("lru_m"), 1)
                        A(lru_r, lru_r, ACT.Sqrt, scale=-1.0).then_inc(sem("lru_mult"), 1)
            for n in range(3):
                for s in range(4):
                    step_hi(U_SC + 4 * n, U_SC // 2 + 2 * n, s)
                    if (n, s) == (0, 0):
                        group_squares(0, Y[:, 4:8, :], Y[:, 8:12, :])
                        act.wait_ge(bank_free, G_SC + 2)
                        A(proj[:, 12:16, PAD:], proj[:, 12:16, PAD:], ACT.Gelu_apprx_tanh).then_inc(sem("sgu_gelu"), 1)
                    if (n, s) == (0, 2):
                        group_root(0)
                        A(proj[:, 8:12, PAD:], proj[:, 8:12, PAD:], ACT.Gelu_apprx_tanh).then_inc(sem("sgu_gelu"), 1)
                    if (n, s) == (1, 1):
                        act.wait_ge(sem("sgu_stats"), 1)
                        A(stats[:, :, 8:9], stats[:, :, 7:8], ACT.Sqrt, bias=eps_c).then_inc(sem("sgu_root"), 1)
                    if (n, s) == (2, 0):
                        act.wait_ge(sem("mix_c_landed"), 16 * 17)
                        A(ba_hi[:, :], ba_raw, ACT.Copy).then_inc(sem("ba_hi_ready"), 1)
                    if (n, s) == (2, 2):
                        group_squares(1, Y[:, 8:12, :], Y[:, 12:16, :])

            def silu_conv(n):
                act.wait_ge(sem("qkv_conved"), n + 1)
                c0 = 4 * (n % 2)
                A(proj[:, (QT, KT_, VT)[n]:(QT, KT_, VT)[n] + 4, PAD:], conv_out[:, c0:c0 + 4, :], ACT.Silu).then_inc(sem("qkv_silu"), 1)

            def l2_squares(n):
                act.wait_ge(sem("qkv_silu"), n + 1)
                for t in range(4 * n, 4 * n + 4):
                    A(conv_out[:, t, :], proj[:, (QT, KT_)[n] + t % 4, PAD:], ACT.Square).then_inc(sem("l2_sq"), 1)

            def l2_roots(n):
                for t in range(4 * n, 4 * n + 4):
                    act.wait_ge(sem("l2_sums"), t + 1)
                    A(conv_out[:, t, :], ps[:, 4 + t % 4, :], ACT.Sqrt, bias=eps_c).then_inc(sem("l2_root"), 1)

            def gates():
                act.wait_ge(sem("ba_tok"), 1)
                A(beta.rearrange("p (h t) -> p t h", h=4), ba_tok.rearrange("p (t c) -> p t c", c=8)[:, :, 0:4],
                  ACT.Sigmoid).then_inc(sem("beta_ready"), 1)
                act.wait_ge(sem("a_dt"), 1)
                A(alog_sb[:, 0:4], alog_sb[:, 0:4], ACT.Exp).then_inc(sem("a_exp"), 1)
                order.link(A(exp_g, g_tmp, ACT.Abs))
                order.link(A(exp_g, exp_g, ACT.Exp, scale=-1.0))
                A(exp_g, exp_g, ACT.Ln, bias=one_c).then_inc(sem("a_log1p"), 1)

            def decays():
                act.wait_ge(sem("g_sums_read"), 1)
                A(exp_g, g_sums[:, 0:16], ACT.Exp).then_inc(sem("exp_g_ready"), 1)
                A(g_last, g_sums[:, 32:64], ACT.Exp).then_inc(sem("exp_g_ready"), 1)
                act.wait_ge(sem("kgs_log"), 1)
                A(kgs, kgs, ACT.Exp).then_inc(sem("exp_g_ready"), 1)

            for n in range(4):
                for s in range(4):
                    step_hi(U_QKVZ + 4 * n, U_QKVZ // 2 + 2 * n, s)
                    if (n, s) == (0, 0):
                        group_root(1)
                    if (n, s) == (0, 3):
                        group_squares(2, Y[:, 12:16, :], sc_sq)
                    if (n, s) == (1, 1):
                        group_root(2)
                    if n in (1, 2) and s == 2:
                        silu_conv(n - 1)
                    if n in (1, 2) and s == 3:
                        l2_squares(n - 1)
                    if n == 1 and s == 3:
                        gates()
                    if n in (2, 3) and s == 0:
                        l2_roots(n - 2)
                    if n == 2 and s == 3:
                        decays()
            silu_conv(2)
            act.wait_ge(bank_free, G_WO2 + 2)
            A(proj[:, ZT:ZT + 4, PAD:], proj[:, ZT:ZT + 4, PAD:], ACT.Silu).then_inc(sem("z_silu"), 1)
            for pair in range(2):
                heads = [(m, 2 * pair + m, 4 * m) for m in range(2)]
                for m, h, b in heads:
                    act.wait_ge(sem("rows_spread"), h + 1)
                    if pair:
                        act.wait_ge(sem("inv_step"), 2 * 5 * pair)
                    A(pows[:, m, 1, 0, :], ps[:, b + 2, :], ACT.Exp).then_inc(sem("exp_row"), 1)
                    act.wait_ge(sem("decay_log"), h + 1)
                    A(tmp_a[:, m, :], tmp_a[:, m, :], ACT.Exp).then_inc(sem("decay_ready"), 1)
                for m, h, b in heads:
                    act.wait_ge(sem("n_turned"), h + 1)
                    A(pows[:, m, 0, 0, :], ps[:, b + 2, :], ACT.Copy).then_inc(sem("n_ready"), 1)
                for it in range(5):
                    for m, h, b in heads:
                        n = (5 * pair + it) * 2 + m
                        act.wait_ge(sem("n_squared"), n + 1)
                        if it == 0:
                            act.wait_ge(sem("q_scaled"), h + 1)
                        A(pows[:, m, 1 - it % 2, 0, :], ps[:, b, :], ACT.Copy).then_inc(sem("n_power"), 1)
                for m, h, b in heads:
                    act.wait_ge(sem("w_t_done"), h + 1)
                    A(w_t[:, h, :], ps[:, b, :], ACT.Copy).then_inc(sem("w_t_ready"), 1)
            for tt in range(4):
                act.wait_ge(sem("o_done"), 4 * tt + 4)
                A(proj[:, VT:VT + 4, PAD + 128 * tt:PAD + 128 * tt + 128], ps[:, 1 + tt % 2, :].rearrange("p (h n) -> p h n", h=4),
                  ACT.Copy).then_inc(sem("o_taken"), 1)
            act.wait_ge(sem("o_taken"), 4)
            for h in range(4):
                A(k_be[:, h, :], proj[:, VT + h, PAD:], ACT.Square).then_inc(sem("gdn_sq"), 1)
            for h in range(4):
                act.wait_ge(sem("gdn_sums"), h + 1)
                A(k_g[:, h, :], ps[:, 4 + h, :], ACT.Sqrt, bias=eps_c, scale=1.0 / GDN_D).then_inc(sem("gdn_root"), 1)

            act.wait_ge(sem("mixer_out"), 4)
            with act.Fori(0, 16) as i:
                A(h_hi[:, i, :], Y[:, i, :], ACT.Copy).then_inc(h_hi_ready, 1)
            for g in range(8):
                for s in range(2):
                    step_hi(U_WO2 + 2 * g, U_WO2 // 2 + g, s)
                act.wait_ge(bank_free, G_WO2 + g + 3)
                for t in (2 * g, 2 * g + 1):
                    square(64 + t, y2[:, t, :])
            one_over_rms_root(4)
            split_tiles(48, 80, "pre_ffn")

            def ffn_up(u, pairs, seg, par_, norm=None):
                for s in range(8):
                    step_hi(u, pairs, s)
                    if norm is not None and s == 1:
                        one_over_rms_root(norm)
                    b, c = (s - 1) // 4, (s - 1) // 2 % 2
                    if s in (2, 6):
                        act.wait_ge(sem("f_gates"), seg * 2 + (b + 1))
                        A(f_gate[:, :, :], f_gate[:, :, :], ACT.Gelu_apprx_tanh).then_inc(sem("f_gelu"), 1)
                    if s == 4:
                        round_values(seg, b, par_)

            def round_values(seg, b, par_):
                act.wait_ge(sem("f_gated"), seg * 2 + (b + 1))
                A(f_hi[:, par_, 2 * b:2 * b + 2, :], f_val[:, :, :], ACT.Copy).then_inc(sem("f_hi_ready"), 1)

            def ffn_down(u, pairs, seg, par_):
                for q in range(4):
                    step_hi(u, pairs, q)
                    if q == 0:
                        round_values(seg, 1, par_)

            ffn_up(U_FFN, U_FFN // 2, 0, 0, norm=5)
            round_values(0, 1, 0)
            with act.Fori(0, (SEGS - 1) // 2) as i:
                for e in range(2):
                    off = 8 + 12 * e
                    ffn_up(U_FFN + off + 24 * i, (U_FFN + off) // 2 + 12 * i, 2 * i + (1 + e), 1 - e)
                    ffn_down(U_FFN + off + 8 + 24 * i, (U_FFN + off + 8) // 2 + 12 * i, 2 * i + (1 + e), 1 - e)
            for q in range(4):
                if q < 3:
                    step_hi(N_UNITS - 4, (N_UNITS - 4) // 2, q)
                for j in range(4):
                    n = 4 * q + j
                    act.wait_ge(down_free, 4 + 16 * (SEGS - 1) + n + 1)
                    square(96 + n, y_acc[:, n, :])
            act.wait_ge(sem("sq_summed"), 7)
            act.wait_ge(rstd_ready, 6)
            A(root[:, :], ps[:, 0, :], ACT.Sqrt, bias=eps_c, scale=1.0 / D).then_inc(root_ready, 1)

        @block.vector
        def _(dve):
            order = Order(dve, dve_order)
            V = nc.vector

            def step_lo(u0, s):
                slot = (s + 1) % 2
                dve.wait_ge(w_hi_ready, u0 + s + 2)
                V.tensor_tensor(w_lo[:, slot, :], raw[:, slot, :], w_hi[:, slot, :].bitcast(F32),
                                ALU.subtract).then_inc(w_ready, 1)

            def low_part(n, t, g):
                dve.wait_ge(h_hi_ready, n + 1)
                V.scalar_tensor_tensor(out=h_lo[:, t, :], in0=X[:, t, :], scalar=g,
                                       in1=h_hi[:, t, :].bitcast(F32), op0=ALU.mult,
                                       op1=ALU.subtract).then_inc(h_ready, 1)

            def one_over_root(k):
                dve.wait_ge(root_ready, k + 1)
                V.reciprocal(rstd[:, :], root[:, :]).then_inc(rstd_ready, 1)
                dve.wait_ge(rstd_ready, k + 1)

            def project(u0, quads, tile0, norm=None):
                def quad(i, norm=None):
                    for s in range(4):
                        step_lo(u0 + 4 * i, s)
                        if norm is not None and s == 1:
                            one_over_root(norm)
                        if s % 2:
                            dve.wait_ge(w_used, u0 + 4 * i + s + 1 + 1)
                            for j in range(2):
                                ins = V.tensor_tensor(proj[:, 4 * i + (tile0 + s - 1 + j), PAD:PAD + S],
                                                      ps[:, s - 1 + j, :], rstd[:, :], ALU.mult)
                            ins.then_inc(bank_free, 1)

                first = 0
                if norm is not None:
                    quad(0, norm)
                    first = 1
                with dve.Fori(first, quads) as i:
                    quad(i)

            V.memset(credit[:, 0:1], 0.0).then_inc(bank_free, 1)
            V.memset(credit[:, 1:2], 0.0).then_inc(bank_free, 1)
            V.memset(credit[:, 4:5], 0.0).then_inc(w_ready, 1)
            V.memset(credit[:, 5:6], 0.0).then_inc(w_ready, 1)
            dve.wait_ge(params_landed, 32)
            dve.wait_ge(w_hi_ready, 1)
            V.tensor_tensor(w_lo[:, 0, :], raw[:, 0, :], w_hi[:, 0, :].bitcast(F32),
                            ALU.subtract).then_inc(w_ready, 1)
            for t in range(KT):
                low_part(t, t, par("g0", t))
            for l in range(2):
                project(U_L[l], 4, 0, norm=l)
                dve.wait_ge(bank_free, G_L[l] + 8 + 2)
                dve.wait_ge(*since("attn_c_landed", l, 16 * 8))
                for n, t in enumerate([0, 1, 2, 3, 8, 9, 10, 11] if l == 0 else [0, 1, 2, 3]):
                    tile = proj[:, t, PAD:PAD + S]
                    dve.wait_ge(*since("rotated", l, n + 1))
                    V.tensor_tensor(rot_sin[:, n % 2, :], ps[:, n % 2, :], sin_sb[:, :], ALU.mult)\
                     .then_inc(sem("rot_read"), 1)
                    order.link(V.tensor_tensor(tile, tile, cos_sb[:, :], ALU.mult))
                    dve.wait_ge(*since("rot_read", l, n + 1))
                    V.tensor_tensor(tile, tile, rot_sin[:, n % 2, :], ALU.add).then_inc(sem("roped"), 1)

                def mask_scores(n, buf, mask, scale, free=None):
                    if free is not None:
                        dve.wait_ge(*free)
                    for i in range(4):
                        dve.wait_ge(*since("l_scores", l, 4 * n + i + 1))
                        V.tensor_tensor_reduce(
                            out=probs[:, buf, Q_OFF[i]:Q_OFF[i] + 128 * (i + 1)], in0=ps[:, i, 0:128 * (i + 1)],
                            in1=mask_sb[:, mask, 128 * (3 - i):512], scale=scale, scalar=-3.0e38, op0=ALU.add,
                            op1=ALU.max, accum_out=row_max[:, 4 * n + i:4 * n + i + 1])\
                         .then_inc(sem("l_scores_read"), 1)
                    dve.wait_ge(*since("l_scores_read", l, 4 * n + 4))
                    V.tensor_scalar(neg_max[:, 4 * n:4 * n + 4], row_max[:, 4 * n:4 * n + 4], -1.0, None,
                                    ALU.mult).then_inc(sem("neg_max"), 1)

                def take_pt_b(n):
                    dve.wait_ge(*since("l_turned", l, n + 1))
                    if n >= 2:
                        dve.wait_ge(*since("l_o", l, n - 1))
                    V.tensor_copy(probs_t[:, n % 2, 512:1280],
                                  ps[:, 5:7, :].rearrange("p b n -> p (b n)")[:, 0:768])\
                     .then_inc(sem("l_pt_b"), 1)

                def finish_y(k, src, gate_t, scale=None):
                    if k >= 1:
                        dve.wait_ge(*since("y1_ready", l, k))
                    if scale is None:
                        V.tensor_tensor(y1[:, :], src, proj[:, gate_t, PAD:], ALU.mult).then_inc(sem("y1"), 1)
                    else:
                        V.scalar_tensor_tensor(out=y1[:, :], in0=src, scalar=scale, in1=proj[:, gate_t, PAD:],
                                               op0=ALU.mult, op1=ALU.mult).then_inc(sem("y1"), 1)
                    dve.wait_ge(*since("y1_hi_ready", l, k + 1))
                    V.tensor_tensor(y1_lo[:, k, :], y1[:, :], y1_hi[:, k, :].bitcast(F32),
                                    ALU.subtract).then_inc(sem("y1_ready"), 1)

                def wait_gates():
                    dve.wait_ge(*since("gates", l, 2))

                if l == 0:
                    mask_scores(0, 0, 0, HEAD ** -0.5)
                    for n in range(8):
                        dve.wait_ge(*since("l_probs", l, 4 * n + 4))
                        order.link(V.reciprocal(rden[:, 4 * n:4 * n + 4], den[:, 4 * n:4 * n + 4]))
                        take_pt_b(n)
                        if n < 7:
                            mask_scores(n + 1, (n + 1) % 4, (n + 1) // 4, HEAD ** -0.5,
                                        since("l_turned", l, n - 2) if n >= 3 else None)
                        dve.wait_ge(*since("l_o", l, n + 1))
                        V.tensor_tensor(o_tok[:, :, 64 * n:64 * n + 64],
                                        ps[:, 7, 0:256].rearrange("p (i d) -> p i d", d=64),
                                        bc(rden[:, 4 * n:4 * n + 4], 64), ALU.mult)\
                         .then_inc(sem("l_o_read"), 1)
                    wait_gates()
                    for k in range(4):
                        dve.wait_ge(*since("l_y_turned", l, k + 1))
                        finish_y(k, ps[:, k, :], (6, 7, 14, 15)[k])
                else:
                    lambda_init = 0.8 - 0.6 * float(np.exp(-0.3))
                    dve.wait_ge(sem("lam_landed"), 16)
                    for k in range(2):
                        V.tensor_tensor_reduce(out=lam_prod, in0=lam_sb[:, 64 * k:64 * k + 32],
                                               in1=lam_sb[:, 64 * k + 32:64 * k + 64], scale=1.0, scalar=0.0,
                                               op0=ALU.mult, op1=ALU.add, accum_out=lam_s[:, k:k + 1])\
                         .then_inc(sem("lam_sums"), 1)
                        dve.wait_ge(sem("lam_sums"), k + 1)
                    dve.wait_ge(sem("lam_exp"), 1)
                    order.link(V.tensor_tensor(lam_s[:, 4:5], lam_s[:, 3:4], lam_s[:, 2:3], ALU.subtract))
                    order.link(V.tensor_scalar(lam_s[:, 5:6], lam_s[:, 4:5], -lambda_init, None, ALU.add))
                    mask_scores(0, 0, 1, 32 ** -0.5)
                    mask_scores(1, 1, 1, 32 ** -0.5)
                    for n in range(4):
                        dve.wait_ge(*since("l_probs", l, 8 * n + 8))
                        order.link(V.reciprocal(rden[:, 8 * n:8 * n + 8], den[:, 8 * n:8 * n + 8]))
                        order.link(V.tensor_scalar(rden[:, 8 * n + 4:8 * n + 8], rden[:, 8 * n + 4:8 * n + 8],
                                                   lam_s[:, 5:6], None, ALU.mult))
                        b0 = 2 * (n % 2)
                        for i in range(4):
                            b = slice(Q_OFF[i], Q_OFF[i] + 128 * (i + 1))
                            ins = V.tensor_scalar(probs[:, b0, b], probs[:, b0, b],
                                                  rden[:, 8 * n + i:8 * n + i + 1], None, ALU.mult)
                        order.link(ins)
                        for i in range(4):
                            b = slice(Q_OFF[i], Q_OFF[i] + 128 * (i + 1))
                            ins = V.scalar_tensor_tensor(out=probs[:, b0, b], in0=probs[:, b0 + 1, b],
                                                         scalar=rden[:, 8 * n + 4 + i:8 * n + 5 + i],
                                                         in1=probs[:, b0, b], op0=ALU.mult, op1=ALU.add)
                        ins.then_inc(sem("diff_probs"), 1)
                        take_pt_b(n)
                        if n < 3:
                            mask_scores(2 * n + 2, (2 * n + 2) % 4, 1, 32 ** -0.5,
                                        since("l_turned", l, n) if n >= 1 else None)
                        dve.wait_ge(*since("l_o", l, n + 1))
                        V.tensor_copy(o_tok[:, :, 64 * n:64 * n + 64],
                                      ps[:, 7, 0:256].rearrange("p (i d) -> p i d", d=64))\
                         .then_inc(sem("l_o_read"), 1)
                        if n < 3:
                            mask_scores(2 * n + 3, (2 * n + 3) % 4, 1, 32 ** -0.5)
                    dve.wait_ge(*since("l_o_read", l, 4))
                    order.link(V.tensor_tensor(o_tok[:, :, 256:512], o_tok[:, :, 0:256], o_tok[:, :, 0:256], ALU.mult))
                    V.tensor_reduce(o_ss, o_tok[:, :, 256:512].rearrange("p i (h d) -> p i h d", d=64), AX,
                                    ALU.add).then_inc(sem("diff_ss"), 1)
                    dve.wait_ge(sem("diff_root"), 1)
                    order.link(V.reciprocal(o_rstd, o_root))
                    order.link(V.tensor_scalar(o_rstd, o_rstd, 1.0 - lambda_init, None, ALU.mult))
                    for i in range(4):
                        o = o_tok[:, i, 0:256].rearrange("p (h d) -> p h d", d=64)
                        ins = V.tensor_tensor(o, o, bc(o_rstd[:, 4 * i:4 * i + 4], 64), ALU.mult)
                    ins.then_inc(sem("diff_normed"), 1)
                    wait_gates()
                    for k in range(2):
                        dve.wait_ge(*since("l_y_turned", l, k + 1))
                        finish_y(k, ps[:, k, :], 6 + k, par("subln"))
                        V.memset(credit[:, 8 + k:9 + k], 0.0).then_inc(sem("y_taken"), 1)

                    def stick_sp(h):
                        z, L = probs[:, 2 * (h % 2), :], probs[:, 2 * (h % 2) + 1, :]
                        dve.wait_ge(sem("log1p"), h + 1)
                        order.link(V.scalar_tensor_tensor(out=L, in0=z, scalar=0.0, in1=L, op0=ALU.max, op1=ALU.add))
                        for kt in range(4):
                            b = L[:, Z_OFF[kt]:Z_OFF[kt] + 128]
                            ins = V.tensor_tensor(b, b, attn_c[:, 2, :], ALU.mult)
                        ins.then_inc(sem("sp_ready"), 1)

                    def stick_log(h):
                        z = probs[:, 2 * (h % 2), :]
                        for kt in range(4):
                            at = (0, 512, 1024, 1280)[kt]
                            n = 512 - 128 * kt
                            dve.wait_ge(sem("tail"), 4 * h + min(kt + 1, 2) + 2 * (kt >= 2))
                            V.tensor_tensor(z[:, Z_OFF[kt]:Z_OFF[kt] + n], z[:, Z_OFF[kt]:Z_OFF[kt] + n],
                                            ps[:, 4 + at // 512, at % 512:at % 512 + n],
                                            ALU.subtract).then_inc(sem("tail_read"), 1)
                        dve.wait_ge(sem("tail_read"), 4 * h + 4)
                        for kt in range(4):
                            b = z[:, Z_OFF[kt]:Z_OFF[kt] + 128]
                            ins = V.tensor_tensor(b, b, attn_c[:, 3, :], ALU.add)
                        ins.then_inc(sem("log_a"), 1)

                    stick_sp(0)
                    for h in range(4):
                        if h < 3:
                            stick_sp(h + 1)
                        stick_log(h)
                    dve.wait_ge(sem("stick_o"), 4)
                    for k in range(2):
                        finish_y(2 + k, ps[:, 3 if k == 0 else 7, :], 14 + k)
                for q in range(4):
                    step_lo(U_L[l] + U_IN, q)
                    for j in range(4):
                        t = 4 * q + j
                        if j < 3:
                            dve.wait_ge(sem("out_tile"), 12 * l + 3 * q + j + 1)
                        else:
                            dve.wait_ge(w_used, U_L[l] + U_IN + q + 1 + 1)
                        V.tensor_tensor(X[:, t, :], X[:, t, :], ps[:, OUT_BANKS[j], :], ALU.add).then_inc(x_ready, 1)
                        if l == 0 and t >= 1:
                            low_part(16 + t - 1, t - 1, par("g1", t - 1))
                if l == 0:
                    low_part(31, 15, par("g1", 15))
                if l == 1:
                    one_over_root(2)

            def low_pair(n0, i, gain):
                for s in range(2):
                    dve.wait_ge(h_hi_ready, n0 + 2 * i + s + 1)
                    V.scalar_tensor_tensor(out=h_lo[:, 2 * i + s, :], in0=X[:, 2 * i + s, :], scalar=dpar(gain, 2 * i + s),
                                           in1=h_hi[:, 2 * i + s, :].bitcast(F32), op0=ALU.mult,
                                           op1=ALU.subtract).then_inc(h_ready, 1)

            def conv(outs, ins, taps, pad, last, bias=None):
                n = len(taps[0])
                for k in range(n):
                    for r, (o, x) in enumerate(zip(outs, ins)):
                        xk = x[:, pad - n + 1 + k:pad - n + 1 + k + S]
                        if k == 0:
                            ins_ = V.tensor_scalar(o, xk, taps[r][0], bias[r] if bias else None, ALU.mult,
                                                   ALU.add if bias else ALU.bypass)
                        else:
                            ins_ = V.scalar_tensor_tensor(out=o, in0=xk, scalar=taps[r][k], in1=o, op0=ALU.mult, op1=ALU.add)
                        if last is not None and k == n - 1:
                            ins_.then_inc(last, 1)
                    if k < n - 1:
                        order.link(ins_)
                return ins_

            def group_add(k, sq):
                for t in range(1, 4):
                    dve.wait_ge(sem("group_sq"), 4 * k + t + 1)
                    ins = V.tensor_tensor(sq[:, 0, :], sq[:, 0, :], sq[:, t, :], ALU.add)
                    if t < 3:
                        order.link(ins)
                ins.then_inc(sem("group_added"), 1)

            def group_norm(k, y):
                dve.wait_ge(sem("group_root"), k + 1)
                order.link(V.reciprocal(rstd_g, root[:, :]))
                for t in range(4):
                    ins = V.scalar_tensor_tensor(out=y[:, t, :], in0=y[:, t, :], scalar=par("grp", 4 * k + t), in1=rstd_g,
                                                 op0=ALU.mult, op1=ALU.mult)
                ins.then_inc(sem("group_normed"), 1)

            def step(u, s, tile0):
                step_lo(u, s)
                if s % 2:
                    dve.wait_ge(w_used, u + s + 1 + 1)
                    for j in range(2):
                        ins = V.tensor_tensor(proj[:, tile0 + s - 1 + j, PAD:PAD + S], ps[:, s - 1 + j, :],
                                              rstd[:, :], ALU.mult)
                    ins.then_inc(bank_free, 1)

            with dve.Fori(0, 8) as i:
                for s in range(2):
                    t = 2 * i + s
                    V.scalar_tensor_tensor(out=X[:, t, :], in0=X[:, t, :], scalar=dpar("final", t), in1=rstd[:, :],
                                           op0=ALU.mult, op1=ALU.mult).then_inc(x_ready, 1)
                low_pair(32, i, "pre_mix")
            dve.wait_ge(sem("lam_log"), 1)
            order.link(V.tensor_scalar(lru_s[:, 12:16], par("lam", 0, 4), -1.0, 0.0, ALU.mult, ALU.max))
            order.link(V.tensor_tensor(lru_s[:, 16:20], lru_s[:, 12:16], lru_s[:, 4:8], ALU.add))
            V.tensor_scalar(lru_s[:, 8:12], lru_s[:, 16:20], -8.0, None, ALU.mult).then_inc(sem("lru_rate"), 1)
            dve.wait_ge(sem("pads_ready"), 1)
            project(U_LRU, M2_QUADS["lru"], 0, norm=3)
            def lru_conv(taps):
                for k in taps:
                    for t in range(4):
                        o, x, w = lru_xc[:, t, :], proj[:, t, PAD - 3 + k:PAD - 3 + k + S], par("lru_conv", 4 * t + k)
                        if k == 0:
                            ins = V.tensor_scalar(o, x, w, par("lru_b", t), ALU.mult, ALU.add)
                        else:
                            ins = V.scalar_tensor_tensor(out=o, in0=x, scalar=w, in1=o, op0=ALU.mult, op1=ALU.add)
                        if k == 3:
                            ins.then_inc(sem("lru_conved"), 1)
                    if k < 3:
                        order.link(ins)

            for n in range(2):
                for s in range(4):
                    step(U_SGU + 4 * n, s, 8 + 4 * n)
                    if (n, s) == (0, 0):
                        dve.wait_ge(bank_free, G_SGU + 2)
                        dve.wait_ge(sem("x_spilled"), 64)
                        lru_conv((0, 1))
                    if (n, s) == (0, 1):
                        lru_conv((2, 3))
                    if (n, s) == (1, 0):
                        dve.wait_ge(sem("lru_a"), 4)
                        dve.wait_ge(sem("lru_tanh"), 4)
                        for half in range(2):
                            a, r = lru_a[:, 2 * half:2 * half + 2, :], lru_r[:, 2 * half:2 * half + 2, :]
                            order.link(V.tensor_tensor(lru_a2[:, :, :], a, a, ALU.mult))
                            ins = V.scalar_tensor_tensor(out=r, in0=lru_a2[:, :, :], scalar=1.0, in1=r, op0=ALU.add, op1=ALU.mult)
                            if half == 0:
                                order.link(ins)
                            else:
                                ins.then_inc(sem("lru_m"), 1)
                    if (n, s) == (1, 1):
                        order.link(V.tensor_tensor(lru_i, lru_i, lru_xc, ALU.mult))
                    if (n, s) == (1, 2):
                        dve.wait_ge(sem("lru_mult"), 1)
                        order.link(V.tensor_tensor(lru_i, lru_i, lru_r, ALU.mult))
                        for t in range(4):
                            ins = V.tensor_tensor_scan(lru_xc[:, t, :], lru_a[:, t, :], lru_i[:, t, :], 0.0,
                                                       ALU.mult, ALU.add)
                        order.link(ins)
                    if (n, s) == (1, 3):
                        dve.wait_ge(sem("lru_gelu"), 1)
                        V.tensor_tensor(Y[:, 4:8, :], lru_xc, proj[:, 4:8, PAD:], ALU.mult).then_inc(sem("mixer_out"), 1)
            for n in range(3):
                for s in range(4):
                    step(U_SC + 4 * n, s, (0, 4, 12)[n])
                    if (n, s) == (0, 0):
                        dve.wait_ge(sem("mix_c_landed"), 16 * 9)
                        order.link(V.tensor_tensor(sgu_w[:, :, :], sgu_w[:, :, :], bm(tri01[:, :], 4), ALU.mult))
                        group_add(0, Y[:, 8:12, :])
                    if (n, s) == (0, 3):
                        group_norm(0, Y[:, 4:8, :])
                    if (n, s) == (1, 0):
                        for tt in range(4):
                            dve.wait_ge(sem("sgu_turned"), tt + 1)
                            ins = V.bn_stats(stats[:, tt, 0:6], ps[:, 4 + tt, :])
                        order.link(ins)
                        for tt in range(4):
                            ins = V.bn_aggr(stats[:, tt, 6:8], stats[:, tt, 0:6])
                        ins.then_inc(sem("sgu_stats"), 1)
                    if (n, s) == (1, 2):
                        dve.wait_ge(sem("sgu_root"), 1)
                        order.link(V.reciprocal(stats[:, :, 9:10], stats[:, :, 8:9]))
                        for tt in range(4):
                            ins = V.tensor_scalar(Y[:, 12 + tt, :], ps[:, 4 + tt, :], stats[:, tt, 6:7], stats[:, tt, 9:10],
                                                  ALU.subtract, ALU.mult)
                        order.link(ins)
                        order.link(V.tensor_tensor(Y[:, 12:16, :], Y[:, 12:16, :], bm(sgu_sb[:, 0, :], 4), ALU.mult))
                    if (n, s) == (1, 3):
                        V.tensor_tensor(Y[:, 12:16, :], Y[:, 12:16, :], bm(sgu_sb[:, 1, :], 4), ALU.add)\
                         .then_inc(sem("sgu_normed"), 1)
                    if (n, s) == (2, 0):
                        dve.wait_ge(sem("ba_hi_ready"), 1)
                        V.tensor_tensor(ba_lo[:, :], ba_raw, ba_hi[:, :].bitcast(F32), ALU.subtract).then_inc(sem("ba_split"), 1)
                    if (n, s) == (2, 1):
                        for g in range(4):
                            dve.wait_ge(sem("sgu_mixed"), g + 1)
                            ins = V.tensor_tensor(Y[:, 8 + g, :].rearrange("p (n t) -> p n t", t=128),
                                                  ps[:, 4 + g, :].rearrange("p (n t) -> p n t", t=128),
                                                  bm(sgu_sb[:, 2, 128 * g:128 * g + 128], 4), ALU.add)
                        order.link(ins)
                        dve.wait_ge(sem("sgu_gelu"), 2)
                        V.tensor_tensor(Y[:, 8:12, :], Y[:, 8:12, :], proj[:, 8:12, PAD:], ALU.mult)\
                         .then_inc(sem("mixer_out"), 1)
                    if (n, s) == (2, 3):
                        group_add(1, Y[:, 12:16, :])

            def sc_conv(taps):
                for k in taps:
                    for t in range(4):
                        o, x = Y[:, 12 + t, :], proj[:, 4 + t, PAD - 2 + k:PAD - 2 + k + S]
                        w = par("sc_conv", 3 * t + k)
                        if k == 0:
                            ins = V.tensor_scalar(o, x, w, None, ALU.mult)
                        else:
                            ins = V.scalar_tensor_tensor(out=o, in0=x, scalar=w, in1=o, op0=ALU.mult, op1=ALU.add)
                    order.link(ins)

            def conv_taps(n, taps):
                for k in taps:
                    for t in range(4):
                        o = conv_out[:, 4 * (n % 2) + t, :]
                        x = proj[:, (QT, KT_, VT)[n] + t, PAD - 3 + k:PAD - 3 + k + S]
                        w = par("gdn_conv", 4 * (4 * n + t) + k)
                        if k == 0:
                            ins = V.tensor_scalar(o, x, w, None, ALU.mult)
                        else:
                            ins = V.scalar_tensor_tensor(out=o, in0=x, scalar=w, in1=o, op0=ALU.mult, op1=ALU.add)
                    if k < 3:
                        order.link(ins)
                    else:
                        ins.then_inc(sem("qkv_conved"), 1)

            def l2_norm(t):
                dve.wait_ge(sem("l2_root"), t + 1)
                order.link(V.reciprocal(conv_out[:, t, :], conv_out[:, t, :]))
                x = proj[:, (QT, KT_)[t // 4] + t % 4, PAD:]
                V.scalar_tensor_tensor(out=x, in0=x, scalar=GDN_D ** -0.5 if t < 4 else 1.0,
                                       in1=conv_out[:, t, :], op0=ALU.mult, op1=ALU.mult).then_inc(sem("l2_normed"), 1)

            def take_ba():
                dve.wait_ge(sem("ba_done"), 1)
                V.tensor_tensor(ba_rows, ps[0:8, 4, :], rstd[0:8, :], ALU.mult).then_inc(sem("ba_rows"), 1)

            def take_turned():
                dve.wait_ge(sem("ba_turned"), 1)
                V.tensor_copy(ba_tok, ps[:, 5, 0:32]).then_inc(sem("ba_tok"), 1)
                dve.wait_ge(sem("ba_tok"), 1)
                V.tensor_tensor(g_tmp.rearrange("p (h t) -> p t h", h=4), ba_tok.rearrange("p (t c) -> p t c", c=8)[:, :, 4:8],
                                bm(alog_sb[:, 4:8], 4), ALU.add).then_inc(sem("a_dt"), 1)

            def make_gate():
                dve.wait_ge(sem("a_log1p"), 1)
                order.link(V.scalar_tensor_tensor(out=g_tmp, in0=g_tmp, scalar=0.0, in1=exp_g, op0=ALU.max, op1=ALU.add))
                V.scalar_tensor_tensor(out=gate.rearrange("p (h t) -> p h t", h=4),
                                       in0=g_tmp.rearrange("p (h t) -> p h t", h=4), scalar=-1.0,
                                       in1=bc(alog_sb[:, 0:4], 4), op0=ALU.mult, op1=ALU.mult)\
                 .then_inc(sem("gate_ready"), 1)

            def take_sums():
                dve.wait_ge(sem("g_summed"), 1)
                V.tensor_copy(g_sums, ps[:, 4, 0:64]).then_inc(sem("g_sums_read"), 1)
                dve.wait_ge(sem("g_sums_read"), 1)
                V.tensor_tensor(kgs, g_sums[:, 16:32], g_sums[:, 0:16], ALU.subtract).then_inc(sem("kgs_log"), 1)

            def scale_beta():
                dve.wait_ge(sem("exp_g_ready"), 3)
                order.link(V.tensor_tensor(be, beta, exp_g, ALU.mult))

            for n in range(4):
                for s in range(4):
                    u = U_QKVZ + 4 * n
                    step(u, s, (QT, KT_, VT, ZT)[n])
                    if (n, s) == (0, 0):
                        dve.wait_ge(bank_free, G_QKVZ + 2)
                        order.link(V.tensor_tensor(proj[:, 4:8, PAD:], proj[:, 4:8, PAD:], proj[:, 12:16, PAD:], ALU.mult))
                        dve.wait_ge(sem("group_sums"), 2)
                        sc_conv((0,))
                    if (n, s) == (0, 1):
                        sc_conv((1, 2))
                    if (n, s) == (0, 2):
                        V.tensor_tensor(Y[:, 12:16, :], Y[:, 12:16, :], proj[:, 0:4, PAD:], ALU.mult)\
                         .then_inc(sem("mixer_out"), 1)
                        group_norm(1, Y[:, 8:12, :])
                    if (n, s) == (0, 3):
                        group_add(2, sc_sq)
                    if (n, s) == (1, 3):
                        group_norm(2, Y[:, 12:16, :])
                    if (n, s) == (1, 0):
                        dve.wait_ge(bank_free, G_QKVZ + 2 + 2)
                        take_ba()
                    if (n, s) == (1, 2):
                        take_turned()
                    if (n, s) == (2, 0):
                        dve.wait_ge(bank_free, G_QKVZ + 4 + 2)
                        make_gate()
                    if (n, s) == (2, 2):
                        take_sums()
                    if (n, s) == (3, 0):
                        dve.wait_ge(bank_free, G_QKVZ + 6 + 2)
                        scale_beta()
                    if n in (1, 2) and s < 2:
                        conv_taps(n - 1, (2 * s, 2 * s + 1))
                    if n == 2 and s >= 2:
                        l2_norm(s - 2)
                    if n == 3 and s == 0:
                        l2_norm(2)
                        l2_norm(3)
                    if n == 3 and s in (1, 2):
                        if s == 1:
                            dve.wait_ge(sem("l2_normed"), 4)
                        conv_taps(2, (2 * s - 2, 2 * s - 1))
                    if n == 3 and s == 3:
                        l2_norm(4)
            for t in range(5, 8):
                l2_norm(t)

            def t4(ap):
                return ap.rearrange("p (t n) -> p t n", n=128)

            for pair in range(2):
                heads = [(m, 2 * pair + m, 4 * m) for m in range(2)]
                for m, h, b in heads:
                    hs = slice(4 * h, 4 * h + 4)
                    V.tensor_tensor(t4(tmp_a[:, m, :]), bm(ident, 4), bc(g_sums[:, hs], 128), ALU.mult)
                    V.tensor_tensor(t4(tmp_b[:, m, :]), bm(ident, 4), bc(beta[:, hs], 128), ALU.mult)\
                     .then_inc(sem("diags"), 1)
                    dve.wait_ge(sem("kv_turned"), h + 1)
                    if h == 0:
                        dve.wait_ge(sem("l2_normed"), 8)
                    V.tensor_tensor(t4(k_be[:, h, :]), t4(ps[:, b, :]), bc(be[:, hs], 128), ALU.mult)
                    V.tensor_tensor(t4(k_g[:, h, :]), t4(ps[:, b, :]), bc(kgs[:, hs], 128), ALU.mult)
                    V.tensor_tensor(t4(v_b[:, h, :]), t4(ps[:, b + 1, :]), bc(beta[:, hs], 128), ALU.mult)\
                     .then_inc(sem("kv_taken"), 1)
                for m, h, b in heads:
                    hs = slice(4 * h, 4 * h + 4)
                    dve.wait_ge(sem("exp_row"), h + 1)
                    order.link(V.tensor_tensor(t4(tmp_a[:, m, :]), t4(ps[:, b + 2, :]), bc(g_sums[:, hs], 128), ALU.subtract))
                    V.tensor_tensor(t4(tmp_a[:, m, :]), t4(tmp_a[:, m, :]), bm(gdn_c[:, 4, :], 4), ALU.add)\
                     .then_inc(sem("decay_log"), 1)
                    V.tensor_tensor(tmp_b[:, m, :], proj[:, KT_ + h, PAD:], ps[:, b + 3, :], ALU.mult)\
                     .then_inc(sem("kb_ready"), 1)
                for m, h, b in heads:
                    dve.wait_ge(sem("decay_ready"), h + 1)
                    order.link(V.tensor_tensor(t4(inv_t[:, h, :]), t4(tmp_a[:, m, :]), bm(gdn_c[:, 5, :], 4), ALU.mult))
                    dve.wait_ge(sem("kk_done"), h + 1)
                    V.scalar_tensor_tensor(out=pows[:, m, 0, 1, :], in0=ps[:, b + 1, :], scalar=-1.0, in1=inv_t[:, h, :],
                                           op0=ALU.mult, op1=ALU.mult).then_inc(sem("nt_ready"), 1)
                    dve.wait_ge(sem("nt_ready"), h + 1)
                    V.tensor_tensor(t4(inv_t[:, h, :]), t4(pows[:, m, 0, 1, :]), bm(ident, 4), ALU.add)\
                     .then_inc(sem("inv_ready"), 1)
                    V.tensor_tensor(attn_t[:, h, :], ps[:, b, :], tmp_a[:, m, :], ALU.mult).then_inc(sem("attn_ready"), 1)
                    V.tensor_tensor(proj[:, QT + h, PAD:], proj[:, QT + h, PAD:], pows[:, m, 1, 0, :], ALU.mult)\
                     .then_inc(sem("q_scaled"), 1)
                for it in range(5):
                    if it < 4:
                        for m, h, b in heads:
                            dve.wait_ge(sem("nt_squared"), (4 * pair + it) * 2 + m + 1)
                            V.tensor_copy(pows[:, m, 1 - it % 2, 1, :], ps[:, b + 1, :]).then_inc(sem("nt_power"), 1)
                    for m, h, b in heads:
                        dve.wait_ge(sem("inv_step"), (5 * pair + it) * 2 + m + 1)
                        V.tensor_tensor(inv_t[:, h, :], inv_t[:, h, :], ps[:, b + 2, :], ALU.add)\
                         .then_inc(sem("inv_ready"), 1)
                for m, h, b in heads:
                    dve.wait_ge(sem("u_done"), h + 1)
                    V.tensor_copy(u_b[:, h, :], ps[:, b + 1, :]).then_inc(sem("u_ready"), 1)
            dve.wait_ge(sem("inv_step"), 20)
            V.memset(state[:, 0, :], 0.0).then_inc(sem("state_ready"), 1)
            for c in range(8):
                r, tt, half = 64 * (c % 2), c // 2, c % 2
                dve.wait_ge(sem("w_state"), c + 1)
                if tt >= 2:
                    dve.wait_ge(sem("o_done"), 4 * (tt - 1))
                V.tensor_tensor(v_new[r:r + 64, tt % 2, :].rearrange("p (h n) -> p h n", h=4),
                                u_b[r:r + 64, :, 128 * tt:128 * tt + 128],
                                ps[r:r + 64, 0, :].rearrange("p (h n) -> p h n", h=4), ALU.subtract)\
                 .then_inc(sem("v_new_ready"), 1)
                dve.wait_ge(sem("state_ready"), c + 1)
                order.link(V.tensor_tensor(state_g[:, :].rearrange("p (h n) -> p h n", h=4),
                                           state[:, c % N_STATES, :].rearrange("p (h n) -> p h n", h=4),
                                           bc(g_last[:, 16 * half + tt:16 * half + 16:4], 128), ALU.mult))
                dve.wait_ge(sem("state_add"), c + 1)
                if c >= 5:
                    dve.wait_ge(sem("o_done"), 4 * ((c - 5) // 2 + 1))
                V.tensor_tensor(state[:, (c + 1) % N_STATES, :], state_g[:, :], ps[:, 3, :], ALU.add).then_inc(sem("state_ready"), 1)
            dve.wait_ge(sem("z_silu"), 1)
            for h in range(4):
                dve.wait_ge(sem("gdn_root"), h + 1)
                order.link(V.reciprocal(k_g[:, h, :], k_g[:, h, :]))
                order.link(V.scalar_tensor_tensor(out=Y[:, h, :], in0=proj[:, VT + h, PAD:], scalar=par("gdn_norm"),
                                                  in1=k_g[:, h, :], op0=ALU.mult, op1=ALU.mult))
                ins = V.tensor_tensor(Y[:, h, :], Y[:, h, :], proj[:, ZT + h, PAD:], ALU.mult)
            ins.then_inc(sem("mixer_out"), 1)

            with dve.Fori(0, 16) as i:
                dve.wait_ge(h_hi_ready, 48 + i + 1)
                V.tensor_tensor(h_lo[:, i, :], Y[:, i, :], h_hi[:, i, :].bitcast(F32), ALU.subtract).then_inc(h_ready, 1)
            with dve.Fori(0, 4) as i:
                for s in range(4):
                    step_lo(U_WO2 + 4 * i, s)
                    if s % 2:
                        dve.wait_ge(w_used, U_WO2 + 4 * i + s + 1 + 1)
                        V.tensor_copy(y2[:, bass.ds(4 * i + (s - 1), 2), :], ps[:, s - 1:s + 1, :]).then_inc(bank_free, 1)
            one_over_root(4)
            dve.wait_ge(sem("x_back"), 64)
            with dve.Fori(0, 8) as i:
                order.enter(i, 1)
                for s in range(2):
                    t = 2 * i + s
                    ins = V.scalar_tensor_tensor(out=y2[:, t, :], in0=y2[:, t, :], scalar=dpar("post_mix", t),
                                                 in1=rstd[:, :], op0=ALU.mult, op1=ALU.mult)
                order.link(ins)
                for s in range(2):
                    t = 2 * i + s
                    V.tensor_tensor(X[:, t, :], X[:, t, :], y2[:, t, :], ALU.add).then_inc(x_ready, 1)
                low_pair(64, i, "pre_ffn")
                order.leave(8)

            for k in range(4):
                V.memset(credit[:, 4 * k:4 * k + 1], 0.0).then_inc(down_free, 1)
            order.link(V.memset(hid[:, :, 0:2], 0.0))

            def ffn_take(u, s, c):
                dve.wait_ge(w_used, u + s + 1 + 1)
                for j in range(2):
                    ins = V.tensor_tensor(hid[:, j, 2:], ps[:, 2 * c + j, :], rstd[:, :], ALU.mult)
                ins.then_inc(bank_free, 1)

            def ffn_group(seg, b, c, par_):
                dve.wait_ge(bank_free, seg * 4 + (G_FFN + 2 * b + c + 3))
                dst = f_val if c else f_gate
                tile = [seg * 4 + (FFT * c + 2 * b + j) for j in range(2)]
                ins = conv([dst[:, j, :] for j in range(2)], [hid[:, j, :] for j in range(2)],
                           [[dpar("ffn_conv", tile[j] * 3 + k) for k in range(3)] for j in range(2)], 2, None,
                           [dpar("ffn_b", tile[j]) for j in range(2)])
                if c == 0:
                    ins.then_inc(sem("f_gates"), 1)
                    return
                order.link(ins)
                dve.wait_ge(sem("f_gelu"), seg * 2 + (b + 1))
                V.tensor_tensor(f_val[:, :, :], f_gate[:, :, :], f_val[:, :, :], ALU.mult).then_inc(sem("f_gated"), 1)
                dve.wait_ge(sem("f_hi_ready"), seg * 2 + (b + 1))
                V.tensor_tensor(f_lo[:, par_, 2 * b:2 * b + 2, :], f_val[:, :, :],
                                f_hi[:, par_, 2 * b:2 * b + 2, :].bitcast(F32), ALU.subtract).then_inc(f_ready, 1)

            def ffn_up(u, seg, par_, norm=None):
                for s in range(8):
                    step_lo(u, s)
                    if norm is not None and s == 1:
                        one_over_root(norm)
                    if s % 2:
                        ffn_take(u, s, s // 2 % 2)
                    elif s:
                        ffn_group(seg, (s - 1) // 4, (s - 1) // 2 % 2, par_)

            def ffn_down(u, seg, last=False, before=None):
                for q in range(4):
                    if not (last and q == 3):
                        step_lo(u, q)
                    if before is not None and q == 0:
                        ffn_group(before[0], 1, 1, before[1])
                    for j in range(4):
                        if j < 3:
                            dve.wait_ge(down_tile, seg * 12 + (3 * q + j + 1))
                        else:
                            dve.wait_ge(w_used, u + q + 1 + 1)
                        V.tensor_tensor(y_acc[:, 4 * q + j, :], y_acc[:, 4 * q + j, :], ps[:, 4 + j, :],
                                        ALU.add).then_inc(down_free, 1)

            PER_SEG = 2 * (2 + 3)
            ffn_up(U_FFN, 0, 0, norm=5)
            ffn_group(0, 1, 1, 0)
            dve.wait_ge(sem("acc_zeroed"), 1)
            with dve.Fori(0, (SEGS - 1) // 2) as i:
                order.enter(i, 2 * PER_SEG)
                for e in range(2):
                    u = U_FFN + 8 + 12 * e + 24 * i
                    ffn_up(u, 2 * i + (1 + e), 1 - e)
                    ffn_down(u + 8, 2 * i + e, before=(2 * i + (1 + e), 1 - e))
                order.leave((SEGS - 1) // 2)
            ffn_down(N_UNITS - 4, SEGS - 1, last=True)
            one_over_root(6)
            dve.wait_ge(sem("x_back"), 128)
            with dve.Fori(0, 8) as i:
                order.enter(i, 1)
                for s in range(2):
                    t = 2 * i + s
                    ins = V.scalar_tensor_tensor(out=y_acc[:, t, :], in0=y_acc[:, t, :], scalar=dpar("post_ffn", t),
                                                 in1=rstd[:, :], op0=ALU.mult, op1=ALU.mult)
                order.link(ins)
                for s in range(2):
                    t = 2 * i + s
                    V.tensor_tensor(y_acc[:, t, :], y_acc[:, t, :], x_back[:, t, :], ALU.add).then_inc(sem("out_tiles"), 1)
                order.leave(8)


def unit_of(w, t0, nt, cols):
    a = w[t0 * 128:(t0 + nt) * 128, cols].reshape(nt, 128, -1)
    return a.transpose(1, 0, 2).reshape(128, -1)


def group_units(w, c0, groups):
    return [unit_of(w, 8 * half, 8, slice(c0 + 256 * g, c0 + 256 * g + 256)) for g in range(groups) for half in range(2)]


def columns(v):
    return v.reshape(-1, 128).T


def kernel(**inp):
    import concourse.bacc as bacc
    from concourse.bass_utils import run_bass_kernel_spmd

    a = {k: np.ascontiguousarray(v) for k, v in inp.items()}
    units = []
    for l in range(2):
        units += group_units(a["w_in"][l], 0, 8)
        units += [unit_of(a["w_out"][l], 0, 4, slice(512 * q, 512 * q + 512)) for q in range(4)]
    w2 = a["w_in_2"][0]
    units += group_units(w2, 2056, 4) + group_units(w2, 3080, 4) + group_units(w2, 4104, 6) + group_units(w2, 0, 8)
    units += group_units(a["w_out_2"][0], 0, 8)
    up, down = a["ffn_up_2"][0], a["ffn_down_2"][0]

    def ups(s):
        return [u for b in range(2) for c in (0, D_FF) for u in group_units(up, c + 512 * s + 256 * b, 1)]

    def downs(s):
        return [unit_of(down, 4 * s, 4, slice(512 * q, 512 * q + 512)) for q in range(4)]

    units += ups(0)
    for s in range(1, SEGS):
        units += ups(s) + downs(s - 1)
    units += downs(SEGS - 1)
    assert len(units) == N_UNITS
    weights = np.stack(units)

    def taps(w):
        return w.reshape(w.shape[0], -1, 128).transpose(2, 1, 0).reshape(128, -1)

    vals = dict(g0=columns(a["norm_g"][0]), g1=columns(a["norm_g"][1]), final=columns(a["final_norm_g"]),
                pre_mix=columns(a["pre_mix_norm_2"][0]), post_mix=columns(a["post_mix_norm_2"][0]),
                pre_ffn=columns(a["pre_ffn_norm_2"][0]), post_ffn=columns(a["post_ffn_norm_2"][0]),
                gdn_conv=taps(a["gdn_conv_w_2"][0]), gdn_norm=columns(a["gdn_norm_w_2"][0]),
                lru_conv=taps(a["lru_conv_w_2"][0]), lru_b=columns(a["lru_conv_b_2"][0]),
                ba=columns(a["lru_ba_2"][0].reshape(-1)), bx=columns(a["lru_bx_2"][0].reshape(-1)),
                lam=columns(a["lru_lambda_2"][0]), sc_conv=taps(a["sconv_w_2"][0]),
                grp=columns(a["grp_norm_w_2"][0].reshape(-1)),
                subln=columns(np.concatenate([a["diff_subln_g"][0]] * 2)),
                ffn_conv=taps(a["ffn_conv_w_2"][0]), ffn_b=columns(a["ffn_conv_b_2"][0]))
    arrays = {
        "weights": weights,
        "x_in": np.ascontiguousarray(a["x"][0].T.reshape(KT, 128, S).transpose(1, 0, 2)),
        "params": np.ascontiguousarray(np.concatenate([vals[n] for n, _ in PARAM_SIZES], axis=1)),
        "consts": shape_constants(),
        "w_ba": np.ascontiguousarray(unit_of(w2, 0, 16, slice(2048, 2056))),
        "alog_dt": np.concatenate([a["gdn_a_log_2"][0], a["gdn_dt_bias_2"][0]]),
        "lam_rows": a["diff_lam"][0].reshape(-1),
        "sgu_rows": np.stack([a["sgu_ln_w_2"][0], a["sgu_ln_b_2"][0], a["sgu_b_2"][0].reshape(-1)]),
        "sgu_wsT": np.ascontiguousarray(a["sgu_ws_2"][0].transpose(2, 0, 1)),
        "lru_wa": a["lru_wa_2"][0],
        "lru_wx": a["lru_wx_2"][0],
    }
    nc = bacc.Bacc("TRN2", target_bir_lowering=False, num_devices=1)
    args = [nc.dram_tensor(n, v.shape, mybir.dt.from_np(v.dtype), kind="ExternalInput").ap() for n, v in arrays.items()]
    args.append(nc.dram_tensor("out", (128, KT, S), F32, kind="ExternalOutput").ap())
    two_blocks_kernel(nc, *args)
    r = run_bass_kernel_spmd(nc, [arrays], core_ids=[0])
    got = r.results[0]["out"]
    return got.transpose(1, 0, 2).reshape(D, S).T.reshape(1, S, D)
```

```python
from contextlib import ExitStack

import numpy as np

import concourse.bass as bass
from concourse import mybir

F32 = mybir.dt.float32
F32R = mybir.dt.float32r
ALU = mybir.AluOpType
ACT = mybir.ActivationFunctionType
AX = mybir.AxisListType.X

P128 = 128
D = 2048
S = 512
KT = D // P128
UNIT = 2048
NEG = -1.0e30
EPS = 1e-6
HEAD = 64
N_HEADS = 4
PAD = 4
D_FF = (D * 11) // 4
SEGS = D_FF // 512
FFT = D_FF // P128

U_IN = 16
U_OUT = 4
U_UP, U_DOWN = 8, 4
U_L = [0, U_IN + U_OUT]
U_M2 = 2 * (U_IN + U_OUT)
M2_QUADS = dict(lru=2, sgu=2, sc=3, qkvz=4)
U_LRU = U_M2
U_SGU = U_LRU + 4 * M2_QUADS["lru"]
U_SC = U_SGU + 4 * M2_QUADS["sgu"]
U_QKVZ = U_SC + 4 * M2_QUADS["sc"]
U_WO2 = U_QKVZ + 4 * M2_QUADS["qkvz"]
U_FFN = U_WO2 + 16
N_UNITS = U_FFN + SEGS * (U_UP + U_DOWN)
G_L = [0, 8]
G_LRU = 16
G_SGU = G_LRU + 4
G_SC = G_SGU + 4
G_QKVZ = G_SC + 6
G_WO2 = G_QKVZ + 8
G_FFN = G_WO2 + 8

PARAM_SIZES = [("g0", 16), ("g1", 16), ("final", 16), ("pre_mix", 16), ("post_mix", 16), ("pre_ffn", 16),
               ("post_ffn", 16), ("gdn_conv", 48), ("gdn_norm", 1), ("lru_conv", 16), ("lru_b", 4),
               ("ba", 4), ("bx", 4), ("lam", 4), ("sc_conv", 12), ("grp", 12), ("subln", 1),
               ("ffn_conv", 6 * FFT), ("ffn_b", 2 * FFT)]
PARAM = {}
_n = 0
for _name, _size in PARAM_SIZES:
    PARAM[_name] = _n
    _n += _size
N_PARAM = _n

CONST_SIZES = [("ident", 128), ("ones", 128), ("eps", 1), ("one", 1), ("halves", 2), ("quarters", 4),
               ("rot0", 128), ("rot1", 128), ("suffix", 128), ("before01", 128), ("notbefore", 128),
               ("dilated", 512), ("causal", 512), ("cos0", 512), ("sin0", 512), ("cos1", 512), ("sin1", 512),
               ("chunk_tri", 128), ("chunk_all", 128), ("half_a", 128), ("half_b", 128),
               ("decay_mask", 128), ("strict01", 128), ("tri01", 128)]
CONST = {}
_n = 0
for _name, _size in CONST_SIZES:
    CONST[_name] = _n
    _n += _size
N_CONST = _n


def shape_constants():
    c = np.zeros((P128, N_CONST), np.float32)

    def put(name, a):
        c[:, CONST[name]:CONST[name] + a.shape[1]] = a

    p, f = np.arange(128)[:, None], np.arange(128)[None, :]
    same = (p // 64) == (f // 64)
    put("ident", (p == f).astype(np.float32))
    put("ones", np.ones((128, 128), np.float32))
    put("eps", np.full((128, 1), EPS, np.float32))
    put("one", np.ones((128, 1), np.float32))
    put("halves", (p // 64 == np.arange(2)[None, :]).astype(np.float32))
    put("quarters", (p // 32 == np.arange(4)[None, :]).astype(np.float32))
    for n, dim in ((0, 64), (1, 32)):
        half = dim // 2
        rot = np.zeros((128, 128), np.float32)
        for i in range(128):
            if i % dim < half:
                rot[i + half, i] = -1.0
            else:
                rot[i - half, i] = 1.0
        put(f"rot{n}", rot)
        inv = np.float32(10000.0) ** (-np.arange(half, dtype=np.float32) / np.float32(half))
        ang = np.arange(S, dtype=np.float32)[None, :] * inv.astype(np.float32)[np.arange(128) % half][:, None]
        put(f"cos{n}", np.cos(ang).astype(np.float32))
        put(f"sin{n}", np.sin(ang).astype(np.float32))
    put("suffix", (p >= f).astype(np.float32))
    put("before01", (p < f).astype(np.float32))
    put("notbefore", np.where(p < f, 0.0, NEG).astype(np.float32))
    dist = np.concatenate([128 * b + p - f for b in (3, 2, 1, 0)], axis=1)
    put("causal", np.where(dist >= 0, 0.0, NEG).astype(np.float32))
    n = ((dist >= 0) & (dist <= 128)).astype(int) + ((dist >= 0) & (dist % 4 == 0)) + ((dist >= 0) & (dist % 16 == 0))
    put("dilated", np.where(n > 0, np.log(np.maximum(n, 1)) * HEAD ** 0.5, NEG).astype(np.float32))
    put("chunk_tri", (same & (p <= f)).astype(np.float32))
    put("chunk_all", same.astype(np.float32))
    put("half_a", np.broadcast_to(p < 64, (128, 128)).astype(np.float32))
    put("half_b", np.broadcast_to(p >= 64, (128, 128)).astype(np.float32))
    put("decay_mask", np.where(same & (f >= p), 0.0, NEG).astype(np.float32))
    put("strict01", (same & (f > p)).astype(np.float32))
    put("tri01", (f >= p).astype(np.float32))
    return c


class Order:

    def __init__(self, eng, sem):
        self.eng, self.sem, self.n, self.loop = eng, sem, 0, None

    def link(self, ins):
        ins.then_inc(self.sem, 1)
        self.n += 1
        self.eng.wait_ge(self.sem, self.value())

    def value(self):
        if self.loop is None:
            return self.n
        i, start, per, first = self.loop
        return i * per + (self.n - first * per)

    def enter(self, i, per, first=0):
        self.loop = (i, self.n, per, first)

    def leave(self, trips):
        _, start, per, _ = self.loop
        assert self.n - start == per, (self.n - start, per)
        self.n, self.loop = start + trips * per, None


def bc(ap, n):
    return ap.unsqueeze(2).broadcast_to([ap.shape[0], ap.shape[1], n])


def bm(ap, n):
    return ap.unsqueeze(1).broadcast_to([ap.shape[0], n, ap.shape[1]])


def two_blocks_kernel(nc, weights, x_in, params, consts, w_ba, alog_dt, lam_rows, sgu_rows, sgu_wsT,
                      lru_wa, lru_wx, out):
    ctx = ExitStack()
    with ctx:
        sems = {}

        def sem(name):
            if name not in sems:
                sems[name] = ctx.enter_context(nc.semaphore(name))
            return sems[name]

        IN_LAYER_0 = dict(l_scores=32, qk_split=12, qk_hi_ready=12, l_scores_read=32, l_probs=32, neg_max=8, l_turned=8, l_pt_a=8, l_pt_b=8,
                          l_o=8, l_o_read=8, l_y_turned=4, rotated=8, rot_read=8, roped=8, v_turned=4,
                          v_tok_ready=4, gates=2, y1=4, y1_hi_ready=4, y1_ready=4, attn_c_landed=80, rope_c_landed=48, y_taken=0)

        def since(name, l, n):
            return sem(name), n + (IN_LAYER_0[name] if l else 0)

        class Region:
            def __init__(self, at, end):
                self.at, self.end = at, end

            def take(self, name, shape, dt=F32):
                size = int(np.prod(shape[1:])) * 4
                at = self.at
                self.at = (at + size + 31) // 32 * 32
                assert self.at <= self.end, (name, self.at, self.end)
                return nc.alloc_sbuf_tensor_at(name, shape, dt, offset=at)

        BASE, END = 16512, 229344
        top = Region(BASE, END)
        params_sb = top.take("params_sb", [128, N_PARAM])
        head_c = top.take("head_c", [128, 264])
        rstd = top.take("rstd", [128, S])
        root = top.take("root", [128, S])
        credit = top.take("credit", [128, 16])
        squares = top.take("squares", [128, 2, S])
        raw = top.take("raw", [128, 2, UNIT])
        w_hi = top.take("w_hi", [128, 2, UNIT], F32R)
        w_lo = top.take("w_lo", [128, 2, UNIT], F32R)
        X0 = top.at
        X = top.take("X", [128, KT, S])
        H0 = top.at
        h_hi = top.take("h_hi", [128, KT, S], F32R)
        h_lo = top.take("h_lo", [128, KT, S], F32R)
        W0 = top.at
        ident, ones = head_c[:, 0:128], head_c[:, 128:256]
        eps_c, one_c = head_c[:, 256:257], head_c[:, 257:258]
        halves, quarters = head_c[:, 258:260], head_c[:, 260:264]

        wl = Region(W0, END)
        proj = wl.take("proj", [128, 16, PAD + S])
        y1_hi = wl.take("y1_hi", [128, 4, S], F32R)
        y1_lo = wl.take("y1_lo", [128, 4, S], F32R)
        cos_sb = wl.take("cos_sb", [128, S])
        sin_sb = wl.take("sin_sb", [128, S])
        rotation = squares[:, 0, 0:128]
        hl = Region(H0, W0)
        probs = hl.take("probs", [128, 4, 1280])
        probs_t_at = hl.at
        probs_t = hl.take("probs_t", [128, 2, 1280])
        v_tok = hl.take("v_tok", [128, 4, 512])
        o_tok = hl.take("o_tok", [128, 4, 512])
        mask_sb = hl.take("mask_sb", [128, 2, 512])
        rot_sin_at = hl.at
        rot_sin = nc.alloc_sbuf_tensor_at("rot_sin", [128, 2, S], F32, offset=rot_sin_at)
        q_split = hl.take("q_split", [128, 2, 2, S], F32R)
        attn_c = hl.take("attn_c", [128, 4, 128])
        sp_split = nc.alloc_sbuf_tensor_at("sp_split", [128, 2, 1280], F32R, offset=probs_t_at)
        sums_r = nc.alloc_sbuf_tensor_at("sums_r", [128, 2, 128], F32R, offset=rot_sin_at)
        y1 = root
        small = hl.take("small", [128, 512])
        row_max, neg_max, den, rden = (small[:, 32 * k:32 * k + 32] for k in range(4))
        lam_sb = small[:, 128:256]
        lam_s = small[:, 256:264]
        lam_prod = small[:, 264:296]
        o_ss, o_root, o_rstd = (small[:, 320 + 16 * k:336 + 16 * k] for k in range(3))

        Y = nc.alloc_sbuf_tensor_at("Y", [128, 16, S], F32, offset=X0)
        wm = Region(proj_end := (W0 + 16 * (PAD + S) * 4 + 31) // 32 * 32, END)
        gate_a = wm.take("gate_a", [128, 4, 128])
        gate_x = wm.take("gate_x", [128, 4, 128])
        sgu_sb = wm.take("sgu_sb", [128, 3, 512])
        sgu_w = wm.take("sgu_w", [128, 4, 128])
        tri01 = wm.take("tri01", [128, 128])
        lru_s = wm.take("lru_s", [128, 32])
        lru_a2 = wm.take("lru_a2", [128, 2, S])
        stats = wm.take("stats", [128, 4, 16])
        wg = Region(proj_end, END)
        pows = wg.take("pows", [128, 2, 2, 2, 512])
        wscan = Region(proj_end, END)
        N_STATES = 6
        state = wscan.take("state", [128, N_STATES, 512])
        state_g = wscan.take("state_g", [128, 512])
        v_new = wscan.take("v_new", [128, 2, 512])
        wconv = Region(proj_end, END)
        conv_out = wconv.take("conv_out", [128, 8, S])
        hg = Region(H0, W0)
        w_t = hg.take("w_t", [128, 4, 512])
        u_b = hg.take("u_b", [128, 4, 512])
        v_b = hg.take("v_b", [128, 4, 512])
        inv_t = hg.take("inv_t", [128, 4, 512])
        k_g = hg.take("k_g", [128, 4, 512])
        attn_t = hg.take("attn_t", [128, 4, 512])
        k_be = hg.take("k_be", [128, 4, 512])
        tmp_a = hg.take("tmp_a", [128, 2, 512])
        tmp_b = hg.take("tmp_b", [128, 2, 512])
        gs0 = nc.alloc_sbuf_tensor_at("gdn_small", [128, 1024], F32, offset=X0)
        gdn_c = nc.alloc_sbuf_tensor_at("gdn_c", [128, 6, 128], F32, offset=X0 + 4096)
        ba_raw = gs0[:, 0:128]
        ba_tok = gs0[:, 128:160]
        beta, gate, g_tmp, exp_g, be, kgs = (gs0[:, 160 + 16 * k:176 + 16 * k] for k in range(6))
        g_sums = gs0[:, 256:320]
        g_last = gs0[:, 320:352]
        rstd_tok = gs0[:, 352:356]
        alog_sb = gs0[:, 360:368]
        ba_hi = nc.alloc_sbuf_tensor_at("ba_hi", [128, 128], F32R, offset=X0 + 8192 - 1024)
        ba_lo = nc.alloc_sbuf_tensor_at("ba_lo", [128, 128], F32R, offset=X0 + 8192 - 512)
        y2 = nc.alloc_sbuf_tensor_at("y2", [128, 16, S], F32, offset=W0)

        y_acc = nc.alloc_sbuf_tensor_at("y_acc", [128, 16, S], F32, offset=X0)
        wf = Region(W0, END)
        f_hi = wf.take("f_hi", [128, 2, 4, S], F32R)
        f_lo = wf.take("f_lo", [128, 2, 4, S], F32R)
        hid = wf.take("hid", [128, 2, 2 + S])
        f_gate = wf.take("f_gate", [128, 2, S])
        f_val = wf.take("f_val", [128, 2, S])
        x_back = nc.alloc_sbuf_tensor_at("x_back", [128, 16, S], F32, offset=H0)

        ps = ctx.enter_context(nc.psum_tensor("ps", [128, 8, 512], F32))
        SS = 7

        rstd_g = squares[:, 0, :]
        ba_rows = squares[0:8, 1, :]
        lru_xc, lru_r, lru_i, lru_a = Y[:, 8:12, :], Y[:, 12:16, :], Y[:, 0:4, :], Y[:, 4:8, :]
        def head_rows(l, n):
            if l == 0:
                return 8 * (n // 4) + n % 4 // 2, halves[:, n % 2:n % 2 + 1]
            return n // 4, quarters[:, n % 4:n % 4 + 1]

        KEY_TILES = ((2, 3, 10, 11), (2, 3))

        SPLIT_PARTS = ((0, 4, 0), (4, 6, 1), (6, 8, None))

        def l2_root_at(t):
            return squares[:, t - 6, :] if t >= 6 else conv_out[:, t, :]

        Y_ORDER = [*range(8, 16), *range(4, 8), *range(0, 4)]
        Q_T, KEY_T, V_T, Z_T = 8, 0, 4, 12
        sc_sq = conv_out[:, 4:8, :]
        GDN_D = 128

        x_spill = nc.dram_tensor("x_spill", (128, KT, S), F32, kind="Internal").ap()
        x_spill2 = nc.dram_tensor("x_spill2", (128, KT, S), F32, kind="Internal").ap()

        def par(name, at=0, n=1):
            c = PARAM[name]
            return params_sb[:, c + at:c + at + n]

        def dpar(name, at):
            return params_sb[:, bass.ds(at + PARAM[name], 1)]

        raw_landed = [sem("raw_landed_0"), sem("raw_landed_1")]
        w_hi_ready = sem("w_hi_ready")
        w_ready = sem("w_ready")
        w_used = sem("w_used")
        bank_free = sem("bank_free")
        x_ready = sem("x_ready")
        h_hi_ready = sem("h_hi_ready")
        h_ready = sem("h_ready")
        sq_ready = sem("sq_ready")
        sq_used = sem("sq_used")
        root_ready = sem("root_ready")
        rstd_ready = sem("rstd_ready")
        params_landed = sem("params_landed")
        down_free = sem("down_free")
        down_tile = sem("down_tile")
        f_ready = sem("f_ready")
        x_landed = [sem(f"x_landed_{k}") for k in range(4)]
        dve_order, act_order, pool_order = sem("dve_order"), sem("act_order"), sem("pool_order")

        block = ctx.enter_context(nc.Block())

        OUT_BANKS = [4, 5, 6, 3]
        Q_OFF = [0, 128, 384, 768]
        K_OFF = [0, 512, 1024, 896]
        Z_OFF = [0, 512, 896, 1152]

        @block.sync
        def _(sp):
            for k in range(4):
                sp.dma_start(X[:, 4 * k:4 * k + 4, :], x_in[:, 4 * k:4 * k + 4, :]).then_inc(x_landed[k], 16)
                if k in (0, 2):
                    sp.dma_start(raw[:, k // 2, :], weights[k // 2]).then_inc(raw_landed[k // 2], 16)
            with sp.Fori(1, N_UNITS // 2) as i:
                for s in range(2):
                    sp.wait_ge(w_ready, 2 * i + (s + 1))
                    sp.dma_start(raw[:, s, :], weights[2 * i + s]).then_inc(raw_landed[s], 16)
            for k in range(8):
                sp.wait_ge(sem("out_tiles"), 2 * k + 2)
                sp.dma_start(out[:, 2 * k:2 * k + 2, :], y_acc[:, 2 * k:2 * k + 2, :]).then_inc(sem("out_stored"), 16)
            sp.wait_ge(sem("out_stored"), 16 * 8)

        @block.gpsimd
        def _(pool):
            order = Order(pool, pool_order)

            def add_squares(stage, tiles):
                for t in tiles:
                    if t == 0:
                        continue
                    n = 16 * stage + t
                    pool.wait_ge(sq_ready, n + 1)
                    if t == 1:
                        nc.gpsimd.tensor_tensor(root[:, :], squares[:, 0, :], squares[:, 1, :], ALU.add).then_inc(sq_used, 2)
                    else:
                        pool.wait_ge(sq_used, n)
                        nc.gpsimd.tensor_tensor(root[:, :], root[:, :], squares[:, t % 2, :], ALU.add).then_inc(sq_used, 1)

            add_squares(0, range(16))
            for l in range(2):
                for dst, name, n in ((rotation, f"rot{l}", 128), (cos_sb[:, :], f"cos{l}", 512), (sin_sb[:, :], f"sin{l}", 512)):
                    pool.dma_start(dst, consts[:, CONST[name]:CONST[name] + n]).then_inc(sem("rope_c_landed"), 16)
                pool.wait_ge(w_used, U_L[l] + U_IN + 1)
                for dst, name, n in ((mask_sb[:, 0, :], "dilated", 512), (mask_sb[:, 1, :], "causal", 512),
                                     (attn_c[:, 1, :], "suffix", 128),
                                     (attn_c[:, 2, :], "before01", 128), (attn_c[:, 3, :], "notbefore", 128)):
                    pool.dma_start(dst, consts[:, CONST[name]:CONST[name] + n]).then_inc(sem("attn_c_landed"), 16)
                if l == 1:
                    pool.dma_start(lam_sb, lam_rows.partition_broadcast(128)).then_inc(sem("lam_landed"), 16)
                add_squares(l + 1, range(16))
            pool.wait_ge(x_ready, 2 * 16)
            order.link(pool.memset(proj[:, :, 0:PAD], 0.0))
            order.link(pool.memset(gate_a[:, :, :], 0.0))
            pool.memset(gate_x[:, :, :], 0.0).then_inc(sem("pads_ready"), 1)
            pool.wait_ge(sem("pads_ready"), 1)
            for dst, src in ((gate_a, lru_wa), (gate_x, lru_wx)):
                for b in range(2):
                    pool.dma_start(dst[64 * b:64 * b + 64, :, 64 * b:64 * b + 64],
                                   src.rearrange("(t b) i j -> b i t j", b=2)[b]).then_inc(sem("mix_c_landed"), 16)
            for k in range(3):
                pool.dma_start(sgu_sb[:, k, :], sgu_rows[k].partition_broadcast(128)).then_inc(sem("mix_c_landed"), 16)
            pool.dma_start(sgu_w[:, :, :], sgu_wsT).then_inc(sem("mix_c_landed"), 16)
            pool.dma_start(tri01[:, :], consts[:, CONST["tri01"]:CONST["tri01"] + 128]).then_inc(sem("mix_c_landed"), 16)
            add_squares(3, range(16))
            for k in range(4):
                pool.dma_start(x_spill[:, 4 * k:4 * k + 4, :], X[:, 4 * k:4 * k + 4, :]).then_inc(sem("x_spilled"), 16)
            pool.wait_ge(sem("mixer_out"), 1)
            for k, name in enumerate(("chunk_tri", "chunk_all", "half_a", "half_b", "decay_mask", "strict01")):
                pool.dma_start(gdn_c[:, k, :], consts[:, CONST[name]:CONST[name] + 128]).then_inc(sem("mix_c_landed"), 16)
            pool.dma_start(ba_raw, w_ba).then_inc(sem("mix_c_landed"), 16)
            pool.dma_start(alog_sb, alog_dt.partition_broadcast(128)).then_inc(sem("mix_c_landed"), 16)
            pool.wait_ge(h_ready, 64)
            pool.wait_ge(sem("x_spilled"), 64)
            for k in range(4):
                pool.dma_start(X[:, 4 * k:4 * k + 4, :], x_spill[:, 4 * k:4 * k + 4, :]).then_inc(sem("x_back"), 16)
            add_squares(4, range(16))
            add_squares(5, range(16))
            for k in range(4):
                pool.dma_start(x_spill2[:, 4 * k:4 * k + 4, :], X[:, 4 * k:4 * k + 4, :]).then_inc(sem("x_spilled"), 16)
            pool.wait_ge(sem("x_spilled"), 128)
            pool.wait_ge(h_ready, 80)
            pool.wait_ge(sq_ready, 96)
            pool.memset(y_acc[:, :, :], 0.0).then_inc(sem("acc_zeroed"), 1)
            pool.wait_ge(w_used, N_UNITS - U_DOWN - U_DOWN + 1)
            for k in range(4):
                pool.dma_start(x_back[:, 4 * k:4 * k + 4, :], x_spill2[:, 4 * k:4 * k + 4, :]).then_inc(sem("x_back"), 16)
            add_squares(6, range(16))

        @block.tensor
        def _(pe):
            pe.nop().then_inc(w_used, 1)
            pe.wait_ge(params_landed, 32)

            def turn(o, x):
                return pe.transpose(o, x, ident)

            def sum_squares(stage, bank=SS):
                pe.wait_ge(sq_used, 16 * (stage + 1))
                pe.matmul(ps[:, bank, :], ones, root[:, :], start=True, stop=True).then_inc(sem("sq_summed"), 1)

            def project_unit(u0, g0, i, s, h0, opening=False):
                g, half = (s % 2, s // 2) if opening else (s // 2, s % 2)
                pe.wait_ge(w_ready, u0 + 4 * i + s + 3)
                if half == 0:
                    pe.wait_ge(bank_free, g0 + 2 * i + g + 1)
                for k in range(8):
                    t = 8 * half + k
                    pe.wait_ge(h_ready, h0 + t + 1)
                    for j in range(2):
                        w = slice(k * 256 + j * 128, k * 256 + j * 128 + 128)
                        o = ps[:, 2 * g + j, :]
                        pe.matmul(o, w_hi[:, s % 2, w], h_hi[:, t, :], start=(t == 0), stop=False)
                        pe.matmul(o, w_hi[:, s % 2, w], h_lo[:, t, :], start=False, stop=False)
                        mm = pe.matmul(o, w_lo[:, s % 2, w], h_hi[:, t, :], start=False, stop=(t == 15))
                mm.then_inc(w_used, 1)

            def project(u0, g0, quads, h0, norm=None):
                first = 0
                if norm is not None:
                    for s in range(4):
                        project_unit(u0, g0, 0, s, h0, opening=True)
                        if s == 2:
                            sum_squares(norm)
                    first = 1
                with pe.Fori(first, quads) as i:
                    for s in range(4):
                        project_unit(u0, g0, i, s, h0)

            def scores(n, kt):
                pe.wait_ge(*since("qk_split", l, (4, 2)[l] + n + 1))
                for i in range(4):
                    if n >= 1:
                        pe.wait_ge(*since("l_scores_read", l, 4 * (n - 1) + i + 1))
                    o, qs, ks = ps[:, i, 0:128 * (i + 1)], slice(128 * i, 128 * i + 128), slice(0, 128 * (i + 1))
                    pe.matmul(o, q_split[:, n % 2, 0, qs], y1_hi[:, kt, ks], start=True, stop=False)
                    pe.matmul(o, q_split[:, n % 2, 0, qs], y1_lo[:, kt, ks], start=False, stop=False)
                    pe.matmul(o, q_split[:, n % 2, 1, qs], y1_hi[:, kt, ks], start=False, stop=True)\
                      .then_inc(sem("l_scores"), 1)

            def turn_probs(n, buf):
                if n >= 1:
                    pe.wait_ge(*since("l_pt_a", l, n))
                    pe.wait_ge(*since("l_pt_b", l, n))
                for kt in (0, 1, 3, 2):
                    for i in range(kt, 4):
                        at = K_OFF[kt] + 128 * (i - kt)
                        mm = turn(ps[:, 4 + at // 512, at % 512:at % 512 + 128],
                                          probs[:, buf, Q_OFF[i] + 128 * kt:Q_OFF[i] + 128 * kt + 128])
                mm.then_inc(sem("l_turned"), 1)

            def weigh_values(n, h, br):
                pe.wait_ge(*since("l_pt_a", l, n + 1))
                pe.wait_ge(*since("l_pt_b", l, n + 1))
                if n >= 1:
                    pe.wait_ge(*since("l_o_read", l, n))
                for i in range(4):
                    for kt in range(i + 1):
                        at = K_OFF[kt] + 128 * (i - kt)
                        mm = pe.matmul(ps[:, 7, 64 * i:64 * i + 64], probs_t[:, n % 2, at:at + 128],
                                       v_tok[:, kt, 256 * br + 64 * h:256 * br + 64 * h + 64],
                                       start=(kt == 0), stop=(kt == i))
                mm.then_inc(sem("l_o"), 1)

            def turn_outputs(tiles, n_read):
                pe.wait_ge(*since("l_o_read", l, n_read))
                for t in tiles:
                    for i in range(4):
                        mm = turn(ps[:, t, 128 * i:128 * i + 128], o_tok[:, i, 128 * t:128 * t + 128])
                    mm.then_inc(sem("l_y_turned"), 1)

            def stick_scores(h):
                q, k = proj[:, 8 + h // 2, :], proj[:, 10 + h // 2, :]
                r0 = 64 * (h % 2)
                if h >= 1:
                    pe.wait_ge(sem("z_read"), 4 * h)
                for kt in range(4):
                    at = (0, 512, 1024, 1280)[kt]
                    mm = pe.matmul(ps[:, at // 512, at % 512:at % 512 + 512 - 128 * kt],
                                   k[r0:r0 + 64, PAD + 128 * kt:PAD + 128 * kt + 128],
                                   q[r0:r0 + 64, PAD + 128 * kt:PAD + 512], start=True, stop=True)
                mm.then_inc(sem("z_scores"), 1)

            def stick_suffix(h):
                pe.wait_ge(sem("sp_split"), h + 1)
                if h >= 1:
                    pe.wait_ge(sem("tail_read"), 4 * h)
                for kt in range(4):
                    at = (0, 512, 1024, 1280)[kt]
                    n = 512 - 128 * kt
                    for k2 in range(kt, 4):
                        o = at % 512 + 128 * (k2 - kt)
                        for part in range(2):
                            mm = pe.matmul(ps[:, 4 + at // 512, o:at % 512 + n], sums_r[:, 0 if k2 == kt else 1, :],
                                           sp_split[:, part, Z_OFF[k2]:Z_OFF[k2] + 512 - 128 * k2],
                                           start=(k2 == kt and part == 0), stop=(k2 == 3 and part == 1))
                    mm.then_inc(sem("tail"), 1)

            def stick_values(h):
                pe.wait_ge(sem("stick_a"), h + 1)
                a_b = probs[:, 2 * (h % 2), :]
                for kt in range(4):
                    mm = pe.matmul(ps[64 * (h % 2):64 * (h % 2) + 64, 3 if h < 2 else 7, 128 * kt:512],
                                   v_tok[:, kt, 256 + 64 * h:320 + 64 * h],
                                   a_b[:, Z_OFF[kt]:Z_OFF[kt] + 512 - 128 * kt], start=(kt == 0), stop=(kt == 3))
                mm.then_inc(sem("stick_o"), 1)

            def project_out(l):
                for q in range(4):
                    u = U_L[l] + U_IN + q
                    pe.wait_ge(w_ready, u + 3)
                    for j in range(4):
                        if q >= 1:
                            pe.wait_ge(x_ready, 16 * l + 4 * (q - 1) + j + 1)
                        for k in range(4):
                            if q == 0 and j == 0:
                                pe.wait_ge(*since("y1_ready", l, k + 1))
                            w = slice(k * 512 + j * 128, k * 512 + j * 128 + 128)
                            o = ps[:, OUT_BANKS[j], :]
                            pe.matmul(o, w_hi[:, q % 2, w], y1_hi[:, k, :], start=(k == 0), stop=False)
                            pe.matmul(o, w_hi[:, q % 2, w], y1_lo[:, k, :], start=False, stop=False)
                            mm = pe.matmul(o, w_lo[:, q % 2, w], y1_hi[:, k, :], start=False, stop=(k == 3))
                        if j < 3:
                            mm.then_inc(sem("out_tile"), 1)
                        else:
                            mm.then_inc(w_used, 1)

            for l in range(2):
                project(U_L[l], G_L[l], 4, 16 * l, norm=l)
                pe.wait_ge(*since("rope_c_landed", l, 16 * 3))
                pe.wait_ge(bank_free, G_L[l] + 8 + 2)
                for n, t in enumerate([0, 1, 2, 3, 8, 9, 10, 11] if l == 0 else [0, 1, 2, 3]):
                    if n >= 2:
                        pe.wait_ge(*since("rot_read", l, n - 1))
                    pe.matmul(ps[:, n % 2, :], rotation, proj[:, t, PAD:PAD + S], start=True,
                              stop=True).then_inc(sem("rotated"), 1)
                for tt in range(4):
                    for c, t in enumerate((4, 5, 12, 13)):
                        mm = turn(ps[:, 2 + tt, 128 * c:128 * c + 128],
                                          proj[:, t, PAD + 128 * tt:PAD + 128 * tt + 128])
                    mm.then_inc(sem("v_turned"), 1)
                pe.wait_ge(*since("rot_read", l, 8 if l == 0 else 4))
                pe.wait_ge(*since("v_tok_ready", l, 4))
                if l == 0:
                    pe.wait_ge(*since("roped", l, 8))
                    scores(0, 0)
                    for n in range(8):
                        pe.wait_ge(*since("l_probs", l, 4 * (n + 1)))
                        turn_probs(n, n % 4)
                        if n < 7:
                            scores(n + 1, (n + 1) // 2)
                        weigh_values(n, n % 4, n // 4)
                    turn_outputs(range(4), 8)
                else:
                    pe.wait_ge(*since("roped", l, 4))
                    scores(0, 0)
                    scores(1, 0)
                    for n in range(4):
                        if n < 3:
                            scores(2 * n + 2, (n + 1) // 2)
                            scores(2 * n + 3, (n + 1) // 2)
                        pe.wait_ge(sem("diff_probs"), n + 1)
                        turn_probs(n, 2 * (n % 2))
                        weigh_values(n, n, 0)
                    pe.wait_ge(sem("diff_normed"), 1)
                    turn_outputs(range(2), 4)
                    pe.wait_ge(*since("y_taken", l, 2))
                    pe.wait_ge(*since("l_scores_read", l, 32))
                    stick_scores(0)
                    stick_scores(1)
                    for h in range(4):
                        stick_suffix(h)
                        if h < 2:
                            stick_scores(h + 2)
                        stick_values(h)
                project_out(l)

            def group_norm(k, sq):
                pe.wait_ge(sem("group_added"), k + 1)
                pe.matmul(ps[:, SS, :], ones, sq[:, 0, :], start=True, stop=True).then_inc(sem("group_sums"), 1)

            sum_squares(2)
            project(U_LRU, G_LRU, M2_QUADS["lru"], 32, norm=3)
            def lru_gates(gate, first):
                for t in range(4):
                    if first:
                        pe.wait_ge(sem("lru_conved"), t + 1)
                    else:
                        pe.wait_ge(sem("lru_sig"), t + 1)
                    pe.matmul(ps[:, 4 + t, :], gate[:, t, :], lru_xc[:, t, :], start=True,
                              stop=True).then_inc(sem("lru_gates"), 1)

            pe.wait_ge(sem("mix_c_landed"), 16 * 9)
            for n in range(2):
                for s in range(4):
                    project_unit(U_SGU, G_SGU, n, s, 32)
                    if (n, s) == (0, 2):
                        lru_gates(gate_a, True)
                    if (n, s) == (0, 3):
                        lru_gates(gate_x, False)
            for n in range(3):
                for s in range(4):
                    project_unit(U_SC, G_SC, n, s, 32)
                    if (n, s) == (0, 1):
                        pe.wait_ge(sem("lru_sig"), 8)
                        group_norm(0, Y[:, 8:12, :])
                    if (n, s) == (0, 2):
                        pe.wait_ge(sem("sgu_gelu"), 1)
                        pe.wait_ge(sem("group_root"), 1)
                        for tt in range(4):
                            for t in range(4):
                                mm = turn(ps[:, 4 + tt, 128 * t:128 * t + 128],
                                          proj[:, 12 + t, PAD + 128 * tt:PAD + 128 * tt + 128])
                            mm.then_inc(sem("sgu_turned"), 1)
                    if (n, s) == (1, 3):
                        pe.wait_ge(sem("sgu_normed"), 1)
                        for g in range(4):
                            for tt in range(4):
                                mm = pe.matmul(ps[:, 4 + g, 128 * tt:128 * tt + 128], Y[:, 12 + tt, 128 * g:128 * g + 128],
                                               sgu_w[:, g, :], start=True, stop=True)
                            mm.then_inc(sem("sgu_mixed"), 1)
                    if (n, s) == (2, 3):
                        group_norm(1, Y[:, 12:16, :])

            def l2_sums(tiles):
                for t in tiles:
                    pe.wait_ge(sem("l2_sq"), t + 1)
                    if t >= 4:
                        pe.wait_ge(sem("l2_root"), t - 3)
                    pe.matmul(ps[:, 4 + t % 4, :], ones, conv_out[:, t, :], start=True,
                              stop=True).then_inc(sem("l2_sums"), 1)

            def turn_ba():
                pe.wait_ge(sem("ba_rows"), 1)
                for tt in range(4):
                    mm = pe.transpose(ps[:, 5, 8 * tt:8 * tt + 8], ba_rows[:, 128 * tt:128 * tt + 128], ident[0:8, 0:8])
                mm.then_inc(sem("ba_turned"), 1)

            def sum_gates():
                pe.wait_ge(sem("gate_ready"), 1)
                pe.wait_ge(sem("l2_root"), 1)
                for k in range(4):
                    mm = pe.matmul(ps[:, 4, 16 * k:16 * k + 16], gdn_c[:, k, :], gate, start=True, stop=True)
                mm.then_inc(sem("g_summed"), 1)

            for n in range(4):
                for s in range(4):
                    project_unit(U_QKVZ, G_QKVZ, n, s, 32)
                    if (n, s) == (0, 3):
                        pe.wait_ge(sem("ba_split"), 1)
                        for k in range(KT):
                            w = slice(8 * k, 8 * k + 8)
                            o = ps[0:8, 4, :]
                            pe.matmul(o, ba_hi[:, w], h_hi[:, k, :], start=(k == 0), stop=False)
                            pe.matmul(o, ba_hi[:, w], h_lo[:, k, :], start=False, stop=False)
                            mm = pe.matmul(o, ba_lo[:, w], h_hi[:, k, :], start=False, stop=(k == KT - 1))
                        mm.then_inc(sem("ba_done"), 1)
                    if (n, s) == (1, 0):
                        pe.wait_ge(sem("group_root"), 2)
                        group_norm(2, sc_sq)
                    if (n, s) == (1, 1):
                        turn_ba()
                    if (n, s) == (1, 3):
                        pe.wait_ge(sem("ba_tok"), 1)
                        pe.wait_ge(sem("group_root"), 3)
                        l2_sums(range(4))
                    if (n, s) == (2, 1):
                        sum_gates()
                    if (n, s) == (2, 3):
                        pe.wait_ge(sem("g_sums_read"), 1)
                        l2_sums(range(4, 8))
            pe.wait_ge(bank_free, G_WO2 + 2)
            pe.wait_ge(sem("qkv_silu"), 3)

            def per_tile(o, lhs, rhs):
                for tt in range(4):
                    x = slice(128 * tt, 128 * tt + 128)
                    mm = pe.matmul(o[:, x], lhs[:, x], rhs[:, x], start=True, stop=True)
                return mm

            for pair in range(2):
                heads = [(m, 2 * pair + m, 4 * m) for m in range(2)]
                for m, h, b in heads:
                    pe.wait_ge(sem("l2_normed"), 5 + h)
                    if pair:
                        pe.wait_ge(sem("w_t_ready"), h - 1)
                        pe.wait_ge(sem("u_ready"), h - 1)
                    k, v = proj[:, KEY_T + h, PAD:], proj[:, V_T + h, PAD:]
                    for tt in range(4):
                        x = slice(128 * tt, 128 * tt + 128)
                        turn(ps[:, b, x], k[:, x])
                        mm = turn(ps[:, b + 1, x], v[:, x])
                    mm.then_inc(sem("kv_turned"), 1)
                    pe.wait_ge(sem("diags"), h + 1)
                    pe.matmul(ps[:, b + 2, :], ones, tmp_a[:, m, :], start=True, stop=True)
                    pe.matmul(ps[:, b + 3, :], ones, tmp_b[:, m, :], start=True, stop=True).then_inc(sem("rows_spread"), 1)
                for m, h, b in heads:
                    q, k = proj[:, Q_T + h, PAD:], proj[:, KEY_T + h, PAD:]
                    pe.wait_ge(sem("kv_taken"), h + 1)
                    per_tile(ps[:, b, :], k, q)
                    pe.wait_ge(sem("kb_ready"), h + 1)
                    per_tile(ps[:, b + 1, :], k, tmp_b[:, m, :]).then_inc(sem("kk_done"), 1)
                for m, h, b in heads:
                    pe.wait_ge(sem("nt_ready"), h + 1)
                    for tt in range(4):
                        x = slice(128 * tt, 128 * tt + 128)
                        mm = turn(ps[:, b + 2, x], pows[:, m, 0, 1, x])
                    mm.then_inc(sem("n_turned"), 1)
                for it in range(5):
                    v, w = it % 2, 1 - it % 2
                    for m, h, b in heads:
                        if it == 0:
                            pe.wait_ge(sem("n_ready"), h + 1)
                            pe.wait_ge(sem("attn_ready"), h + 1)
                        per_tile(ps[:, b, :], pows[:, m, v, 1, :], pows[:, m, v, 0, :]).then_inc(sem("n_squared"), 1)
                    for m, h, b in heads:
                        pe.wait_ge(sem("n_power"), (5 * pair + it) * 2 + m + 1)
                        if it < 4:
                            for tt in range(4):
                                x = slice(128 * tt, 128 * tt + 128)
                                mm = turn(ps[:, b + 1, x], pows[:, m, w, 0, x])
                            mm.then_inc(sem("nt_squared"), 1)
                    for m, h, b in heads:
                        pe.wait_ge(sem("inv_ready"), (6 * pair + it) * 2 + m + 1)
                        per_tile(ps[:, b + 2, :], pows[:, m, w, 0, :], inv_t[:, h, :]).then_inc(sem("inv_step"), 1)
                        if it < 4:
                            pe.wait_ge(sem("nt_power"), (4 * pair + it) * 2 + m + 1)
                for m, h, b in heads:
                    pe.wait_ge(sem("inv_ready"), (6 * pair + 5) * 2 + m + 1)
                    per_tile(ps[:, b, :], k_be[:, h, :], inv_t[:, h, :]).then_inc(sem("w_t_done"), 1)
                    per_tile(ps[:, b + 1, :], inv_t[:, h, :], v_b[:, h, :]).then_inc(sem("u_done"), 1)
            pe.wait_ge(sem("w_t_ready"), 4)
            pe.wait_ge(sem("u_ready"), 4)
            def scan_output(tt, h):
                if tt >= 2:
                    pe.wait_ge(sem("o_taken"), tt - 1)
                hs = slice(128 * h, 128 * h + 128)
                o = ps[:, 1 + tt % 2, hs]
                pe.matmul(o, v_new[:, tt % 2, hs], attn_t[:, h, 128 * tt:128 * tt + 128], start=True, stop=False)
                for half in range(2):
                    q = PAD + 128 * tt + 64 * half
                    mm = pe.matmul(o[:, 64 * half:64 * half + 64], state[:, (2 * tt + half) % N_STATES, hs],
                                   proj[:, Q_T + h, q:q + 64], start=False, stop=(half == 1))
                mm.then_inc(sem("o_done"), 1)

            for c in range(8):
                r, tt = 64 * (c % 2), c // 2
                x = slice(128 * tt + r, 128 * tt + r + 64)
                rows = slice(r, r + 64)
                done = c // 2 - 1
                pe.wait_ge(sem("state_ready"), c + 1)
                for h in range(4):
                    mm = pe.matmul(ps[rows, 0, 128 * h:128 * h + 128], w_t[:, h, x],
                                   state[:, c % N_STATES, 128 * h:128 * h + 128], start=True, stop=True)
                mm.then_inc(sem("w_state"), 1)
                if done >= 0:
                    scan_output(done, 2 * (c % 2))
                pe.wait_ge(sem("v_new_ready"), c + 1)
                if c < 7:
                    for h in range(4):
                        mm = pe.matmul(ps[:, 3, 128 * h:128 * h + 128], k_g[rows, h, 128 * tt:128 * tt + 128],
                                       v_new[rows, tt % 2, 128 * h:128 * h + 128], start=True, stop=True)
                    mm.then_inc(sem("state_add"), 1)
                if done >= 0:
                    scan_output(done, 2 * (c % 2) + 1)
            for h in range(4):
                scan_output(3, h)
            for h in range(4):
                pe.wait_ge(sem("gdn_sq"), h + 1)
                pe.matmul(ps[:, 4 + h, :], ones, conv_out[:, h, :], start=True, stop=True).then_inc(sem("gdn_sums"), 1)

            def project_y(i):
                for s in range(4):
                    g, half = s // 2, s % 2
                    pe.wait_ge(w_ready, U_WO2 + 4 * i + s + 3)
                    if half == 0:
                        pe.wait_ge(bank_free, G_WO2 + 2 * i + g + 1)
                    for n in range(8 * half, 8 * half + 8):
                        t = Y_ORDER[n]
                        k = t % 8
                        pe.wait_ge(h_ready, 48 + n + 1)
                        for j in range(2):
                            w = slice(k * 256 + j * 128, k * 256 + j * 128 + 128)
                            o = ps[:, 2 * g + j, :]
                            pe.matmul(o, w_hi[:, s % 2, w], h_hi[:, t, :], start=(n == 0), stop=False)
                            pe.matmul(o, w_hi[:, s % 2, w], h_lo[:, t, :], start=False, stop=False)
                            mm = pe.matmul(o, w_lo[:, s % 2, w], h_hi[:, t, :], start=False, stop=(n == 15))
                    mm.then_inc(w_used, 1)

            with pe.Fori(0, 4) as i:
                project_y(i)
            sum_squares(4)
            def ffn_up(u, g, norm=None):
                for s in range(8):
                    opening = norm is not None and s < 4
                    grp, half = (s % 2, s // 2) if opening else (s // 2, s % 2)
                    pe.wait_ge(w_ready, u + s + 3)
                    if half == 0:
                        pe.wait_ge(bank_free, g + grp + 1)
                    for k in range(8):
                        t = 8 * half + k
                        pe.wait_ge(h_ready, 64 + t + 1)
                        for j in range(2):
                            w = slice(k * 256 + j * 128, k * 256 + j * 128 + 128)
                            o = ps[:, 2 * (grp % 2) + j, :]
                            pe.matmul(o, w_hi[:, s % 2, w], h_hi[:, t, :], start=(t == 0), stop=False)
                            pe.matmul(o, w_hi[:, s % 2, w], h_lo[:, t, :], start=False, stop=False)
                            mm = pe.matmul(o, w_lo[:, s % 2, w], h_hi[:, t, :], start=False, stop=(t == 15))
                    mm.then_inc(w_used, 1)
                    if norm is not None and s == 2:
                        sum_squares(norm)

            def ffn_down(u, seg, par_):
                for q in range(4):
                    pe.wait_ge(w_ready, u + q + 3)
                    for j in range(4):
                        pe.wait_ge(down_free, seg * 16 + (4 * q + j + 1))
                        for k in range(4):
                            if q == 0 and j == 0:
                                pe.wait_ge(f_ready, seg * 2 + (k // 2 + 1))
                            w = slice(k * 512 + j * 128, k * 512 + j * 128 + 128)
                            o = ps[:, 4 + j, :]
                            pe.matmul(o, w_hi[:, q % 2, w], f_hi[:, par_, k, :], start=(k == 0), stop=False)
                            pe.matmul(o, w_hi[:, q % 2, w], f_lo[:, par_, k, :], start=False, stop=False)
                            mm = pe.matmul(o, w_lo[:, q % 2, w], f_hi[:, par_, k, :], start=False, stop=(k == 3))
                        mm.then_inc(w_used if j == 3 else down_tile, 1)

            ffn_up(U_FFN, G_FFN, norm=5)
            with pe.Fori(0, (SEGS - 1) // 2) as i:
                for e in range(2):
                    u = U_FFN + 8 + 24 * i + 12 * e
                    ffn_up(u, G_FFN + 4 + 8 * i + 4 * e)
                    ffn_down(u + 8, 2 * i + e, e)
            ffn_down(N_UNITS - 4, SEGS - 1, (SEGS - 1) % 2)
            sum_squares(6, 0)

        @block.scalar
        def _(act):
            order = Order(act, act_order)
            A = nc.scalar.activation

            def step_hi(u0, pairs, s):
                slot = (s + 1) % 2
                act.wait_ge(raw_landed[slot], (pairs + ((s + 1) // 2 + 1)) * 16)
                act.wait_ge(w_used, u0 + s + 1)
                A(w_hi[:, slot, :], raw[:, slot, :], ACT.Copy).then_inc(w_hi_ready, 1)

            def square(n, t_ap):
                if n >= 2:
                    act.wait_ge(sq_used, n - 1)
                A(squares[:, n % 2, :], t_ap, ACT.Square).then_inc(sq_ready, 1)

            def one_over_rms_root(k):
                act.wait_ge(sem("sq_summed"), k + 1)
                if k >= 1:
                    act.wait_ge(rstd_ready, k)
                A(root[:, :], ps[:, SS, :], ACT.Sqrt, bias=eps_c, scale=1.0 / D).then_inc(root_ready, 1)

            def norm_beside(u0, norm, x, split=None):
                for t in range(KT):
                    if split is not None:
                        wait_x(x, t)
                        A(h_hi[:, t, :], X[:, t, :], ACT.Identity, scale=par(split, t)).then_inc(h_hi_ready, 1)
                    if t % 2:
                        square(16 * norm + t // 2, X[:, t // 2, :])
                    if t == 7:
                        step_hi(u0, u0 // 2, 0)
                    if t == 11:
                        step_hi(u0, u0 // 2, 1)
                for t in range(KT // 2, KT):
                    square(16 * norm + t, X[:, t, :])
                step_hi(u0, u0 // 2, 2)
                one_over_rms_root(norm)
                step_hi(u0, u0 // 2, 3)

            def wait_x(x, t):
                if x is None:
                    act.wait_ge(x_landed[t // 4], 16)
                else:
                    act.wait_ge(x_ready, x + t + 1)

            def steps_hi(u0, quads, first=0):
                with act.Fori(first, quads) as i:
                    for s in range(4):
                        step_hi(u0 + 4 * i, u0 // 2 + 2 * i, s)

            act.dma_start(params_sb[:, :], params).then_inc(params_landed, 16)
            act.dma_start(head_c[:, :], consts[:, 0:264]).then_inc(params_landed, 16)
            act.wait_ge(params_landed, 32)
            act.wait_ge(raw_landed[0], 16)
            A(w_hi[:, 0, :], raw[:, 0, :], ACT.Copy).then_inc(w_hi_ready, 1)
            norm_beside(0, 0, None, "g0")
            for l in range(2):
                if l == 1:
                    for s in range(4):
                        step_hi(U_L[l], U_L[l] // 2, s)
                        if s == 2:
                            one_over_rms_root(l)
                steps_hi(U_L[l], 4, first=1)
                for tt in range(4):
                    act.wait_ge(*since("v_turned", l, tt + 1))
                    A(v_tok[:, tt, :], ps[:, 2 + tt, :], ACT.Copy).then_inc(sem("v_tok_ready"), 1)
                act.wait_ge(bank_free, G_L[l] + 8 + 2)
                for t in (6, 14):
                    A(proj[:, t:t + 2, PAD:], proj[:, t:t + 2, PAD:], ACT.Silu).then_inc(sem("gates"), 1)

                act.wait_ge(*since("roped", l, (8, 4)[l]))
                for n, t in enumerate(KEY_TILES[l]):
                    A(y1_hi[:, n, :], proj[:, t, PAD:], ACT.Copy).then_inc(sem("qk_hi_ready"), 1)

                def round_q(n):
                    t, rows = head_rows(l, n)
                    if n >= 2:
                        act.wait_ge(*since("l_scores", l, 4 * (n - 2) + 4))
                    A(q_split[:, n % 2, 0, :], proj[:, t, PAD:], ACT.Identity, scale=rows).then_inc(sem("qk_hi_ready"), 1)

                round_q(0)
                round_q(1)

                def exps(n, buf):
                    act.wait_ge(*since("neg_max", l, n + 1))
                    for i in range(4):
                        b = probs[:, buf, Q_OFF[i]:Q_OFF[i] + 128 * (i + 1)]
                        A(b, b, ACT.Exp, bias=neg_max[:, 4 * n + i:4 * n + i + 1],
                          accum_out=den[:, 4 * n + i:4 * n + i + 1]).then_inc(sem("l_probs"), 1)

                def take_pt_a(n):
                    act.wait_ge(*since("l_turned", l, n + 1))
                    if n >= 2:
                        act.wait_ge(*since("l_o", l, n - 1))
                    A(probs_t[:, n % 2, 0:512], ps[:, 4, :], ACT.Copy).then_inc(sem("l_pt_a"), 1)

                if l == 0:
                    exps(0, 0)
                    for n in range(8):
                        if n < 6:
                            round_q(n + 2)
                        take_pt_a(n)
                        if n < 7:
                            exps(n + 1, (n + 1) % 4)
                else:
                    act.wait_ge(sem("lam_sums"), 2)
                    A(lam_s[:, 2:4], lam_s[:, 0:2], ACT.Exp).then_inc(sem("lam_exp"), 1)
                    exps(0, 0)
                    exps(1, 1)
                    for n in range(4):
                        if n < 3:
                            round_q(2 * n + 2)
                            round_q(2 * n + 3)
                            exps(2 * n + 2, (2 * n + 2) % 4)
                        take_pt_a(n)
                        if n < 3:
                            exps(2 * n + 3, (2 * n + 3) % 4)
                    act.wait_ge(sem("diff_ss"), 1)
                    A(o_root, o_ss, ACT.Sqrt, bias=eps_c, scale=1.0 / HEAD).then_inc(sem("diff_root"), 1)

                def round_y(k):
                    act.wait_ge(*since("y1", l, k + 1))
                    A(y1_hi[:, k, :], y1[:, :], ACT.Copy).then_inc(sem("y1_hi_ready"), 1)

                if l == 1:
                    round_y(0)
                    round_y(1)

                    def stick_z(h):
                        z, L = probs[:, 2 * (h % 2), :], probs[:, 2 * (h % 2) + 1, :]
                        act.wait_ge(sem("z_scores"), h + 1)
                        if h >= 2:
                            act.wait_ge(sem("stick_o"), h - 1)
                        for kt in range(4):
                            at = (0, 512, 1024, 1280)[kt]
                            n = 512 - 128 * kt
                            A(z[:, Z_OFF[kt]:Z_OFF[kt] + n], ps[:, at // 512, at % 512:at % 512 + n], ACT.Copy,
                              scale=HEAD ** -0.5).then_inc(sem("z_read"), 1)
                        act.wait_ge(sem("z_read"), 4 * h + 4)
                        order.link(A(L, z, ACT.Abs))
                        order.link(A(L, L, ACT.Exp, scale=-1.0))
                        A(L, L, ACT.Ln, bias=one_c).then_inc(sem("log1p"), 1)

                    def stick_exp(h):
                        z = probs[:, 2 * (h % 2), :]
                        act.wait_ge(sem("log_a"), h + 1)
                        A(z, z, ACT.Exp).then_inc(sem("stick_a"), 1)

                    def round_sp(h):
                        act.wait_ge(sem("sp_ready"), h + 1)
                        if h >= 1:
                            act.wait_ge(sem("tail"), 4 * h)
                        A(sp_split[:, 0, :], probs[:, 2 * (h % 2) + 1, :], ACT.Copy).then_inc(sem("sp_hi_ready"), 1)

                    act.wait_ge(*since("roped", l, 4))
                    act.wait_ge(*since("attn_c_landed", l, 16 * 5))
                    A(sums_r[:, 0, :], attn_c[:, 1, :], ACT.Copy)
                    A(sums_r[:, 1, :], ones, ACT.Copy)
                    stick_z(0)
                    round_sp(0)
                    for h in range(4):
                        if h < 3:
                            stick_z(h + 1)
                        stick_exp(h)
                        if h < 3:
                            round_sp(h + 1)
                    round_y(2)
                    round_y(3)
                else:
                    for k in range(4):
                        round_y(k)
                for q in range(4):
                    step_hi(U_L[l] + U_IN, (U_L[l] + U_IN) // 2, q)
                    for j in range(4):
                        t = 4 * q + j
                        act.wait_ge(x_ready, 16 * l + t + 1)
                        if l == 0:
                            A(h_hi[:, t, :], X[:, t, :], ACT.Identity, scale=par("g1", t)).then_inc(h_hi_ready, 1)
                        square(16 * (l + 1) + t, X[:, t, :])
                if l == 1:
                    one_over_rms_root(2)

            def group_squares(k, y, sq):
                act.wait_ge(sem("mixer_out"), k + 1)
                for t in range(4):
                    A(sq[:, t, :], y[:, t, :], ACT.Square).then_inc(sem("group_sq"), 1)

            def group_root(k):
                if k >= 1:
                    act.wait_ge(sem("group_normed"), k)
                act.wait_ge(sem("group_sums"), k + 1)
                A(root[:, :], ps[:, SS, :], ACT.Sqrt, bias=eps_c, scale=1.0 / 512).then_inc(sem("group_root"), 1)

            order.link(A(lru_s[:, 0:4], par("lam", 0, 4), ACT.Abs))
            order.link(A(lru_s[:, 0:4], lru_s[:, 0:4], ACT.Exp, scale=-1.0))
            A(lru_s[:, 4:8], lru_s[:, 0:4], ACT.Ln, bias=one_c).then_inc(sem("lam_log"), 1)
            norm_beside(U_LRU, 3, 32, "pre_mix")
            steps_hi(U_LRU, M2_QUADS["lru"], first=1)
            for n in range(2):
                for s in range(4):
                    step_hi(U_SGU + 4 * n, U_SGU // 2 + 2 * n, s)
                    if (n, s) == (0, 3):
                        for t in range(4):
                            act.wait_ge(sem("lru_gates"), t + 1)
                            A(lru_r[:, t, :], ps[:, 4 + t, :], ACT.Sigmoid, bias=par("ba", t)).then_inc(sem("lru_sig"), 1)
                    if (n, s) == (1, 0):
                        for t in range(4):
                            act.wait_ge(sem("lru_gates"), 4 + t + 1)
                            A(lru_i[:, t, :], ps[:, 4 + t, :], ACT.Sigmoid, bias=par("bx", t)).then_inc(sem("lru_sig"), 1)
                        act.wait_ge(sem("lru_rate"), 1)
                        act.wait_ge(sem("lru_sig"), 8)
                        for t in range(4):
                            A(lru_a[:, t, :], lru_r[:, t, :], ACT.Exp, scale=lru_s[:, 8 + t:9 + t]).then_inc(sem("lru_a"), 1)
                        for t in range(4):
                            A(lru_r[:, t, :], lru_r[:, t, :], ACT.Tanh, scale=lru_s[:, 8 + t:9 + t]).then_inc(sem("lru_tanh"), 1)
                    if (n, s) == (1, 1):
                        A(proj[:, 4:8, PAD:], proj[:, 4:8, PAD:], ACT.Gelu_apprx_tanh).then_inc(sem("lru_gelu"), 1)
                    if (n, s) == (1, 2):
                        act.wait_ge(sem("lru_m"), 1)
                        A(lru_r, lru_r, ACT.Sqrt, scale=-1.0).then_inc(sem("lru_mult"), 1)
            for n in range(3):
                for s in range(4):
                    step_hi(U_SC + 4 * n, U_SC // 2 + 2 * n, s)
                    if (n, s) == (0, 0):
                        group_squares(0, Y[:, 4:8, :], Y[:, 8:12, :])
                        act.wait_ge(bank_free, G_SC + 2)
                        A(proj[:, 12:16, PAD:], proj[:, 12:16, PAD:], ACT.Gelu_apprx_tanh).then_inc(sem("sgu_gelu"), 1)
                    if (n, s) == (0, 2):
                        group_root(0)
                        A(proj[:, 8:12, PAD:], proj[:, 8:12, PAD:], ACT.Gelu_apprx_tanh).then_inc(sem("sgu_gelu"), 1)
                    if (n, s) == (1, 1):
                        act.wait_ge(sem("sgu_stats"), 1)
                        A(stats[:, :, 8:9], stats[:, :, 7:8], ACT.Sqrt, bias=eps_c).then_inc(sem("sgu_root"), 1)
                    if (n, s) == (2, 0):
                        act.wait_ge(sem("mix_c_landed"), 16 * 17)
                        A(ba_hi[:, :], ba_raw, ACT.Copy).then_inc(sem("ba_hi_ready"), 1)
                    if (n, s) == (2, 2):
                        group_squares(1, Y[:, 8:12, :], Y[:, 12:16, :])

            def silu_conv(n):
                act.wait_ge(sem("qkv_conved"), n + 1)
                c0 = 4 * (n % 2)
                A(proj[:, (Q_T, KEY_T, V_T)[n]:(Q_T, KEY_T, V_T)[n] + 4, PAD:], conv_out[:, c0:c0 + 4, :], ACT.Silu).then_inc(sem("qkv_silu"), 1)

            def l2_squares(n):
                act.wait_ge(sem("qkv_silu"), n + 1)
                for t in range(4 * n, 4 * n + 4):
                    A(conv_out[:, t, :], proj[:, (Q_T, KEY_T)[n] + t % 4, PAD:], ACT.Square).then_inc(sem("l2_sq"), 1)

            def l2_roots(n):
                for t in range(4 * n, 4 * n + 4):
                    act.wait_ge(sem("l2_sums"), t + 1)
                    A(l2_root_at(t), ps[:, 4 + t % 4, :], ACT.Sqrt, bias=eps_c).then_inc(sem("l2_root"), 1)

            def gates():
                act.wait_ge(sem("ba_tok"), 1)
                A(beta.rearrange("p (h t) -> p t h", h=4), ba_tok.rearrange("p (t c) -> p t c", c=8)[:, :, 0:4],
                  ACT.Sigmoid)
                act.wait_ge(sem("a_dt"), 1)
                A(alog_sb[:, 0:4], alog_sb[:, 0:4], ACT.Exp)
                order.link(A(exp_g, g_tmp, ACT.Abs))
                order.link(A(exp_g, exp_g, ACT.Exp, scale=-1.0))
                A(exp_g, exp_g, ACT.Ln, bias=one_c).then_inc(sem("a_log1p"), 1)

            def decays():
                act.wait_ge(sem("g_sums_read"), 1)
                A(exp_g, g_sums[:, 0:16], ACT.Exp).then_inc(sem("exp_g_ready"), 1)
                A(g_last, g_sums[:, 32:64], ACT.Exp).then_inc(sem("exp_g_ready"), 1)
                act.wait_ge(sem("kgs_log"), 1)
                A(kgs, kgs, ACT.Exp).then_inc(sem("exp_g_ready"), 1)

            for n in range(4):
                for s in range(4):
                    step_hi(U_QKVZ + 4 * n, U_QKVZ // 2 + 2 * n, s)
                    if (n, s) == (0, 0):
                        group_root(1)
                    if (n, s) == (0, 3):
                        group_squares(2, Y[:, 12:16, :], sc_sq)
                    if (n, s) == (1, 1):
                        group_root(2)
                    if n in (1, 2) and s == 2:
                        silu_conv(n - 1)
                    if n in (1, 2) and s == 3:
                        l2_squares(n - 1)
                    if n == 1 and s == 3:
                        gates()
                    if n in (2, 3) and s == 0:
                        if n == 3:
                            act.wait_ge(sem("group_normed"), 3)
                        l2_roots(n - 2)
                    if n == 2 and s == 3:
                        decays()
            silu_conv(2)
            act.wait_ge(bank_free, G_WO2 + 2)
            A(proj[:, Z_T:Z_T + 4, PAD:], proj[:, Z_T:Z_T + 4, PAD:], ACT.Silu).then_inc(sem("z_silu"), 1)
            for pair in range(2):
                heads = [(m, 2 * pair + m, 4 * m) for m in range(2)]
                for m, h, b in heads:
                    act.wait_ge(sem("rows_spread"), h + 1)
                    if pair:
                        act.wait_ge(sem("inv_step"), 2 * 5 * pair)
                    A(pows[:, m, 1, 0, :], ps[:, b + 2, :], ACT.Exp).then_inc(sem("exp_row"), 1)
                    act.wait_ge(sem("decay_log"), h + 1)
                    A(tmp_a[:, m, :], tmp_a[:, m, :], ACT.Exp).then_inc(sem("decay_ready"), 1)
                for m, h, b in heads:
                    act.wait_ge(sem("n_turned"), h + 1)
                    A(pows[:, m, 0, 0, :], ps[:, b + 2, :], ACT.Copy).then_inc(sem("n_ready"), 1)
                for it in range(5):
                    for m, h, b in heads:
                        n = (5 * pair + it) * 2 + m
                        act.wait_ge(sem("n_squared"), n + 1)
                        if it == 0:
                            act.wait_ge(sem("q_scaled"), h + 1)
                        A(pows[:, m, 1 - it % 2, 0, :], ps[:, b, :], ACT.Copy).then_inc(sem("n_power"), 1)
                for m, h, b in heads:
                    act.wait_ge(sem("w_t_done"), h + 1)
                    A(w_t[:, h, :], ps[:, b, :], ACT.Copy).then_inc(sem("w_t_ready"), 1)
            def round_y2(tiles):
                for t in tiles:
                    A(h_hi[:, t, :], Y[:, t, :], ACT.Copy).then_inc(h_hi_ready, 1)

            act.wait_ge(sem("u_done"), 4)
            act.wait_ge(sem("group_normed"), 3)
            round_y2(range(8, 16))
            for tt in range(4):
                act.wait_ge(sem("o_done"), 4 * tt + 4)
                A(proj[:, V_T:V_T + 4, PAD + 128 * tt:PAD + 128 * tt + 128], ps[:, 1 + tt % 2, :].rearrange("p (h n) -> p h n", h=4),
                  ACT.Copy).then_inc(sem("o_taken"), 1)
            act.wait_ge(sem("o_taken"), 4)
            for h in range(4):
                A(conv_out[:, h, :], proj[:, V_T + h, PAD:], ACT.Square).then_inc(sem("gdn_sq"), 1)
            act.wait_ge(sem("v_new_ready"), 8)
            round_y2(range(4, 8))
            step_hi(U_WO2, U_WO2 // 2, 0)
            for h in range(4):
                act.wait_ge(sem("gdn_sums"), h + 1)
                A(conv_out[:, 4 + h, :], ps[:, 4 + h, :], ACT.Sqrt, bias=eps_c, scale=1.0 / GDN_D).then_inc(sem("gdn_root"), 1)

            for t in range(4):
                act.wait_ge(sem("mixer_out"), 4 + t)
                round_y2([t])
            for g in range(8):
                for s in range(2):
                    if (g, s) != (0, 0):
                        step_hi(U_WO2 + 2 * g, U_WO2 // 2 + g, s)
                act.wait_ge(bank_free, G_WO2 + g + 3)
                for t in (2 * g, 2 * g + 1):
                    square(64 + t, y2[:, t, :])
            one_over_rms_root(4)

            def ffn_up(u, pairs, seg, par_, done=0):
                for s in range(done, 8):
                    step_hi(u, pairs, s)
                    b = s // 5
                    if s in (2, 6):
                        act.wait_ge(sem("f_gates"), seg * 2 + (b + 1))
                        A(f_gate[:, :, :], f_gate[:, :, :], ACT.Gelu_apprx_tanh).then_inc(sem("f_gelu"), 1)
                    if s == 4:
                        round_values(seg, b, par_)

            def round_values(seg, b, par_):
                act.wait_ge(sem("f_gated"), seg * 2 + (b + 1))
                A(f_hi[:, par_, 2 * b:2 * b + 2, :], f_val[:, :, :], ACT.Copy).then_inc(sem("f_hi_ready"), 1)

            def ffn_down(u, pairs, seg, par_):
                for q in range(4):
                    step_hi(u, pairs, q)
                    if q == 1:
                        round_values(seg, 1, par_)

            norm_beside(U_FFN, 5, 48, "pre_ffn")
            act.wait_ge(sem("f_gates"), 1)
            A(f_gate[:, :, :], f_gate[:, :, :], ACT.Gelu_apprx_tanh).then_inc(sem("f_gelu"), 1)
            ffn_up(U_FFN, U_FFN // 2, 0, 0, done=4)
            round_values(0, 1, 0)
            with act.Fori(0, (SEGS - 1) // 2) as i:
                for e in range(2):
                    off = 8 + 12 * e
                    ffn_up(U_FFN + off + 24 * i, (U_FFN + off) // 2 + 12 * i, 2 * i + (1 + e), 1 - e)
                    ffn_down(U_FFN + off + 8 + 24 * i, (U_FFN + off + 8) // 2 + 12 * i, 2 * i + (1 + e), 1 - e)
            for q in range(4):
                if q < 3:
                    step_hi(N_UNITS - 4, (N_UNITS - 4) // 2, q)
                for j in range(4):
                    n = 4 * q + j
                    act.wait_ge(down_free, 4 + 16 * (SEGS - 1) + n + 1)
                    square(96 + n, y_acc[:, n, :])
            act.wait_ge(sem("sq_summed"), 7)
            act.wait_ge(rstd_ready, 6)
            A(root[:, :], ps[:, 0, :], ACT.Sqrt, bias=eps_c, scale=1.0 / D).then_inc(root_ready, 1)

        @block.vector
        def _(dve):
            order = Order(dve, dve_order)
            V = nc.vector

            def step_lo(u0, s):
                slot = (s + 1) % 2
                dve.wait_ge(w_hi_ready, u0 + s + 2)
                V.tensor_tensor(w_lo[:, slot, :], raw[:, slot, :], w_hi[:, slot, :].bitcast(F32),
                                ALU.subtract).then_inc(w_ready, 1)

            def low_part(n, t, g):
                dve.wait_ge(h_hi_ready, n + 1)
                V.scalar_tensor_tensor(out=h_lo[:, t, :], in0=X[:, t, :], scalar=g,
                                       in1=h_hi[:, t, :].bitcast(F32), op0=ALU.mult,
                                       op1=ALU.subtract).then_inc(h_ready, 1)

            def one_over_root(k):
                dve.wait_ge(root_ready, k + 1)
                V.reciprocal(rstd[:, :], root[:, :]).then_inc(rstd_ready, 1)
                dve.wait_ge(rstd_ready, k + 1)

            def project(u0, quads, tile0, norm=None):
                def take(i, s, bank):
                    dve.wait_ge(w_used, u0 + 4 * i + s + 1 + 1)
                    for j in range(2):
                        ins = V.tensor_tensor(proj[:, 4 * i + (tile0 + bank + j), PAD:PAD + S],
                                              ps[:, bank + j, :], rstd[:, :], ALU.mult)
                    ins.then_inc(bank_free, 1)

                first = 0
                if norm is not None:
                    step_lo(u0, 2)
                    one_over_root(norm)
                    take(0, 2, 0)
                    step_lo(u0, 3)
                    take(0, 3, 2)
                    first = 1
                with dve.Fori(first, quads) as i:
                    for s in range(4):
                        step_lo(u0 + 4 * i, s)
                        if s % 2:
                            take(i, s, s - 1)

            V.memset(credit[:, 0:1], 0.0).then_inc(bank_free, 1)
            V.memset(credit[:, 1:2], 0.0).then_inc(bank_free, 1)
            V.memset(credit[:, 4:5], 0.0).then_inc(w_ready, 1)
            V.memset(credit[:, 5:6], 0.0).then_inc(w_ready, 1)
            dve.wait_ge(params_landed, 32)
            dve.wait_ge(w_hi_ready, 1)
            V.tensor_tensor(w_lo[:, 0, :], raw[:, 0, :], w_hi[:, 0, :].bitcast(F32),
                            ALU.subtract).then_inc(w_ready, 1)
            for t in range(KT):
                low_part(t, t, par("g0", t))
                if t in (7, 11):
                    step_lo(0, t // 4 - 1)
            for l in range(2):
                project(U_L[l], 4, 0, norm=l)
                dve.wait_ge(bank_free, G_L[l] + 8 + 2)
                dve.wait_ge(*since("rope_c_landed", l, 16 * 3))
                for n, t in enumerate([0, 1, 2, 3, 8, 9, 10, 11] if l == 0 else [0, 1, 2, 3]):
                    tile = proj[:, t, PAD:PAD + S]
                    dve.wait_ge(*since("rotated", l, n + 1))
                    V.tensor_tensor(rot_sin[:, n % 2, :], ps[:, n % 2, :], sin_sb[:, :], ALU.mult)\
                     .then_inc(sem("rot_read"), 1)
                    order.link(V.tensor_tensor(tile, tile, cos_sb[:, :], ALU.mult))
                    dve.wait_ge(*since("rot_read", l, n + 1))
                    V.tensor_tensor(tile, tile, rot_sin[:, n % 2, :], ALU.add).then_inc(sem("roped"), 1)

                dve.wait_ge(*since("attn_c_landed", l, 16 * 5))

                def mask_scores(n, buf, mask, scale, free=None):
                    if free is not None:
                        dve.wait_ge(*free)
                    for i in range(4):
                        dve.wait_ge(*since("l_scores", l, 4 * n + i + 1))
                        V.tensor_tensor_reduce(
                            out=probs[:, buf, Q_OFF[i]:Q_OFF[i] + 128 * (i + 1)], in0=ps[:, i, 0:128 * (i + 1)],
                            in1=mask_sb[:, mask, 128 * (3 - i):512], scale=scale, scalar=-3.0e38, op0=ALU.add,
                            op1=ALU.max, accum_out=row_max[:, 4 * n + i:4 * n + i + 1])\
                         .then_inc(sem("l_scores_read"), 1)
                    dve.wait_ge(*since("l_scores_read", l, 4 * n + 4))
                    V.tensor_scalar(neg_max[:, 4 * n:4 * n + 4], row_max[:, 4 * n:4 * n + 4], -1.0, None,
                                    ALU.mult).then_inc(sem("neg_max"), 1)

                def low_q(n):
                    t, rows = head_rows(l, n)
                    dve.wait_ge(*since("qk_hi_ready", l, (4, 2)[l] + n + 1))
                    V.scalar_tensor_tensor(out=q_split[:, n % 2, 1, :], in0=proj[:, t, PAD:], scalar=rows,
                                           in1=q_split[:, n % 2, 0, :].bitcast(F32), op0=ALU.mult,
                                           op1=ALU.subtract).then_inc(sem("qk_split"), 1)

                for n, t in enumerate(KEY_TILES[l]):
                    dve.wait_ge(*since("qk_hi_ready", l, n + 1))
                    V.tensor_tensor(y1_lo[:, n, :], proj[:, t, PAD:], y1_hi[:, n, :].bitcast(F32),
                                    ALU.subtract).then_inc(sem("qk_split"), 1)
                low_q(0)
                low_q(1)

                def take_pt_b(n):
                    dve.wait_ge(*since("l_turned", l, n + 1))
                    if n >= 2:
                        dve.wait_ge(*since("l_o", l, n - 1))
                    V.tensor_copy(probs_t[:, n % 2, 512:1280],
                                  ps[:, 5:7, :].rearrange("p b n -> p (b n)")[:, 0:768])\
                     .then_inc(sem("l_pt_b"), 1)

                def finish_y(k, src, gate_t, scale=None):
                    if k >= 1:
                        dve.wait_ge(*since("y1_ready", l, k))
                    if scale is None:
                        V.tensor_tensor(y1[:, :], src, proj[:, gate_t, PAD:], ALU.mult).then_inc(sem("y1"), 1)
                    else:
                        V.scalar_tensor_tensor(out=y1[:, :], in0=src, scalar=scale, in1=proj[:, gate_t, PAD:],
                                               op0=ALU.mult, op1=ALU.mult).then_inc(sem("y1"), 1)
                    dve.wait_ge(*since("y1_hi_ready", l, k + 1))
                    V.tensor_tensor(y1_lo[:, k, :], y1[:, :], y1_hi[:, k, :].bitcast(F32),
                                    ALU.subtract).then_inc(sem("y1_ready"), 1)

                def wait_gates():
                    dve.wait_ge(*since("gates", l, 2))

                if l == 0:
                    mask_scores(0, 0, 0, HEAD ** -0.5)
                    for n in range(8):
                        dve.wait_ge(*since("l_probs", l, 4 * n + 4))
                        order.link(V.reciprocal(rden[:, 4 * n:4 * n + 4], den[:, 4 * n:4 * n + 4]))
                        if n < 6:
                            low_q(n + 2)
                        take_pt_b(n)
                        if n < 7:
                            mask_scores(n + 1, (n + 1) % 4, (n + 1) // 4, HEAD ** -0.5,
                                        since("l_turned", l, n - 2) if n >= 3 else None)
                        dve.wait_ge(*since("l_o", l, n + 1))
                        V.tensor_tensor(o_tok[:, :, 64 * n:64 * n + 64],
                                        ps[:, 7, 0:256].rearrange("p (i d) -> p i d", d=64),
                                        bc(rden[:, 4 * n:4 * n + 4], 64), ALU.mult)\
                         .then_inc(sem("l_o_read"), 1)
                    wait_gates()
                    for k in range(4):
                        dve.wait_ge(*since("l_y_turned", l, k + 1))
                        finish_y(k, ps[:, k, :], (6, 7, 14, 15)[k])
                else:
                    lambda_init = 0.8 - 0.6 * float(np.exp(-0.3))
                    dve.wait_ge(sem("lam_landed"), 16)
                    for k in range(2):
                        V.tensor_tensor_reduce(out=lam_prod, in0=lam_sb[:, 64 * k:64 * k + 32],
                                               in1=lam_sb[:, 64 * k + 32:64 * k + 64], scale=1.0, scalar=0.0,
                                               op0=ALU.mult, op1=ALU.add, accum_out=lam_s[:, k:k + 1])\
                         .then_inc(sem("lam_sums"), 1)
                        dve.wait_ge(sem("lam_sums"), k + 1)
                    dve.wait_ge(sem("lam_exp"), 1)
                    order.link(V.tensor_tensor(lam_s[:, 4:5], lam_s[:, 3:4], lam_s[:, 2:3], ALU.subtract))
                    order.link(V.tensor_scalar(lam_s[:, 5:6], lam_s[:, 4:5], -lambda_init, None, ALU.add))
                    mask_scores(0, 0, 1, 32 ** -0.5)
                    mask_scores(1, 1, 1, 32 ** -0.5)
                    def combine(n):
                        dve.wait_ge(*since("l_probs", l, 8 * n + 8))
                        order.link(V.reciprocal(rden[:, 8 * n:8 * n + 8], den[:, 8 * n:8 * n + 8]))
                        order.link(V.tensor_scalar(rden[:, 8 * n + 4:8 * n + 8], rden[:, 8 * n + 4:8 * n + 8],
                                                   lam_s[:, 5:6], None, ALU.mult))
                        b0 = 2 * (n % 2)
                        for i in range(4):
                            b = slice(Q_OFF[i], Q_OFF[i] + 128 * (i + 1))
                            ins = V.tensor_scalar(probs[:, b0, b], probs[:, b0, b],
                                                  rden[:, 8 * n + i:8 * n + i + 1], None, ALU.mult)
                        order.link(ins)
                        for i in range(4):
                            b = slice(Q_OFF[i], Q_OFF[i] + 128 * (i + 1))
                            ins = V.scalar_tensor_tensor(out=probs[:, b0, b], in0=probs[:, b0 + 1, b],
                                                         scalar=rden[:, 8 * n + 4 + i:8 * n + 5 + i],
                                                         in1=probs[:, b0, b], op0=ALU.mult, op1=ALU.add)
                        ins.then_inc(sem("diff_probs"), 1)

                    for n in range(4):
                        if n < 3:
                            low_q(2 * n + 2)
                            low_q(2 * n + 3)
                        combine(n)
                        if n < 3:
                            mask_scores(2 * n + 2, (2 * n + 2) % 4, 1, 32 ** -0.5,
                                        since("l_turned", l, n) if n >= 1 else None)
                            mask_scores(2 * n + 3, (2 * n + 3) % 4, 1, 32 ** -0.5)
                        take_pt_b(n)
                        dve.wait_ge(*since("l_o", l, n + 1))
                        V.tensor_copy(o_tok[:, :, 64 * n:64 * n + 64],
                                      ps[:, 7, 0:256].rearrange("p (i d) -> p i d", d=64))\
                         .then_inc(sem("l_o_read"), 1)
                    dve.wait_ge(*since("l_o_read", l, 4))
                    order.link(V.tensor_tensor(o_tok[:, :, 256:512], o_tok[:, :, 0:256], o_tok[:, :, 0:256], ALU.mult))
                    V.tensor_reduce(o_ss, o_tok[:, :, 256:512].rearrange("p i (h d) -> p i h d", d=64), AX,
                                    ALU.add).then_inc(sem("diff_ss"), 1)
                    dve.wait_ge(sem("diff_root"), 1)
                    order.link(V.reciprocal(o_rstd, o_root))
                    order.link(V.tensor_scalar(o_rstd, o_rstd, 1.0 - lambda_init, None, ALU.mult))
                    for i in range(4):
                        o = o_tok[:, i, 0:256].rearrange("p (h d) -> p h d", d=64)
                        ins = V.tensor_tensor(o, o, bc(o_rstd[:, 4 * i:4 * i + 4], 64), ALU.mult)
                    ins.then_inc(sem("diff_normed"), 1)
                    wait_gates()
                    for k in range(2):
                        dve.wait_ge(*since("l_y_turned", l, k + 1))
                        finish_y(k, ps[:, k, :], 6 + k, par("subln"))
                        V.memset(credit[:, 8 + k:9 + k], 0.0).then_inc(sem("y_taken"), 1)

                    def stick_sp(h):
                        z, L = probs[:, 2 * (h % 2), :], probs[:, 2 * (h % 2) + 1, :]
                        dve.wait_ge(sem("log1p"), h + 1)
                        order.link(V.scalar_tensor_tensor(out=L, in0=z, scalar=0.0, in1=L, op0=ALU.max, op1=ALU.add))
                        for kt in range(4):
                            b = L[:, Z_OFF[kt]:Z_OFF[kt] + 128]
                            ins = V.tensor_tensor(b, b, attn_c[:, 2, :], ALU.mult)
                        ins.then_inc(sem("sp_ready"), 1)

                    def stick_low(h):
                        dve.wait_ge(sem("sp_hi_ready"), h + 1)
                        V.tensor_tensor(sp_split[:, 1, :], probs[:, 2 * (h % 2) + 1, :], sp_split[:, 0, :].bitcast(F32),
                                        ALU.subtract).then_inc(sem("sp_split"), 1)

                    def stick_log(h):
                        z = probs[:, 2 * (h % 2), :]
                        for kt in range(4):
                            at = (0, 512, 1024, 1280)[kt]
                            n = 512 - 128 * kt
                            dve.wait_ge(sem("tail"), 4 * h + min(kt + 1, 2) + 2 * (kt >= 2))
                            V.tensor_tensor(z[:, Z_OFF[kt]:Z_OFF[kt] + n], z[:, Z_OFF[kt]:Z_OFF[kt] + n],
                                            ps[:, 4 + at // 512, at % 512:at % 512 + n],
                                            ALU.subtract).then_inc(sem("tail_read"), 1)
                        dve.wait_ge(sem("tail_read"), 4 * h + 4)
                        for kt in range(4):
                            b = z[:, Z_OFF[kt]:Z_OFF[kt] + 128]
                            ins = V.tensor_tensor(b, b, attn_c[:, 3, :], ALU.add)
                        ins.then_inc(sem("log_a"), 1)

                    stick_sp(0)
                    stick_low(0)
                    for h in range(4):
                        stick_log(h)
                        if h < 3:
                            stick_sp(h + 1)
                            stick_low(h + 1)
                    dve.wait_ge(sem("stick_o"), 4)
                    for k in range(2):
                        finish_y(2 + k, ps[:, 3 if k == 0 else 7, :], 14 + k)
                for q in range(4):
                    step_lo(U_L[l] + U_IN, q)
                    for j in range(4):
                        t = 4 * q + j
                        if j < 3:
                            dve.wait_ge(sem("out_tile"), 12 * l + 3 * q + j + 1)
                        else:
                            dve.wait_ge(w_used, U_L[l] + U_IN + q + 1 + 1)
                        V.tensor_tensor(X[:, t, :], X[:, t, :], ps[:, OUT_BANKS[j], :], ALU.add).then_inc(x_ready, 1)
                        if l == 0 and t >= 1:
                            low_part(16 + t - 1, t - 1, par("g1", t - 1))
                if l == 0:
                    low_part(31, 15, par("g1", 15))
                    step_lo(U_L[1], 0)
                    step_lo(U_L[1], 1)
                if l == 1:
                    one_over_root(2)

            def low_pair(n0, i, gain):
                for s in range(2):
                    dve.wait_ge(h_hi_ready, n0 + 2 * i + s + 1)
                    V.scalar_tensor_tensor(out=h_lo[:, 2 * i + s, :], in0=X[:, 2 * i + s, :], scalar=dpar(gain, 2 * i + s),
                                           in1=h_hi[:, 2 * i + s, :].bitcast(F32), op0=ALU.mult,
                                           op1=ALU.subtract).then_inc(h_ready, 1)

            def conv(outs, ins, taps, pad, last, bias=None):
                n = len(taps[0])
                for k in range(n):
                    for r, (o, x) in enumerate(zip(outs, ins)):
                        xk = x[:, pad - n + 1 + k:pad - n + 1 + k + S]
                        if k == 0:
                            ins_ = V.tensor_scalar(o, xk, taps[r][0], bias[r] if bias else None, ALU.mult,
                                                   ALU.add if bias else ALU.bypass)
                        else:
                            ins_ = V.scalar_tensor_tensor(out=o, in0=xk, scalar=taps[r][k], in1=o, op0=ALU.mult, op1=ALU.add)
                        if last is not None and k == n - 1:
                            ins_.then_inc(last, 1)
                    if k < n - 1:
                        order.link(ins_)
                return ins_

            def group_add(k, sq):
                for t in range(1, 4):
                    dve.wait_ge(sem("group_sq"), 4 * k + t + 1)
                    ins = V.tensor_tensor(sq[:, 0, :], sq[:, 0, :], sq[:, t, :], ALU.add)
                    if t < 3:
                        order.link(ins)
                ins.then_inc(sem("group_added"), 1)

            def group_norm(k, y):
                dve.wait_ge(sem("group_root"), k + 1)
                order.link(V.reciprocal(rstd_g, root[:, :]))
                for t in range(4):
                    ins = V.scalar_tensor_tensor(out=y[:, t, :], in0=y[:, t, :], scalar=par("grp", 4 * k + t), in1=rstd_g,
                                                 op0=ALU.mult, op1=ALU.mult)
                ins.then_inc(sem("group_normed"), 1)

            def step(u, s, tile0):
                step_lo(u, s)
                if s % 2:
                    dve.wait_ge(w_used, u + s + 1 + 1)
                    for j in range(2):
                        ins = V.tensor_tensor(proj[:, tile0 + s - 1 + j, PAD:PAD + S], ps[:, s - 1 + j, :],
                                              rstd[:, :], ALU.mult)
                    ins.then_inc(bank_free, 1)

            for first, last, unit in SPLIT_PARTS:
                with dve.Fori(first, last) as i:
                    for s in range(2):
                        t = 2 * i + s
                        V.scalar_tensor_tensor(out=X[:, t, :], in0=X[:, t, :], scalar=dpar("final", t), in1=rstd[:, :],
                                               op0=ALU.mult, op1=ALU.mult).then_inc(x_ready, 1)
                    low_pair(32, i, "pre_mix")
                if unit is not None:
                    step_lo(U_LRU, unit)
            dve.wait_ge(sem("lam_log"), 1)
            order.link(V.tensor_scalar(lru_s[:, 12:16], par("lam", 0, 4), -1.0, 0.0, ALU.mult, ALU.max))
            order.link(V.tensor_tensor(lru_s[:, 16:20], lru_s[:, 12:16], lru_s[:, 4:8], ALU.add))
            V.tensor_scalar(lru_s[:, 8:12], lru_s[:, 16:20], -8.0, None, ALU.mult).then_inc(sem("lru_rate"), 1)
            dve.wait_ge(sem("pads_ready"), 1)
            project(U_LRU, M2_QUADS["lru"], 0, norm=3)
            def lru_conv(taps):
                for k in taps:
                    for t in range(4):
                        o, x, w = lru_xc[:, t, :], proj[:, t, PAD - 3 + k:PAD - 3 + k + S], par("lru_conv", 4 * t + k)
                        if k == 0:
                            ins = V.tensor_scalar(o, x, w, par("lru_b", t), ALU.mult, ALU.add)
                        else:
                            ins = V.scalar_tensor_tensor(out=o, in0=x, scalar=w, in1=o, op0=ALU.mult, op1=ALU.add)
                        if k == 3:
                            ins.then_inc(sem("lru_conved"), 1)
                    if k < 3:
                        order.link(ins)

            for n in range(2):
                for s in range(4):
                    step(U_SGU + 4 * n, s, 8 + 4 * n)
                    if (n, s) == (0, 0):
                        dve.wait_ge(bank_free, G_SGU + 2)
                        dve.wait_ge(sem("x_spilled"), 64)
                        lru_conv((0, 1))
                    if (n, s) == (0, 1):
                        lru_conv((2, 3))
                    if (n, s) == (1, 1):
                        dve.wait_ge(sem("lru_a"), 4)
                        dve.wait_ge(sem("lru_tanh"), 4)
                        for half in range(2):
                            a, r = lru_a[:, 2 * half:2 * half + 2, :], lru_r[:, 2 * half:2 * half + 2, :]
                            order.link(V.tensor_tensor(lru_a2[:, :, :], a, a, ALU.mult))
                            ins = V.scalar_tensor_tensor(out=r, in0=lru_a2[:, :, :], scalar=1.0, in1=r, op0=ALU.add, op1=ALU.mult)
                            if half == 0:
                                order.link(ins)
                            else:
                                ins.then_inc(sem("lru_m"), 1)
                    if (n, s) == (1, 2):
                        order.link(V.tensor_tensor(lru_i, lru_i, lru_xc, ALU.mult))
                    if (n, s) == (1, 3):
                        dve.wait_ge(sem("lru_mult"), 1)
                        order.link(V.tensor_tensor(lru_i, lru_i, lru_r, ALU.mult))
                        for t in range(4):
                            ins = V.tensor_tensor_scan(lru_xc[:, t, :], lru_a[:, t, :], lru_i[:, t, :], 0.0,
                                                       ALU.mult, ALU.add)
                        order.link(ins)
                    if (n, s) == (1, 3):
                        dve.wait_ge(sem("lru_gelu"), 1)
                        V.tensor_tensor(Y[:, 4:8, :], lru_xc, proj[:, 4:8, PAD:], ALU.mult).then_inc(sem("mixer_out"), 1)
            for n in range(3):
                for s in range(4):
                    step(U_SC + 4 * n, s, (0, 4, 12)[n])
                    if (n, s) == (0, 0):
                        dve.wait_ge(sem("mix_c_landed"), 16 * 9)
                        order.link(V.tensor_tensor(sgu_w[:, :, :], sgu_w[:, :, :], bm(tri01[:, :], 4), ALU.mult))
                        group_add(0, Y[:, 8:12, :])
                    if (n, s) == (0, 3):
                        group_norm(0, Y[:, 4:8, :])
                    if (n, s) == (1, 0):
                        for tt in range(4):
                            dve.wait_ge(sem("sgu_turned"), tt + 1)
                            ins = V.bn_stats(stats[:, tt, 0:6], ps[:, 4 + tt, :])
                        order.link(ins)
                        for tt in range(4):
                            ins = V.bn_aggr(stats[:, tt, 6:8], stats[:, tt, 0:6])
                        ins.then_inc(sem("sgu_stats"), 1)
                    if (n, s) == (1, 2):
                        dve.wait_ge(sem("sgu_root"), 1)
                        order.link(V.reciprocal(stats[:, :, 9:10], stats[:, :, 8:9]))
                        for tt in range(4):
                            ins = V.tensor_scalar(Y[:, 12 + tt, :], ps[:, 4 + tt, :], stats[:, tt, 6:7], stats[:, tt, 9:10],
                                                  ALU.subtract, ALU.mult)
                        order.link(ins)
                        order.link(V.tensor_tensor(Y[:, 12:16, :], Y[:, 12:16, :], bm(sgu_sb[:, 0, :], 4), ALU.mult))
                    if (n, s) == (1, 3):
                        V.tensor_tensor(Y[:, 12:16, :], Y[:, 12:16, :], bm(sgu_sb[:, 1, :], 4), ALU.add)\
                         .then_inc(sem("sgu_normed"), 1)
                    if (n, s) == (2, 0):
                        dve.wait_ge(sem("ba_hi_ready"), 1)
                        V.tensor_tensor(ba_lo[:, :], ba_raw, ba_hi[:, :].bitcast(F32), ALU.subtract).then_inc(sem("ba_split"), 1)
                    if (n, s) == (2, 1):
                        for g in range(4):
                            dve.wait_ge(sem("sgu_mixed"), g + 1)
                            ins = V.tensor_tensor(Y[:, 8 + g, :].rearrange("p (n t) -> p n t", t=128),
                                                  ps[:, 4 + g, :].rearrange("p (n t) -> p n t", t=128),
                                                  bm(sgu_sb[:, 2, 128 * g:128 * g + 128], 4), ALU.add)
                        order.link(ins)
                        dve.wait_ge(sem("sgu_gelu"), 2)
                        V.tensor_tensor(Y[:, 8:12, :], Y[:, 8:12, :], proj[:, 8:12, PAD:], ALU.mult)\
                         .then_inc(sem("mixer_out"), 1)
                    if (n, s) == (2, 3):
                        group_add(1, Y[:, 12:16, :])

            def sc_conv(taps):
                for k in taps:
                    for t in range(4):
                        o, x = Y[:, 12 + t, :], proj[:, 4 + t, PAD - 2 + k:PAD - 2 + k + S]
                        w = par("sc_conv", 3 * t + k)
                        if k == 0:
                            ins = V.tensor_scalar(o, x, w, None, ALU.mult)
                        else:
                            ins = V.scalar_tensor_tensor(out=o, in0=x, scalar=w, in1=o, op0=ALU.mult, op1=ALU.add)
                    order.link(ins)

            def conv_taps(n, taps):
                for k in taps:
                    for t in range(4):
                        o = conv_out[:, 4 * (n % 2) + t, :]
                        x = proj[:, (Q_T, KEY_T, V_T)[n] + t, PAD - 3 + k:PAD - 3 + k + S]
                        w = par("gdn_conv", 4 * (4 * n + t) + k)
                        if k == 0:
                            ins = V.tensor_scalar(o, x, w, None, ALU.mult)
                        else:
                            ins = V.scalar_tensor_tensor(out=o, in0=x, scalar=w, in1=o, op0=ALU.mult, op1=ALU.add)
                    if k < 3:
                        order.link(ins)
                    else:
                        ins.then_inc(sem("qkv_conved"), 1)

            def l2_norm(t):
                dve.wait_ge(sem("l2_root"), t + 1)
                order.link(V.reciprocal(l2_root_at(t), l2_root_at(t)))
                x = proj[:, (Q_T, KEY_T)[t // 4] + t % 4, PAD:]
                V.scalar_tensor_tensor(out=x, in0=x, scalar=GDN_D ** -0.5 if t < 4 else 1.0,
                                       in1=l2_root_at(t), op0=ALU.mult, op1=ALU.mult).then_inc(sem("l2_normed"), 1)

            def take_ba():
                dve.wait_ge(sem("ba_done"), 1)
                V.tensor_tensor(ba_rows, ps[0:8, 4, :], rstd[0:8, :], ALU.mult).then_inc(sem("ba_rows"), 1)

            def take_turned():
                dve.wait_ge(sem("ba_turned"), 1)
                V.tensor_copy(ba_tok, ps[:, 5, 0:32]).then_inc(sem("ba_tok"), 1)
                dve.wait_ge(sem("ba_tok"), 1)
                V.tensor_tensor(g_tmp.rearrange("p (h t) -> p t h", h=4), ba_tok.rearrange("p (t c) -> p t c", c=8)[:, :, 4:8],
                                bm(alog_sb[:, 4:8], 4), ALU.add).then_inc(sem("a_dt"), 1)

            def make_gate():
                dve.wait_ge(sem("a_log1p"), 1)
                order.link(V.scalar_tensor_tensor(out=g_tmp, in0=g_tmp, scalar=0.0, in1=exp_g, op0=ALU.max, op1=ALU.add))
                V.scalar_tensor_tensor(out=gate.rearrange("p (h t) -> p h t", h=4),
                                       in0=g_tmp.rearrange("p (h t) -> p h t", h=4), scalar=-1.0,
                                       in1=bc(alog_sb[:, 0:4], 4), op0=ALU.mult, op1=ALU.mult)\
                 .then_inc(sem("gate_ready"), 1)

            def take_sums():
                dve.wait_ge(sem("g_summed"), 1)
                V.tensor_copy(g_sums, ps[:, 4, 0:64]).then_inc(sem("g_sums_read"), 1)
                dve.wait_ge(sem("g_sums_read"), 1)
                V.tensor_tensor(kgs, g_sums[:, 16:32], g_sums[:, 0:16], ALU.subtract).then_inc(sem("kgs_log"), 1)

            def scale_beta():
                dve.wait_ge(sem("exp_g_ready"), 3)
                order.link(V.tensor_tensor(be, beta, exp_g, ALU.mult))

            for n in range(4):
                for s in range(4):
                    u = U_QKVZ + 4 * n
                    step(u, s, (Q_T, KEY_T, V_T, Z_T)[n])
                    if (n, s) == (0, 0):
                        dve.wait_ge(bank_free, G_QKVZ + 2)
                        order.link(V.tensor_tensor(proj[:, 4:8, PAD:], proj[:, 4:8, PAD:], proj[:, 12:16, PAD:], ALU.mult))
                        dve.wait_ge(sem("group_sums"), 2)
                        sc_conv((0,))
                    if (n, s) == (0, 1):
                        sc_conv((1, 2))
                    if (n, s) == (0, 2):
                        V.tensor_tensor(Y[:, 12:16, :], Y[:, 12:16, :], proj[:, 0:4, PAD:], ALU.mult)\
                         .then_inc(sem("mixer_out"), 1)
                        group_norm(1, Y[:, 8:12, :])
                    if (n, s) == (0, 3):
                        group_add(2, sc_sq)
                    if (n, s) == (1, 3):
                        group_norm(2, Y[:, 12:16, :])
                    if (n, s) == (1, 0):
                        dve.wait_ge(bank_free, G_QKVZ + 2 + 2)
                        take_ba()
                    if (n, s) == (1, 2):
                        take_turned()
                    if (n, s) == (2, 0):
                        dve.wait_ge(bank_free, G_QKVZ + 4 + 2)
                        make_gate()
                    if (n, s) == (2, 2):
                        take_sums()
                    if (n, s) == (3, 0):
                        dve.wait_ge(bank_free, G_QKVZ + 6 + 2)
                        scale_beta()
                    if n in (1, 2) and s < 2:
                        conv_taps(n - 1, (2 * s, 2 * s + 1))
                    if n == 2 and s >= 2:
                        l2_norm(s - 2)
                    if n == 3 and s == 0:
                        l2_norm(2)
                        l2_norm(3)
                    if n == 3 and s in (1, 2):
                        if s == 1:
                            dve.wait_ge(sem("l2_normed"), 4)
                        conv_taps(2, (2 * s - 2, 2 * s - 1))
                    if n == 3 and s == 3:
                        l2_norm(4)
            l2_norm(5)

            def t4(ap):
                return ap.rearrange("p (t n) -> p t n", n=128)

            for pair in range(2):
                heads = [(m, 2 * pair + m, 4 * m) for m in range(2)]
                for m, h, b in heads:
                    hs = slice(4 * h, 4 * h + 4)
                    V.tensor_tensor(t4(tmp_a[:, m, :]), bm(ident, 4), bc(g_sums[:, hs], 128), ALU.mult)
                    V.tensor_tensor(t4(tmp_b[:, m, :]), bm(ident, 4), bc(beta[:, hs], 128), ALU.mult)\
                     .then_inc(sem("diags"), 1)
                    dve.wait_ge(sem("kv_turned"), h + 1)
                    V.tensor_tensor(t4(k_be[:, h, :]), t4(ps[:, b, :]), bc(be[:, hs], 128), ALU.mult)
                    V.tensor_tensor(t4(k_g[:, h, :]), t4(ps[:, b, :]), bc(kgs[:, hs], 128), ALU.mult)
                    V.tensor_tensor(t4(v_b[:, h, :]), t4(ps[:, b + 1, :]), bc(beta[:, hs], 128), ALU.mult)\
                     .then_inc(sem("kv_taken"), 1)
                for m, h, b in heads:
                    hs = slice(4 * h, 4 * h + 4)
                    dve.wait_ge(sem("exp_row"), h + 1)
                    order.link(V.tensor_tensor(t4(tmp_a[:, m, :]), t4(ps[:, b + 2, :]), bc(g_sums[:, hs], 128), ALU.subtract))
                    V.tensor_tensor(t4(tmp_a[:, m, :]), t4(tmp_a[:, m, :]), bm(gdn_c[:, 4, :], 4), ALU.add)\
                     .then_inc(sem("decay_log"), 1)
                    V.tensor_tensor(tmp_b[:, m, :], proj[:, KEY_T + h, PAD:], ps[:, b + 3, :], ALU.mult)\
                     .then_inc(sem("kb_ready"), 1)
                for m, h, b in heads:
                    dve.wait_ge(sem("decay_ready"), h + 1)
                    order.link(V.tensor_tensor(t4(inv_t[:, h, :]), t4(tmp_a[:, m, :]), bm(gdn_c[:, 5, :], 4), ALU.mult))
                    dve.wait_ge(sem("kk_done"), h + 1)
                    V.scalar_tensor_tensor(out=pows[:, m, 0, 1, :], in0=ps[:, b + 1, :], scalar=-1.0, in1=inv_t[:, h, :],
                                           op0=ALU.mult, op1=ALU.mult).then_inc(sem("nt_ready"), 1)
                    dve.wait_ge(sem("nt_ready"), h + 1)
                    V.tensor_tensor(t4(inv_t[:, h, :]), t4(pows[:, m, 0, 1, :]), bm(ident, 4), ALU.add)\
                     .then_inc(sem("inv_ready"), 1)
                    V.tensor_tensor(attn_t[:, h, :], ps[:, b, :], tmp_a[:, m, :], ALU.mult).then_inc(sem("attn_ready"), 1)
                    V.tensor_tensor(proj[:, Q_T + h, PAD:], proj[:, Q_T + h, PAD:], pows[:, m, 1, 0, :], ALU.mult)\
                     .then_inc(sem("q_scaled"), 1)
                for it in range(5):
                    if it < 4:
                        for m, h, b in heads:
                            dve.wait_ge(sem("nt_squared"), (4 * pair + it) * 2 + m + 1)
                            V.tensor_copy(pows[:, m, 1 - it % 2, 1, :], ps[:, b + 1, :]).then_inc(sem("nt_power"), 1)
                    if pair == 0 and it in (0, 2):
                        l2_norm(6 + it // 2)
                    for m, h, b in heads:
                        dve.wait_ge(sem("inv_step"), (5 * pair + it) * 2 + m + 1)
                        V.tensor_tensor(inv_t[:, h, :], inv_t[:, h, :], ps[:, b + 2, :], ALU.add)\
                         .then_inc(sem("inv_ready"), 1)
                for m, h, b in heads:
                    dve.wait_ge(sem("u_done"), h + 1)
                    V.tensor_copy(u_b[:, h, :], ps[:, b + 1, :]).then_inc(sem("u_ready"), 1)
            dve.wait_ge(sem("inv_step"), 20)
            V.memset(state[:, 0, :], 0.0).then_inc(sem("state_ready"), 1)

            def low_y(n):
                t = Y_ORDER[n]
                dve.wait_ge(h_hi_ready, 48 + n + 1)
                V.tensor_tensor(h_lo[:, t, :], Y[:, t, :], h_hi[:, t, :].bitcast(F32), ALU.subtract).then_inc(h_ready, 1)

            for c in range(8):
                r, tt, half = 64 * (c % 2), c // 2, c % 2
                dve.wait_ge(sem("w_state"), c + 1)
                if tt >= 2:
                    dve.wait_ge(sem("o_done"), 4 * (tt - 1))
                V.tensor_tensor(v_new[r:r + 64, tt % 2, :].rearrange("p (h n) -> p h n", h=4),
                                u_b[r:r + 64, :, 128 * tt:128 * tt + 128],
                                ps[r:r + 64, 0, :].rearrange("p (h n) -> p h n", h=4), ALU.subtract)\
                 .then_inc(sem("v_new_ready"), 1)
                low_y(c)
                if c == 7:
                    continue
                dve.wait_ge(sem("state_ready"), c + 1)
                order.link(V.tensor_tensor(state_g[:, :].rearrange("p (h n) -> p h n", h=4),
                                           state[:, c % N_STATES, :].rearrange("p (h n) -> p h n", h=4),
                                           bc(g_last[:, 16 * half + tt:16 * half + 16:4], 128), ALU.mult))
                dve.wait_ge(sem("state_add"), c + 1)
                if c >= 5:
                    dve.wait_ge(sem("o_done"), 4 * ((c - 5) // 2 + 1))
                V.tensor_tensor(state[:, (c + 1) % N_STATES, :], state_g[:, :], ps[:, 3, :], ALU.add).then_inc(sem("state_ready"), 1)
            dve.wait_ge(sem("o_done"), 16)
            for n in range(8, 12):
                low_y(n)
            step_lo(U_WO2, 0)
            dve.wait_ge(sem("z_silu"), 1)
            for h in range(4):
                dve.wait_ge(sem("gdn_root"), h + 1)
                order.link(V.reciprocal(conv_out[:, 4 + h, :], conv_out[:, 4 + h, :]))
                order.link(V.scalar_tensor_tensor(out=Y[:, h, :], in0=proj[:, V_T + h, PAD:], scalar=par("gdn_norm"),
                                                  in1=conv_out[:, 4 + h, :], op0=ALU.mult, op1=ALU.mult))
                V.tensor_tensor(Y[:, h, :], Y[:, h, :], proj[:, Z_T + h, PAD:], ALU.mult).then_inc(sem("mixer_out"), 1)
                if h >= 1:
                    low_y(12 + h - 1)
            low_y(15)

            def y_quad(i, first=0):
                for s in range(first, 4):
                    step_lo(U_WO2 + 4 * i, s)
                    if s % 2:
                        dve.wait_ge(w_used, U_WO2 + 4 * i + s + 1 + 1)
                        V.tensor_copy(y2[:, bass.ds(4 * i + (s - 1), 2), :], ps[:, s - 1:s + 1, :]).then_inc(bank_free, 1)

            y_quad(0, first=1)
            with dve.Fori(1, 4) as i:
                y_quad(i)
            one_over_root(4)
            dve.wait_ge(sem("x_back"), 64)
            for first, last, unit in SPLIT_PARTS:
                with dve.Fori(first, last) as i:
                    order.enter(i, 1, first)
                    for s in range(2):
                        t = 2 * i + s
                        ins = V.scalar_tensor_tensor(out=y2[:, t, :], in0=y2[:, t, :], scalar=dpar("post_mix", t),
                                                     in1=rstd[:, :], op0=ALU.mult, op1=ALU.mult)
                    order.link(ins)
                    for s in range(2):
                        t = 2 * i + s
                        V.tensor_tensor(X[:, t, :], X[:, t, :], y2[:, t, :], ALU.add).then_inc(x_ready, 1)
                    low_pair(64, i, "pre_ffn")
                    order.leave(last - first)
                if unit is not None:
                    step_lo(U_FFN, unit)

            for k in range(4):
                V.memset(credit[:, 4 * k:4 * k + 1], 0.0).then_inc(down_free, 1)
            order.link(V.memset(hid[:, :, 0:2], 0.0))

            def ffn_take(u, s, c):
                dve.wait_ge(w_used, u + s + 1 + 1)
                for j in range(2):
                    ins = V.tensor_tensor(hid[:, j, 2:], ps[:, 2 * c + j, :], rstd[:, :], ALU.mult)
                ins.then_inc(bank_free, 1)

            def ffn_group(seg, b, c, par_, finish=True):
                dve.wait_ge(bank_free, seg * 4 + (G_FFN + 2 * b + c + 3))
                dst = f_val if c else f_gate
                tile = [seg * 4 + (FFT * c + 2 * b + j) for j in range(2)]
                ins = conv([dst[:, j, :] for j in range(2)], [hid[:, j, :] for j in range(2)],
                           [[dpar("ffn_conv", tile[j] * 3 + k) for k in range(3)] for j in range(2)], 2, None,
                           [dpar("ffn_b", tile[j]) for j in range(2)])
                if c == 0:
                    ins.then_inc(sem("f_gates"), 1)
                    return
                order.link(ins)
                if finish:
                    ffn_split(seg, b, par_)

            def ffn_split(seg, b, par_):
                dve.wait_ge(sem("f_gelu"), seg * 2 + (b + 1))
                V.tensor_tensor(f_val[:, :, :], f_gate[:, :, :], f_val[:, :, :], ALU.mult).then_inc(sem("f_gated"), 1)
                dve.wait_ge(sem("f_hi_ready"), seg * 2 + (b + 1))
                V.tensor_tensor(f_lo[:, par_, 2 * b:2 * b + 2, :], f_val[:, :, :],
                                f_hi[:, par_, 2 * b:2 * b + 2, :].bitcast(F32), ALU.subtract).then_inc(f_ready, 1)

            def ffn_up(u, seg, par_, norm=None):
                for s in range(8):
                    if norm is not None and s < 4:
                        if s >= 2:
                            step_lo(u, s)
                        if s == 2:
                            one_over_root(norm)
                            ffn_take(u, 2, 0)
                        if s == 3:
                            ffn_group(seg, 0, 0, par_)
                            dve.wait_ge(sem("f_gates"), 1)
                            ffn_take(u, 3, 1)
                        continue
                    step_lo(u, s)
                    if s % 2:
                        ffn_take(u, s, s // 2 % 2)
                    elif s:
                        ffn_group(seg, (s - 1) // 4, (s - 1) // 2 % 2, par_)

            def ffn_down(u, seg, last=False, before=None):
                for q in range(4):
                    if not (last and q == 3):
                        step_lo(u, q)
                    if before is not None and q == 0:
                        ffn_group(before[0], 1, 1, before[1], finish=False)
                    if before is not None and q == 1:
                        ffn_split(before[0], 1, before[1])
                    for j in range(4):
                        if j < 3:
                            dve.wait_ge(down_tile, seg * 12 + (3 * q + j + 1))
                        else:
                            dve.wait_ge(w_used, u + q + 1 + 1)
                        V.tensor_tensor(y_acc[:, 4 * q + j, :], y_acc[:, 4 * q + j, :], ps[:, 4 + j, :],
                                        ALU.add).then_inc(down_free, 1)

            PER_SEG = 2 * (2 + 3)
            ffn_up(U_FFN, 0, 0, norm=5)
            ffn_group(0, 1, 1, 0)
            dve.wait_ge(sem("acc_zeroed"), 1)
            with dve.Fori(0, (SEGS - 1) // 2) as i:
                order.enter(i, 2 * PER_SEG)
                for e in range(2):
                    u = U_FFN + 8 + 12 * e + 24 * i
                    ffn_up(u, 2 * i + (1 + e), 1 - e)
                    ffn_down(u + 8, 2 * i + e, before=(2 * i + (1 + e), 1 - e))
                order.leave((SEGS - 1) // 2)
            ffn_down(N_UNITS - 4, SEGS - 1, last=True)
            one_over_root(6)
            dve.wait_ge(sem("x_back"), 128)
            with dve.Fori(0, 8) as i:
                order.enter(i, 1)
                for s in range(2):
                    t = 2 * i + s
                    ins = V.scalar_tensor_tensor(out=y_acc[:, t, :], in0=y_acc[:, t, :], scalar=dpar("post_ffn", t),
                                                 in1=rstd[:, :], op0=ALU.mult, op1=ALU.mult)
                order.link(ins)
                for s in range(2):
                    t = 2 * i + s
                    V.tensor_tensor(y_acc[:, t, :], y_acc[:, t, :], x_back[:, t, :], ALU.add).then_inc(sem("out_tiles"), 1)
                order.leave(8)


def unit_of(w, t0, nt, cols):
    a = w[t0 * 128:(t0 + nt) * 128, cols].reshape(nt, 128, -1)
    return a.transpose(1, 0, 2).reshape(128, -1)


def group_units(w, c0, groups, halves=(0, 1)):
    return [unit_of(w, 8 * half, 8, slice(c0 + 256 * g, c0 + 256 * g + 256)) for g in range(groups) for half in halves]


def columns(v):
    return v.reshape(-1, 128).T


def kernel(**inp):
    import concourse.bacc as bacc
    from concourse.bass_utils import run_bass_kernel_spmd

    a = {k: np.ascontiguousarray(v) for k, v in inp.items()}
    def opening(u):
        return [u[0], u[2], u[1], u[3]] + u[4:]

    units = []
    for l in range(2):
        units += opening(group_units(a["w_in"][l], 0, 8))
        units += [unit_of(a["w_out"][l], 0, 4, slice(512 * q, 512 * q + 512)) for q in range(4)]
    w2 = a["w_in_2"][0]
    units += opening(group_units(w2, 2056, 4)) + group_units(w2, 3080, 4) + group_units(w2, 4104, 6) + group_units(w2, 0, 8)
    units += group_units(a["w_out_2"][0], 0, 8, halves=(1, 0))
    up, down = a["ffn_up_2"][0], a["ffn_down_2"][0]

    def ups(s):
        return [u for b in range(2) for c in (0, D_FF) for u in group_units(up, c + 512 * s + 256 * b, 1)]

    def downs(s):
        return [unit_of(down, 4 * s, 4, slice(512 * q, 512 * q + 512)) for q in range(4)]

    units += opening(ups(0))
    for s in range(1, SEGS):
        units += ups(s) + downs(s - 1)
    units += downs(SEGS - 1)
    assert len(units) == N_UNITS
    weights = np.stack(units)

    def taps(w):
        return w.reshape(w.shape[0], -1, 128).transpose(2, 1, 0).reshape(128, -1)

    vals = dict(g0=columns(a["norm_g"][0]), g1=columns(a["norm_g"][1]), final=columns(a["final_norm_g"]),
                pre_mix=columns(a["pre_mix_norm_2"][0]), post_mix=columns(a["post_mix_norm_2"][0]),
                pre_ffn=columns(a["pre_ffn_norm_2"][0]), post_ffn=columns(a["post_ffn_norm_2"][0]),
                gdn_conv=taps(a["gdn_conv_w_2"][0]), gdn_norm=columns(a["gdn_norm_w_2"][0]),
                lru_conv=taps(a["lru_conv_w_2"][0]), lru_b=columns(a["lru_conv_b_2"][0]),
                ba=columns(a["lru_ba_2"][0].reshape(-1)), bx=columns(a["lru_bx_2"][0].reshape(-1)),
                lam=columns(a["lru_lambda_2"][0]), sc_conv=taps(a["sconv_w_2"][0]),
                grp=columns(a["grp_norm_w_2"][0].reshape(-1)),
                subln=columns(np.concatenate([a["diff_subln_g"][0]] * 2)),
                ffn_conv=taps(a["ffn_conv_w_2"][0]), ffn_b=columns(a["ffn_conv_b_2"][0]))
    arrays = {
        "weights": weights,
        "x_in": np.ascontiguousarray(a["x"][0].T.reshape(KT, 128, S).transpose(1, 0, 2)),
        "params": np.ascontiguousarray(np.concatenate([vals[n] for n, _ in PARAM_SIZES], axis=1)),
        "consts": shape_constants(),
        "w_ba": np.ascontiguousarray(unit_of(w2, 0, 16, slice(2048, 2056))),
        "alog_dt": np.concatenate([a["gdn_a_log_2"][0], a["gdn_dt_bias_2"][0]]),
        "lam_rows": a["diff_lam"][0].reshape(-1),
        "sgu_rows": np.stack([a["sgu_ln_w_2"][0], a["sgu_ln_b_2"][0], a["sgu_b_2"][0].reshape(-1)]),
        "sgu_wsT": np.ascontiguousarray(a["sgu_ws_2"][0].transpose(2, 0, 1)),
        "lru_wa": a["lru_wa_2"][0],
        "lru_wx": a["lru_wx_2"][0],
    }
    nc = bacc.Bacc("TRN2", target_bir_lowering=False, num_devices=1)
    args = [nc.dram_tensor(n, v.shape, mybir.dt.from_np(v.dtype), kind="ExternalInput").ap() for n, v in arrays.items()]
    args.append(nc.dram_tensor("out", (128, KT, S), F32, kind="ExternalOutput").ap())
    two_blocks_kernel(nc, *args)
    r = run_bass_kernel_spmd(nc, [arrays], core_ids=[0])
    got = r.results[0]["out"]
    return got.transpose(1, 0, 2).reshape(D, S).T.reshape(1, S, D)
```
